# Optimizing a Trainium2 kernel written in Bass

```python
import jax
import jax.numpy as jnp
from jax import lax
import numpy as np

D_MODEL = 1024
BATCH = 1
SEQ = 256
DEPTH = 2

CTX_LEN = 256
GRID_W = 64
EPS = 1e-6

GLA_HEADS = 4
GLA_DK = 48
GLA_DV = 96
GLA_QK = GLA_HEADS * GLA_DK
GLA_WIDTH = GLA_HEADS * GLA_DV
GLA_LOWRANK = 16
GLA_TAU = 16.0
GLA_CHUNK = 64
ROPE_BASE = 10000.0

NA_HEADS = 6
NA_DH = 64
NA_WIDTH = NA_HEADS * NA_DH
NA_KH = 8
NA_KW = 16

CONV_WIDTH = 256
CONV_K = 31

MIX_WIDTH = GLA_WIDTH + NA_WIDTH + CONV_WIDTH
IN_SIZES = (GLA_QK, GLA_QK, GLA_WIDTH, GLA_WIDTH, 2 * GLA_LOWRANK, NA_WIDTH, NA_WIDTH, NA_WIDTH, 2 * CONV_WIDTH)
IN_COLS = sum(IN_SIZES)

N_EXPERTS = 16
N_GROUPS = 4
EXPERTS_PER_GROUP = N_EXPERTS // N_GROUPS
TOP_K = 2
D_FF_EXPERT = 1024
MOE_BLOCK = 256

kernel_name = 'hybrid_gla_natten_conformer_groupmoe_dit'

def rmsnorm(x, g):
    xf = x.astype(jnp.float32)
    y = xf * lax.rsqrt(jnp.mean(xf * xf, axis=-1, keepdims=True) + EPS)
    return (y * g.astype(jnp.float32)).astype(x.dtype)

def layernorm(x, g, b):
    xf = x.astype(jnp.float32)
    xc = xf - jnp.mean(xf, axis=-1, keepdims=True)
    y = xc * lax.rsqrt(jnp.mean(xc * xc, axis=-1, keepdims=True) + EPS)
    return (y * g.astype(jnp.float32) + b.astype(jnp.float32)).astype(x.dtype)

def to_heads(a, n_heads):
    bb, n, _ = a.shape
    return a.reshape(bb, n, n_heads, -1).transpose(0, 2, 1, 3)

def from_heads(a):
    bb, h, n, d = a.shape
    return a.transpose(0, 2, 1, 3).reshape(bb, n, h * d)

def axial_rope(n, dim):
    t = jnp.arange(n)
    row = (t // GRID_W).astype(jnp.float32)
    col = (t % GRID_W).astype(jnp.float32)
    half = dim // 2
    inv = ROPE_BASE ** (-jnp.arange(0, half, 2, dtype=jnp.float32) / half)
    ang = jnp.concatenate([row[:, None] * inv, col[:, None] * inv], axis=-1)
    return jnp.cos(ang), jnp.sin(ang)

def apply_rope(x, cos, sin):
    cos = cos.astype(x.dtype)
    sin = sin.astype(x.dtype)
    x1, x2 = x[..., 0::2], x[..., 1::2]
    return jnp.stack([x1 * cos - x2 * sin, x1 * sin + x2 * cos], axis=-1).reshape(x.shape)

def gla_scan(q, k, v, log_g, s0):
    bb, h, n, dk = q.shape
    dv = v.shape[-1]
    nc = n // GLA_CHUNK
    order_mask = jnp.tril(jnp.ones((GLA_CHUNK, GLA_CHUNK), dtype=bool))[:, :, None]

    def chunks(a):
        return jnp.moveaxis(a.reshape(bb, h, nc, GLA_CHUNK, a.shape[-1]), 2, 0)

    def step(state, inp):
        qc, kc, vc, gc = [t.astype(jnp.float32) for t in inp]
        cum = jnp.cumsum(gc, axis=2)
        o_inter = jnp.einsum('bhtd,bhde->bhte', qc * jnp.exp(cum), state)
        decay = jnp.exp(jnp.where(order_mask, cum[:, :, :, None, :] - cum[:, :, None, :, :], -jnp.inf))
        att = jnp.einsum('bhtd,bhsd,bhtsd->bhts', qc, kc, decay)
        o = o_inter + jnp.einsum('bhts,bhse->bhte', att, vc)
        end = cum[:, :, -1:, :]
        new_state = (jnp.exp(end[:, :, 0, :])[..., None] * state
                     + jnp.einsum('bhsd,bhse->bhde', kc * jnp.exp(end - cum), vc))
        return new_state, o

    s_fin, o = lax.scan(step, s0, (chunks(q), chunks(k), chunks(v), chunks(log_g)))
    return jnp.moveaxis(o, 0, 2).reshape(bb, h, n, dv).astype(v.dtype), s_fin

def gla_inputs(q, k, v, a, wa_f, ba_f, wa_b, ba_b):
    q = to_heads(q, GLA_HEADS) * (GLA_DK ** -0.5)
    k = to_heads(k, GLA_HEADS)
    v = to_heads(v, GLA_HEADS)
    a_f, a_b = jnp.split(a, 2, axis=-1)
    g_f = to_heads(jax.nn.log_sigmoid((a_f @ wa_f + ba_f).astype(jnp.float32)) / GLA_TAU, GLA_HEADS)
    g_b = to_heads(jax.nn.log_sigmoid((a_b @ wa_b + ba_b).astype(jnp.float32)) / GLA_TAU, GLA_HEADS)
    return q, k, v, g_f, g_b

def gla_bidir(q, k, v, g_f, g_b, s_f, s_b):
    o_f, s_f_new = gla_scan(q, k, v, g_f, s_f)
    flip = lambda t: jnp.flip(t, axis=2)
    o_b, s_b_new = gla_scan(flip(q), flip(k), flip(v), flip(g_b), s_b)
    return o_f + flip(o_b), s_f_new, s_b_new

def gla_output(o, gate, g_norm):
    of = o.astype(jnp.float32)
    of = of * lax.rsqrt(jnp.mean(of * of, axis=-1, keepdims=True) + EPS)
    of = from_heads(of) * g_norm.astype(jnp.float32)
    return of.astype(gate.dtype) * jax.nn.silu(gate)

def na_heads(q, k, v):
    return to_heads(q, NA_HEADS) * (NA_DH ** -0.5), to_heads(k, NA_HEADS), to_heads(v, NA_HEADS)

def na_latent(q, k, v, kc, vc, rpb):
    bb, h, n, dh = q.shape
    rows = n // GRID_W
    kh = min(NA_KH, rows)
    kw = NA_KW
    cq = np.arange(GRID_W)
    c0 = np.clip(cq - kw // 2, 0, GRID_W - kw)
    colidx = c0[:, None] + np.arange(kw)[None, :]
    dcol = colidx - cq[:, None] + (NA_KW - 1)
    kg = k.reshape(bb, h, rows, GRID_W, dh)
    vg = v.reshape(bb, h, rows, GRID_W, dh)
    q_rows = jnp.moveaxis(q.reshape(bb, h, rows, GRID_W, dh), 2, 0)

    def row_block(args):
        qr, r = args
        r0 = jnp.clip(r - kh // 2, 0, rows - kh)
        kb = lax.dynamic_slice_in_dim(kg, r0, kh, axis=2)[:, :, :, colidx]
        vb = lax.dynamic_slice_in_dim(vg, r0, kh, axis=2)[:, :, :, colidx]
        drow = r0 + jnp.arange(kh) - r + (NA_KH - 1)
        bias = jnp.transpose(rpb[:, drow][:, :, dcol], (0, 2, 1, 3))
        s_loc = jnp.einsum('bhqd,bhiqjd->bhqij', qr, kb).astype(jnp.float32) + bias.astype(jnp.float32)
        s_ctx = jnp.einsum('bhqd,bhld->bhql', qr, kc).astype(jnp.float32)
        s = jnp.concatenate([s_loc.reshape(bb, h, GRID_W, kh * kw), s_ctx], axis=-1)
        p = jax.nn.softmax(s, axis=-1).astype(v.dtype)
        p_loc = p[..., :kh * kw].reshape(bb, h, GRID_W, kh, kw)
        return (jnp.einsum('bhqij,bhiqjd->bhqd', p_loc, vb)
                + jnp.einsum('bhql,bhld->bhqd', p[..., kh * kw:], vc))

    o = lax.map(row_block, (q_rows, jnp.arange(rows)))
    return jnp.moveaxis(o, 0, 2).reshape(bb, h, n, dh)

def na_context(qc, kc, vc):
    s = jnp.einsum('bhqd,bhkd->bhqk', qc, kc).astype(jnp.float32)
    p = jax.nn.softmax(s, axis=-1).astype(vc.dtype)
    return jnp.einsum('bhqk,bhkd->bhqd', p, vc)

def conv_module(u, w_dw, b_dw, ln_g, ln_b):
    a, gate = jnp.split(u, 2, axis=-1)
    hcv = a * jax.nn.sigmoid(gate)
    hcv = lax.conv_general_dilated(
        hcv, w_dw[:, None, :].astype(hcv.dtype), window_strides=(1,),
        padding=((CONV_K // 2, CONV_K // 2),), dimension_numbers=('NWC', 'WIO', 'NWC'),
        feature_group_count=CONV_WIDTH) + b_dw
    return jax.nn.silu(layernorm(hcv, ln_g, ln_b))

def moe(h, router_w, router_bias, wg, wu, wd):
    t, d = h.shape
    aff = jax.nn.sigmoid((h @ router_w).astype(jnp.float32))
    sel = aff + router_bias.astype(jnp.float32)
    gscore = lax.top_k(sel.reshape(t, N_GROUPS, EXPERTS_PER_GROUP), TOP_K)[0].sum(-1)
    gbest = jnp.argmax(gscore, axis=-1)
    in_group = (jnp.arange(N_EXPERTS) // EXPERTS_PER_GROUP)[None, :] == gbest[:, None]
    _, eidx = lax.top_k(jnp.where(in_group, sel, -jnp.inf), TOP_K)
    w = jnp.take_along_axis(aff, eidx, axis=-1)
    w = w / jnp.sum(w, axis=-1, keepdims=True)
    flat_e = eidx.reshape(-1)
    flat_tok = jnp.repeat(jnp.arange(t, dtype=jnp.int32), TOP_K)
    flat_w = w.reshape(-1)
    n_slots = flat_e.shape[0]
    order = jnp.argsort(flat_e)
    e_s, tok_s, w_s = flat_e[order], flat_tok[order], flat_w[order]
    counts = jnp.bincount(flat_e, length=N_EXPERTS)
    padded = (counts + MOE_BLOCK - 1) // MOE_BLOCK * MOE_BLOCK
    pad_end = jnp.cumsum(padded)
    pad_start = pad_end - padded
    start = jnp.cumsum(counts) - counts
    dest = pad_start[e_s] + jnp.arange(n_slots) - start[e_s]
    n_blocks = -(-n_slots // MOE_BLOCK) + N_EXPERTS
    p_rows = n_blocks * MOE_BLOCK
    row_tok = jnp.full((p_rows,), t, jnp.int32).at[dest].set(tok_s)
    row_w = jnp.zeros((p_rows,), h.dtype).at[dest].set(w_s.astype(h.dtype))
    blk_e = jnp.minimum(jnp.sum(pad_end[None, :] <= (jnp.arange(n_blocks) * MOE_BLOCK)[:, None], axis=-1),
                        N_EXPERTS - 1)
    h_pad = jnp.concatenate([h, jnp.zeros((1, d), h.dtype)], axis=0)
    xb = h_pad[row_tok].reshape(n_blocks, MOE_BLOCK, d)

    def expert_block(args):
        xe, e = args
        return (jax.nn.silu(xe @ wg[e]) * (xe @ wu[e])) @ wd[e]

    yb = lax.map(expert_block, (xb, blk_e)).reshape(p_rows, d)
    out = jnp.zeros((t + 1, d), h.dtype).at[row_tok].add(yb * row_w[:, None])
    return out[:t]

def setup_inputs(seed: int = 0) -> dict:
    key = jax.random.key(seed)
    ks = iter(jax.random.split(key, 40))
    nrm = lambda shape, s: jax.random.normal(next(ks), shape, jnp.float32) * s
    L, D = DEPTH, D_MODEL
    return {
        'x': nrm((BATCH, SEQ, D), 1.0),
        'c': nrm((BATCH, D), 1.0),
        'ctx': nrm((BATCH, CTX_LEN, D), 1.0),
        'c_ctx': nrm((D,), 1.0),
        'w_mod': nrm((L, D, 6 * D), 0.5 * D ** -0.5),
        'b_mod': nrm((L, 6 * D), 0.01),
        'g_mix': 1.0 + nrm((L, D), 0.01),
        'g_ffn': 1.0 + nrm((L, D), 0.01),
        'w_in': nrm((L, D, IN_COLS), D ** -0.5),
        'gla_wa_f': nrm((L, GLA_LOWRANK, GLA_QK), GLA_LOWRANK ** -0.5),
        'gla_ba_f': nrm((L, GLA_QK), 0.01),
        'gla_wa_b': nrm((L, GLA_LOWRANK, GLA_QK), GLA_LOWRANK ** -0.5),
        'gla_ba_b': nrm((L, GLA_QK), 0.01),
        'gla_g_norm': 1.0 + nrm((L, GLA_WIDTH), 0.01),
        'na_rpb': nrm((L, NA_HEADS, 2 * NA_KH - 1, 2 * NA_KW - 1), 0.1),
        'conv_w': nrm((L, CONV_K, CONV_WIDTH), CONV_K ** -0.5),
        'conv_b': nrm((L, CONV_WIDTH), 0.01),
        'conv_ln_g': 1.0 + nrm((L, CONV_WIDTH), 0.01),
        'conv_ln_b': nrm((L, CONV_WIDTH), 0.01),
        'w_out': nrm((L, MIX_WIDTH, D), MIX_WIDTH ** -0.5),
        'router_w': nrm((D, N_EXPERTS), D ** -0.5),
        'router_bias': nrm((N_EXPERTS,), 0.01),
        'w_gate': nrm((L, N_EXPERTS, D, D_FF_EXPERT), D ** -0.5),
        'w_up': nrm((L, N_EXPERTS, D, D_FF_EXPERT), D ** -0.5),
        'w_down': nrm((L, N_EXPERTS, D_FF_EXPERT, D), D_FF_EXPERT ** -0.5),
        'g_final': 1.0 + nrm((D,), 0.01),
    }

def reference(x, c, ctx, c_ctx, w_mod, b_mod, g_mix, g_ffn, w_in, gla_wa_f, gla_ba_f, gla_wa_b, gla_ba_b,
              gla_g_norm, na_rpb, conv_w, conv_b, conv_ln_g, conv_ln_b, w_out, router_w, router_bias,
              w_gate, w_up, w_down, g_final):
    b, n, d = x.shape
    split_at = [int(s) for s in np.cumsum(IN_SIZES)[:-1]]
    cos, sin = axial_rope(n, GLA_DK)
    s_lat = jax.nn.silu(c)
    s_ctx = jax.nn.silu(c_ctx)[None]
    xc = ctx
    for l in range(DEPTH):
        last = l == DEPTH - 1
        mx = jnp.split((s_lat @ w_mod[l] + b_mod[l])[:, None, :], 6, axis=-1)
        mc = jnp.split((s_ctx @ w_mod[l] + b_mod[l])[:, None, :], 6, axis=-1)
        hx = rmsnorm(x, g_mix[l]) * (1 + mx[1]) + mx[0]
        hc = rmsnorm(xc, g_mix[l]) * (1 + mc[1]) + mc[0]
        px = jnp.split(hx @ w_in[l], split_at, axis=-1)
        pc = jnp.split(hc @ w_in[l], split_at, axis=-1)
        gw = (gla_wa_f[l], gla_ba_f[l], gla_wa_b[l], gla_ba_b[l])
        q_c, k_c, v_c, gf_c, gb_c = gla_inputs(pc[0], pc[1], pc[2], pc[4], *gw)
        q_x, k_x, v_x, gf_x, gb_x = gla_inputs(px[0], px[1], px[2], px[4], *gw)
        q_x, k_x = apply_rope(q_x, cos, sin), apply_rope(k_x, cos, sin)
        zero = jnp.zeros((b, GLA_HEADS, GLA_DK, GLA_DV), jnp.float32)
        o_gc, st_f, st_b = gla_bidir(q_c, k_c, v_c, gf_c, gb_c, zero, zero)
        o_gx, _, _ = gla_bidir(q_x, k_x, v_x, gf_x, gb_x, st_f, st_b)
        nq_x, nk_x, nv_x = na_heads(px[5], px[6], px[7])
        nq_c, nk_c, nv_c = na_heads(pc[5], pc[6], pc[7])
        o_nx = na_latent(nq_x, nk_x, nv_x, nk_c, nv_c, na_rpb[l])
        o_cx = conv_module(px[8], conv_w[l], conv_b[l], conv_ln_g[l], conv_ln_b[l])
        y_x = jnp.concatenate([gla_output(o_gx, px[3], gla_g_norm[l]), from_heads(o_nx), o_cx], axis=-1) @ w_out[l]
        x = x + mx[2] * y_x
        h2x = rmsnorm(x, g_ffn[l]) * (1 + mx[4]) + mx[3]
        if last:
            x = x + mx[5] * moe(h2x.reshape(b * n, d), router_w, router_bias,
                                w_gate[l], w_up[l], w_down[l]).reshape(b, n, d)
        else:
            o_nc = na_context(nq_c, nk_c, nv_c)
            o_cc = conv_module(pc[8], conv_w[l], conv_b[l], conv_ln_g[l], conv_ln_b[l])
            y_c = jnp.concatenate([gla_output(o_gc, pc[3], gla_g_norm[l]), from_heads(o_nc), o_cc], axis=-1) @ w_out[l]
            xc = xc + mc[2] * y_c
            h2c = rmsnorm(xc, g_ffn[l]) * (1 + mc[4]) + mc[3]
            lc = xc.shape[1]
            y = moe(jnp.concatenate([h2x.reshape(b * n, d), h2c.reshape(b * lc, d)], axis=0),
                    router_w, router_bias, w_gate[l], w_up[l], w_down[l])
            x = x + mx[5] * y[:b * n].reshape(b, n, d)
            xc = xc + mc[5] * y[b * n:].reshape(b, lc, d)
    return rmsnorm(x, g_final)


_drawn_inputs = setup_inputs


def setup_inputs(seed=0):
    import zlib

    import numpy as np

    out = dict(_drawn_inputs(seed))
    spreads = {}
    factors = {'g_mix': 7.028,
     'gla_ba_f': 28.821,
     'gla_ba_b': 29.895,
     'gla_g_norm': 8.0,
     'na_rpb': 35.405,
     'conv_b': 30.4,
     'conv_ln_g': 64.0,
     'conv_ln_b': 64.0,
     'g_final': 31.796,
     'g_ffn': 8.0,
     'router_bias': 5.623}
    for name, (base, spread) in spreads.items():
        noise = np.random.default_rng([zlib.crc32(name.encode()), seed]).standard_normal(out[name].shape)
        drawn = base * np.exp(spread * noise) if base else spread * noise
        out[name] = jnp.asarray(drawn.astype(out[name].dtype))
    for name, factor in factors.items():
        out[name] = (out[name] * factor).astype(out[name].dtype)
    return out
```

```python
from contextlib import ExitStack

import numpy as np

import concourse.bass as bass
import concourse.mybir as mybir
from concourse.alu_op_type import AluOpType as ALU

F32 = mybir.dt.float32
BF16 = mybir.dt.bfloat16
I32 = mybir.dt.int32
ACT = mybir.ActivationFunctionType
AX = mybir.AxisListType

P = 128
D = 1024
KD = D // P
DEPTH = 2
SEQ = 256
CTX = 256
T = SEQ + CTX
NT = T // P
NX = SEQ // P
EPS = 1e-6
GRID_W = 64
GH, DK, DV = 4, 48, 96
DKP = 64
GQK, GWID = GH * DK, GH * DV
LR = 16
TAU = 16.0
NH, DH = 6, 64
NWID = NH * DH
NKH, NKW = 8, 16
CW, CK = 256, 31
COLS = 2848
UW = 384
E, FF = 16, 1024
NG, EG = 4, 4
SLOTS = T * 2
MAXB = SLOTS // P + E - 1
TAB = MAXB + 1
MOD = 6 * D
MW = 256
MU = D // MW
CLAMP = 80.0 * TAU
HALF = CK // 2
PADW = SEQ + 2 * HALF

C_QK, C_V, C_GATE, C_A = 0, 2 * GQK, 2 * GQK + GWID, 2 * GQK + 2 * GWID
C_NQ = C_A + 2 * LR
C_NK, C_NV = C_NQ + NWID, C_NQ + 2 * NWID
C_CONV = C_NQ + 3 * NWID


def constants():
    p = np.arange(P)
    parts = {}
    parts["ident"] = np.eye(P)
    rot = np.zeros((P, P))
    for i in range(0, P, 2):
        rot[i + 1, i] = -1.0
        rot[i, i + 1] = 1.0
    parts["rot"] = rot
    parts["before"] = (p[:, None] < p[None, :]).astype(float)
    parts["causal0"] = (p[:, None] <= p[None, :]).astype(float)
    parts["causal1"] = (p[:, None] >= p[None, :]).astype(float)
    half = DK // 2
    inv = 10000.0 ** (-np.arange(0, half, 2, dtype=np.float32) / half)
    t = np.arange(SEQ)
    ang = np.concatenate([(t // GRID_W)[:, None] * inv, (t % GRID_W)[:, None] * inv], -1).astype(np.float32)
    cos, sin = np.zeros((P, SEQ)), np.zeros((P, SEQ))
    for h in range(2):
        cos[h * DKP:h * DKP + DK] = np.repeat(np.cos(ang).T, 2, axis=0)
        sin[h * DKP:h * DKP + DK] = np.repeat(np.sin(ang).T, 2, axis=0)
    parts["cos"], parts["sin"] = cos, sin
    cq = p % GRID_W
    c0 = np.clip(cq - NKW // 2, 0, GRID_W - NKW)[:, None]
    ck = np.arange(GRID_W)[None, :]
    parts["window"] = np.where((ck >= c0) & (ck < c0 + NKW), 0.0, -1e30)
    parts["iota4"] = np.tile(np.arange(NG), (P, 1))
    parts["iota16"] = np.tile(np.arange(E), (P, 1))
    parts["iotab"] = np.tile(np.arange(TAB), (P, 1))
    first = np.ones((P, T))
    first[:, ::P] = 0.0
    parts["notfirst"] = first
    at, off = {}, 0
    for k, v in parts.items():
        at[k] = (off, off + v.shape[1])
        off += v.shape[1]
    return np.concatenate(list(parts.values()), 1).astype(np.float32), at


CONST, CAT = constants()
NCONST = CONST.shape[1]


class Ledger:

    def __init__(self, known):
        self.known, self.now, self.count, self.order, self.last = known, {}, {}, {}, {}

    def note(self, name, key, by):
        self.count[name] = self.count.get(name, 0) + by
        self.now[(name, key)] = self.count[name]


def build(nc, io, known):
    led = Ledger(known)
    ctx = ExitStack()
    with ctx:
        sems = {}

        def sem(name):
            if name not in sems:
                sems[name] = ctx.enter_context(nc.semaphore(name))
            return sems[name]

        def up(name, *key, by=1):
            led.note(name, key, by)
            return sem(name), by

        def dma(name, *key):
            return up(name, *key, by=16)

        def past(name, *key):
            assert not known or (name, key) in known, (name, key)
            return sem(name), known.get((name, key), 1)

        def sb(name, shape, dt=F32):
            return ctx.enter_context(nc.sbuf_tensor(name, shape, dt))

        const = sb("const", [P, NCONST])

        def cst(name):
            a, b = CAT[name]
            return const[:, a:b]

        ident = cst("ident")
        ones = sb("ones", [P, P])
        zeros = sb("zeros", [P, 512], BF16)
        zeroi = sb("zeroi", [P, TAB], I32)
        tokid = sb("tokid", [P, NT], I32)
        xres = sb("xres", [P, NT, D])
        ND = 3
        dring = sb("dring", [P, ND, KD * UW])
        rows = sb("rows", [P, 4, D])
        scol = sb("scol", [P, KD, 2])
        rw = sb("rw", [P, KD, E])
        rbias = sb("rbias", [P, E])
        wap = sb("wap", [2 * LR, 2, GH, DKP])
        bacol = sb("bacol", [P, 2, 2])
        gnrow = sb("gnrow", [P, GWID])
        crow = sb("crow", [CK + 3, CW])
        ccol = sb("ccol", [P, 2, CK + 3])
        stat = sb("stat", [P, 64])
        rt = sb("rt", [P, 14, NT * E])
        rti = sb("rti", [P, 2 * NT], I32)
        tabi = sb("tabi", [P, 32], I32)
        idx = sb("idx", [P, 1], I32)

        NAR = 12 * 2048 + 6144
        arena = sb("arena", [P, NAR])
        ends = {}

        def carve(name, n, at):
            ends[name] = (at, at + n)
            assert at + n <= NAR, name
            return arena[:, at:at + n]

        MR = 12 * 2048
        o = 0
        tmp = carve("tmp", 4096, o); o += 4096
        q = carve("q", 2 * T, o); o += 2 * T
        k = carve("k", 2 * T, o); o += 2 * T
        v = carve("v", NT * GWID, o); o += NT * GWID
        gate = carve("gate", NT * GWID, o); o += NT * GWID
        aT = carve("aT", T, o); o += T
        cum = carve("cum", 4 * T, o); o += 4 * T
        nq = carve("nq", 3 * T, o); o += 3 * T
        nk = carve("nk", 3 * T, o); o += 3 * T
        nv = carve("nv", NT * NWID, o); o += NT * NWID
        bias = carve("bias", 2 * NH * SEQ, o); o += 2 * NH * SEQ
        cpad = carve("cpad", 2 * 2 * PADW, o); o += 2 * 2 * PADW
        ST = carve("ST", 1024, o); o += 1024
        kit = carve("kit", 512, o); o += 512
        states = carve("states", 4 * 2 * DV, o); o += 4 * 2 * DV
        cacc = carve("cacc", 1024, o); o += 1024
        assert o <= MR, o
        hT = carve("hT", KD * T, MR)
        nh = carve("nh", 2048, MR + 4096)
        gout = arena[:, 4096:4096 + NT * GWID]
        mring = arena[:, 0:MR].rearrange("p (u n) -> p u n", u=12)
        xe = carve("xe", D, MR)
        xT = carve("xT", D, MR + 1024)
        hb = carve("hb", D, MR + 2048)
        hbT = carve("hbT", D, MR + 3072)
        yb = carve("yb", D, MR + 4096)
        comb = arena[:, MR:MR + 4096].rearrange("p (b k n) -> p b k n", b=2, k=2)

        q3 = q.rearrange("p (f t) -> p f t", f=2)
        k3 = k.rearrange("p (f t) -> p f t", f=2)
        v3 = v.rearrange("p (t n) -> p t n", t=NT)
        gate3 = gate.rearrange("p (t n) -> p t n", t=NT)
        cum4 = cum.rearrange("p (d f t) -> p d f t", d=2, f=2)
        nout3 = hT[:, 0:NT * NWID].rearrange("p (t n) -> p t n", t=NT)
        mrow, mgain = rows[0:2, 2, :], rows[0:2, 3, :]
        nq3 = nq.rearrange("p (f t) -> p f t", f=3)
        nk3 = nk.rearrange("p (f t) -> p f t", f=3)
        nv3 = nv.rearrange("p (t n) -> p t n", t=NT)
        bias4 = bias.rearrange("p (q h n) -> p q h n", q=2, h=NH)
        cp4 = cpad.rearrange("p (c s n) -> p c s n", c=2, s=2)
        ca4 = cacc.rearrange("p (c s n) -> p c s n", c=2, s=2)
        wqk = tmp.rearrange("p (k h d) -> p k h d", k=KD, h=2 * GH)
        hT3 = hT.rearrange("p (k t) -> p k t", k=KD)
        gout3 = gout.rearrange("p (t n) -> p t n", t=NT)
        X64, X32, Qd, Kd, QI, KI = (tmp[:, i * T:(i + 1) * T] for i in range(6))
        tb = sb("tb", [42, P])

        psum = [ctx.enter_context(nc.psum_tensor(f"ps{i}", [P, 512], F32)) for i in range(8)]

        modd = nc.dram_tensor("modd", [DEPTH, 2, MOD], F32)
        toep = nc.dram_tensor("toep", [DEPTH * 42 * GRID_W * P], F32)
        h2d = nc.dram_tensor("h2d", [DEPTH, T, D], F32)
        rtok = [nc.dram_tensor(f"rtok{l}", [TAB * P, 1], I32) for l in range(DEPTH)]
        yd = [nc.dram_tensor(f"yd{l}", [TAB * P, D], F32) for l in range(DEPTH)]
        h2l = [nc.dram_tensor(f"h2l{l}", [SEQ if l == DEPTH - 1 else T, D], F32) for l in range(DEPTH)]

        jobs = []

        def bank_of(key):
            return psum[4 + known.get(("order",), {}).get(key, 0) % 4]

        def take(pe, *key):
            jobs.append(key)
            led.order[key] = len(jobs) - 1
            n = len(jobs) - 1
            if n >= 4:
                pe.wait_ge(*emptied(*jobs[n - 4]))
            return psum[4 + n % 4]

        def emptied(*key):
            for name in ("w_act", "w_dve"):
                if (name, key) in known:
                    return sem(name), known[(name, key)]
            assert not known, key
            return sem("w_act"), 1

        dunits = []

        def dslot(key):
            return known.get(("dorder",), {}).get(key, 0) % ND

        def landed(*key):
            return past(f"dense{dslot(key)}", *key)

        def released(key):
            kind, l, u = key
            if kind == "mod":
                return past("w_full", "mod", l, *u)
            if kind == "out":
                return past("y_full", l, tiles_out(l)[-1], 1)
            if u == "qk":
                return past("wqk", l)
            return past("w_full", *{"v": ("v", l, NT - 1), "gate": ("gate", l, tiles_out(l)[-1]), "nq": ("nq", l, 2),
                                    "nk": ("nk", l, 2), "nv": ("nv", l, NT - 1), "c0": ("ca", l, 1), "c1": ("a", l)}[u])

        def tiles_out(l):
            return range(NX if l == DEPTH - 1 else NT)

        def streams_out(l):
            return 1 if l == DEPTH - 1 else 2

        def mod_late(l):
            return [(0, 2), (0, 3), (0, 4), (0, 5), (1, 0), (1, 1)] if l == 0 else [(l, 2), (l, 3), (l, 4), (l, 5)]

        def mod_units(l):
            return [(ml, (part, u)) for ml, part in mod_late(l) for u in range(MU)]

        def share(items, n, of):
            return items[n * len(items) // of:(n + 1) * len(items) // of]

        def na_between(l):
            return (2, 1, 3) if l < DEPTH - 1 else (1, 1, 1)

        GROUPS = [(d, f) for d in range(2) for f in range(2)]

        def na_steps(l, n_g, stage):
            before, between, behind = na_between(l)
            at = n_g * (before + between + behind) + (0, before, before + between)[stage]
            return range(at, at + na_between(l)[stage])

        def zbuf(n_g):
            return tmp[:, n_g * T:(n_g + 1) * T], tmp[:, (4 + n_g) * T:(5 + n_g) * T]

        def rows_load(eng, l, which):
            S = streams_out(l)
            plan = {"mix": [(0, 0, 1), (1, 0, 0), (2, 1, 1), (3, 1, 0)],
                    "gate_mix": [(s, s, 2) for s in range(S)],
                    "ffn": [(2 * s, s, 4) for s in range(S)] + [(2 * s + 1, s, 3) for s in range(S)],
                    "gate_ffn": [(s, s, 5) for s in range(S)]}[which]
            before = {"mix": ("rows_used", l - 1, "gate_ffn") if l else ("modd", 0, 1),
                      "gate_mix": ("rows_used", l, "mix"), "ffn": ("rows_used", l, "gate_mix"),
                      "gate_ffn": ("rows_used", l, "ffn")}[which]
            eng.wait_ge(*past(*before))
            for slot, s, part in plan:
                eng.dma_start(rows[:, slot, :], modd[l, s:s + 1, part * D:(part + 1) * D].to_broadcast([P, D])
                              ).then_inc(*dma("rows", l, which))
            if which == "gate_ffn" and l == DEPTH - 1:
                eng.dma_start(rows[:, 2, :], io["g_final"].rearrange("(a d) -> a d", a=1).to_broadcast([P, D])
                              ).then_inc(*dma("rows", l, which))

        def na_sc(b):
            return nh[:, b * 512:(b + 1) * 512]

        def na_pt(b):
            return nh[:, 1024 + b * 512:1024 + (b + 1) * 512]

        def lnb(i):
            return tmp[:, i * 512:(i + 1) * 512]

        def na_list(l):
            return [(h, t) for t in tiles_out(l) for h in range(NH)]

        def norm_act(act, did, own, l, which, tiles):
            for t in tiles:
                act.wait_ge(*past("xready", l, which, t))
                if t >= 2:
                    act.wait_ge(*past("w_full", "ht", l, which, t - 2, 1))
                    if which == "ffn":
                        act.wait_ge(*past(f"h2d{t - 2}", l, t - 2))
                did(act.activation(nh[:, (t % 2) * D:(t % 2 + 1) * D], xres[:, t, :], ACT.Square,
                                   accum_out=stat[:, 24 + t:25 + t]), "sumsq", l, which, t)
                act.wait_ge(*past("nvar", l, which, t))
                did(act.activation(stat[:, 28 + t:29 + t], stat[:, 28 + t:29 + t], ACT.Sqrt), "nstd", l, which, t)

        def stat2(f):
            return ST[:, f * SEQ:(f + 1) * SEQ]

        def gla_order(d):
            return [2, 3, 0, 1] if d == 0 else [3, 2, 1, 0]

        block = ctx.enter_context(nc.Block())

        @block.sync
        def _(sp):
            def dense_load(key, pieces):
                n = len(dunits)
                dunits.append(key)
                led.order[("d",) + key] = n
                if n >= ND:
                    sp.wait_ge(*released(dunits[n - ND]))
                for i, (dst, src) in enumerate(pieces(dring[:, n % ND, :])):
                    sp.dma_start(dst, src).then_inc(*dma(f"dense{n % ND}", *key))

            def wide(src):
                w = src.shape[1]
                return lambda slot: [(slot[:, 0:KD * w].rearrange("p (k n) -> p k n", k=KD),
                                      src.rearrange("(k p) n -> p k n", p=P))]

            sp.dma_start(const[:, :], io["const"]).then_inc(*dma("const"))
            for s, src in enumerate((io["c"], io["c_ctx"].rearrange("(a d) -> a d", a=1))):
                sp.dma_start(nh[s:s + 1, 0:D], src).then_inc(*dma("crows", s))
            for s, src in enumerate((io["x"], io["ctx"])):
                sp.dma_start(xres[:, 2 * s:2 * s + 2, :], src.rearrange("b (t p) d -> p (b t) d", p=P)).then_inc(*dma("xin", s))
            sp.dma_start(rw[:, :, :], io["router_w"].rearrange("(k p) e -> p k e", p=P)).then_inc(*dma("rw", 0))
            sp.dma_start(rbias[:, :], io["router_bias"].rearrange("(a e) -> a e", a=1).to_broadcast([P, E])).then_inc(*dma("rw", 1))
            def mod_load(l, pu):
                part, u = pu
                c0 = part * D + u * MW
                dense_load(("mod", l, pu), wide(io["w_mod"][l, :, c0:c0 + MW]))

            for part in range(2):
                for u in range(MU):
                    mod_load(0, (part, u))
            for l in range(DEPTH):
                w = io["w_in"][l]
                cols = {"qk": C_QK, "v": C_V, "gate": C_GATE, "nq": C_NQ, "nk": C_NK, "nv": C_NV}
                dense_load(("in", l, "c0"), wide(w[:, C_CONV:C_CONV + 256]))

                def last_unit(slot, w=w):
                    return [(slot[:, 0:KD * 256].rearrange("p (k n) -> p k n", k=KD),
                             w[:, C_CONV + 256:C_CONV + 512].rearrange("(k p) n -> p k n", p=P)),
                            (slot[:, KD * 256:KD * 288].rearrange("p (k n) -> p k n", k=KD),
                             w[:, C_A:C_A + 2 * LR].rearrange("(k p) n -> p k n", p=P))]
                dense_load(("in", l, "c1"), last_unit)
                for nm in ("qk", "v", "gate", "nq", "nk", "nv"):
                    dense_load(("in", l, nm), wide(w[:, cols[nm]:cols[nm] + UW]))
                for ml, pu in mod_units(l):
                    mod_load(ml, pu)
                for u, (a, b) in enumerate(((0, 3), (3, 6), (6, 8))):
                    dense_load(("out", l, u), lambda slot, a=a, b=b, l=l: [
                        (slot[:, 0:(b - a) * D].rearrange("p (k n) -> p k n", n=D),
                         io["w_out"][l, a * P:b * P, :].rearrange("(k p) n -> p k n", p=P))])
                sp.wait_ge(*past("mixed", l))
                sp.wait_ge(*past("cact", l, 1))
                sp.wait_ge(*past("w_full", "gt", l, tiles_out(l)[-1]))
                gsem = [sem(f"m{l}_land{j}") for j in range(12)]
                guse, duse = sem(f"m{l}_gused"), sem(f"m{l}_dused")

                def gu_unit(m, pos, e):
                    src = io["w_gate"] if m % 2 == 0 else io["w_up"]
                    kk = m // 2
                    sp.dma_start(mring[:, pos, :].rearrange("p (k n) -> p k n", k=2),
                                 src[l, bass.ds(e, 1), kk * 256:(kk + 1) * 256, :].rearrange("a (k p) n -> p (a k) n", p=P)
                                 ).then_inc(gsem[pos], 16)

                def d_unit(m, pos, e):
                    sp.dma_start(mring[:, pos, :].rearrange("p (k n) -> p k n", k=2),
                                 io["w_down"][l, bass.ds(e, 1), m * 256:(m + 1) * 256, :].rearrange("a (k p) n -> p (a k) n", p=P)
                                 ).then_inc(gsem[pos], 16)

                sp.sem_inc(guse, 8)
                sp.sem_inc(duse, 4)
                for m in range(8):
                    gu_unit(m, m, 0)
                sp.wait_ge(*past("table", l))
                nb = sp.value_load(tabi[0:1, TAB:TAB + 1], min_val=4, max_val=MAXB)
                e0 = sp.value_load(tabi[0:1, 0:1], min_val=0, max_val=E - 1)
                redo = sem(f"m{l}_redo")
                with sp.If(e0 > 0):
                    for m in range(8):
                        sp.wait_ge(gsem[m], 16)
                    for m in range(8):
                        src = io["w_gate"] if m % 2 == 0 else io["w_up"]
                        sp.dma_start(mring[:, m, :].rearrange("p (k n) -> p k n", k=2),
                                     src[l, bass.ds(e0, 1), m // 2 * 256:(m // 2 + 1) * 256, :].rearrange("a (k p) n -> p (a k) n", p=P)
                                     ).then_inc(redo, 16)
                    sp.wait_ge(redo, 8 * 16)
                sp.sem_inc(sem(f"m{l}_first"), 1)
                with sp.Fori(1, nb) as i:
                    e = sp.value_load(tabi[0:1, bass.ds(i, 1)], min_val=0, max_val=E - 1)
                    for m in range(8):
                        sp.wait_ge(guse, i * 8 + (m + 1))
                        gu_unit(m, (8 + m) % 12, e)
                    ep = sp.value_load(tabi[0:1, bass.ds(i - 1, 1)], min_val=0, max_val=E - 1)
                    for m in range(4):
                        sp.wait_ge(duse, (i - 1) * 4 + (m + 1))
                        d_unit(m, 4 + m, ep)
                el = sp.value_load(tabi[0:1, bass.ds(nb - 1, 1)], min_val=0, max_val=E - 1)
                for m in range(4):
                    sp.wait_ge(guse, nb * 8 + (m + 1))
                    d_unit(m, 8 + m, el)

        @block.gpsimd
        def _(pool):
            pool.memset(ones[:, :], 1.0).then_inc(*up("fill", "ones"))
            def carry_wait():
                pool.sem_inc(sem("pool_pace"), 1)

            pool.memset(zeros[:, :], 0.0).then_inc(*up("fill", "zeros"))
            pool.memset(zeroi[:, :], 0).then_inc(*up("fill", "zeroi"))
            pool.memset(wap[:, :, :, :], 0.0).then_inc(*up("fill", "wap"))
            pool.memset(bacol[:, :, :], 0.0).then_inc(*up("fill", "bacol"))
            pool.memset(tb[:, :], 0.0).then_inc(*up("fill", "tb"))
            pool.iota(tokid[:, :], [[P, NT]], base=0, channel_multiplier=1).then_inc(*up("fill", "tokid"))
            pool.wait_ge(*past("fill", "zeroi"))
            for l in range(DEPTH):
                pool.dma_start(rtok[l][:, :].rearrange("(p n) a -> p (n a)", p=P), zeroi[:, :]).then_inc(*dma(f"rtok{l}", 0))

            def mod_part(l, part):
                for s_ in range(2):
                    pool.dma_start(mrow[s_:s_ + 1, :], io["b_mod"][l:l + 1, part * D:(part + 1) * D]).then_inc(*dma("mbias", l, part))
                    if part in (1, 4):
                        pool.dma_start(mgain[s_:s_ + 1, :], io["g_mix" if part == 1 else "g_ffn"][l:l + 1, :]
                                       ).then_inc(*dma("mbias", l, part))
                pool.wait_ge(*past("modrow", l, part))
                pool.dma_start(modd[l, :, part * D:(part + 1) * D], mrow).then_inc(*dma("modd", l, part))
                pool.wait_ge(*past("modd", l, part))

            def small(l):
                if l:
                    pool.wait_ge(*past("gout", l - 1, tiles_out(l - 1)[-1]))
                    pool.wait_ge(*emptied("cc", l - 1))
                else:
                    for nm in ("wap", "bacol", "tb"):
                        pool.wait_ge(*past("fill", nm))
                for d, nm in enumerate(("gla_wa_f", "gla_wa_b")):
                    pool.dma_start(wap[d * LR:(d + 1) * LR, d, :, 0:DK],
                                   io[nm][l].rearrange("r (h d) -> r h d", h=GH)).then_inc(*dma("small", l))
                for d, nm in enumerate(("gla_ba_f", "gla_ba_b")):
                    for hh in range(2):
                        for f in range(2):
                            h = 2 * f + hh
                            pool.dma_start(bacol[hh * DKP:hh * DKP + DK, d, f:f + 1],
                                           io[nm][l, h * DK:(h + 1) * DK].rearrange("(d a) -> d a", a=1)
                                           ).then_inc(*dma("small", l))
                pool.dma_start(gnrow[:, :], io["gla_g_norm"][l:l + 1, :].to_broadcast([P, GWID])).then_inc(*dma("small", l))
                pool.dma_start(crow[0:CK, :], io["conv_w"][l]).then_inc(*dma("small", l))
                for j, nm in enumerate(("conv_b", "conv_ln_g", "conv_ln_b")):
                    pool.dma_start(crow[CK + j:CK + j + 1, :], io[nm][l:l + 1, :]).then_inc(*dma("small", l))
                if l:
                    pool.wait_ge(*past("toep", l - 1))
                for h in range(NH):
                    pool.dma_start(tb[7 * h:7 * h + 7, 48:79], io["na_rpb"][l, h, 4:11, :]).then_inc(*dma("tb", l))
                pool.wait_ge(*past("tb", l))
                pool.dma_start(bass.AP(toep, l * 42 * GRID_W * P, [[GRID_W * P, 42], [P, GRID_W], [1, P]]),
                               tb[:, :].rearrange("p (a n) -> p a n", a=1).to_broadcast([42, GRID_W, P])
                               ).then_inc(*dma("toep", l))

            for part in range(2):
                mod_part(0, part)
            rows_load(pool, 0, "mix")
            small(0)
            for l in range(DEPTH):
                if l:
                    pool.wait_ge(*past("arena_free", l))
                pool.memset(cpad, 0.0).then_inc(*up("padded", l, 0))
                pool.memset(wqk[:, :, :, DK:DKP], 0.0).then_inc(*up("padded", l, 1))
                pool.wait_ge(*past("toep", l))
                for qt in range(2):
                    for rl in range(2):
                        r = 2 * qt + rl
                        for h in range(NH):
                            off = (l * 42 + h * 7 + 3 - r) * GRID_W * P + GRID_W - 1
                            pool.dma_start(
                                bias4[64 * rl:64 * rl + 64, qt, h, :].rearrange("p (i n) -> p i n", i=4),
                                bass.AP(toep, off, [[P - 1, GRID_W], [GRID_W * P, 4], [1, GRID_W]])
                            ).then_inc(*dma("bias", l))
                least = (SLOTS if l < DEPTH - 1 else 2 * SEQ) // P
                if l == 0:
                    pool.wait_ge(*past("fill", "zeros"))
                n = (TAB - least) * D // 256
                pool.dma_start(yd[l][least * P:, :].rearrange("(p a) d -> p (a d)", p=P).rearrange("p (a n) -> p a n", a=n),
                               zeros[:, :].bitcast(F32).rearrange("p (a n) -> p a n", a=1).to_broadcast([P, n, 256])
                               ).then_inc(*dma("ydfill", l))
                pool.wait_ge(*past("rows_used", l, "mix"))
                for ml, part in mod_late(l):
                    mod_part(ml, part)
                rows_load(pool, l, "gate_mix")
                rows_load(pool, l, "ffn")
                for t in tiles_out(l):
                    pool.wait_ge(*past("h2", l, t))
                    pool.dma_start(h2l[l][t * P:(t + 1) * P, :], nh[:, (t % 2) * D:(t % 2 + 1) * D]).then_inc(*dma(f"h2d{t}", l, t))
                pool.wait_ge(*past(f"rtok{l}", 0))
                pool.wait_ge(*past("dest", l))
                for t in tiles_out(l):
                    for kk in range(2):
                        pool.indirect_dma_start(
                            out=rtok[l][:, :], out_offset=bass.IndirectOffsetOnAxis(ap=rti[:, 2 * t + kk:2 * t + kk + 1], axis=0),
                            in_=tokid[:, t:t + 1], in_offset=None).then_inc(*dma(f"rtok{l}", 1))
                pool.wait_ge(*past(f"rtok{l}", 1))
                for t in tiles_out(l):
                    pool.wait_ge(*past(f"h2d{t}", l, t))
                pool.wait_ge(*past("routed", l))
                nb = pool.value_load(tabi[0:1, TAB:TAB + 1], min_val=4, max_val=MAXB)
                s_idx, s_xg, s_xf = sem(f"m{l}_idx"), sem(f"m{l}_xg"), sem(f"m{l}_xf")

                def gather(idx_src, n_idx):
                    pool.dma_start(idx[:, :], idx_src).then_inc(s_idx, 16)
                    pool.wait_ge(s_idx, n_idx)
                    carry_wait()
                    pool.indirect_dma_start(out=xe[:, :], out_offset=None, in_=h2l[l][:, :],
                                            in_offset=bass.IndirectOffsetOnAxis(ap=idx[:, 0:1], axis=0)).then_inc(s_xg, 16)

                gather(rtok[l][0:P, :], 16)
                with pool.Fori(1, nb + 1) as i:
                    pool.wait_ge(s_xf, i)
                    carry_wait()
                    gather(rtok[l][bass.ds(i * P, P), :], (i + 1) * 16)
                rows_load(pool, l, "gate_ffn")
                if l < DEPTH - 1:
                    small(l + 1)
                pool.wait_ge(sem(f"m{l}_yd"), nb * 16 + 16)
                pool.wait_ge(s_xf, nb + 1)
                pool.wait_ge(sem(f"m{l}_xe"), nb * 2 + 2)
                pool.wait_ge(sem(f"m{l}_dused"), nb * 4 + 4)
                carry_wait()
                for t in tiles_out(l):
                    if t >= 2:
                        pool.wait_ge(*past("combined", l, t - 2))
                    for kk in range(2):
                        pool.indirect_dma_start(
                            out=comb[:, t % 2, kk, :], out_offset=None, in_=yd[l][:, :],
                            in_offset=bass.IndirectOffsetOnAxis(ap=rti[:, 2 * t + kk:2 * t + kk + 1], axis=0)
                        ).then_inc(*dma(f"comb{t % 2}", l, t))
                if l < DEPTH - 1:
                    rows_load(pool, l + 1, "mix")

        @block.scalar
        def _(act):
            last = []

            def did(ins, *key):
                ins.then_inc(*up(*(key or ("act_chain",))))
                last[:] = [(sem(key[0] if key else "act_chain"), led.count[key[0] if key else "act_chain"])]

            def own():
                act.wait_ge(*last[0])

            def full(*key):
                act.wait_ge(*past("w_full", *key))
                return bank_of(key)

            act.wait_ge(*past("crows", 1))
            did(act.activation(nh[0:2, D:2 * D], nh[0:2, 0:D], ACT.Silu), "csilu")
            act.wait_ge(*emptied("scol"))
            for l in range(DEPTH):
                norm_act(act, did, own, l, "mix", range(NT))
                act.wait_ge(*landed("in", l, "qk"))
                act.wait_ge(*past("padded", l, 1))
                did(act.copy(wqk[:, :, :, 0:DK], dring[:, dslot(("in", l, "qk")), :].rearrange("p (k h d) -> p k h d", k=KD, h=2 * GH)),
                    "wqk", l)
                for ct in range(2):
                    n = streams_out(l)
                    did(act.activation(ca4[:, ct, 0:n, :],
                                       full("cg", l, ct)[:, 0:n * SEQ].rearrange("p (s n) -> p s n", s=n), ACT.Sigmoid),
                        "w_act", "cg", l, ct)
                for f in range(2):
                    did(act.copy(k3[:, f, :], full("k", l, f)[:, :]), "w_act", "k", l, f)
                for n_g, (d, f) in enumerate(GROUPS):
                    act.wait_ge(*past("zready", l, d, f))
                    did(act.activation(zbuf(n_g)[1], cum4[:, d, f, :], ACT.Abs))
                    own()
                    did(act.activation(zbuf(n_g)[1], zbuf(n_g)[1], ACT.Exp, scale=-1.0))
                own()
                for n_g, (d, f) in enumerate(GROUPS):
                    did(act.activation(zbuf(n_g)[1], zbuf(n_g)[1], ACT.Ln, bias=1.0), "zln", l, d, f)
                for t in tiles_out(l):
                    did(act.activation(gate3[:, t, :], full("gate", l, t)[:, 0:GWID], ACT.Silu), "w_act", "gate", l, t)
                for f in range(3):
                    did(act.mul(nq3[:, f, :], full("nq", l, f)[:, :], DH ** -0.5), "w_act", "nq", l, f)
                for t in range(NT):
                    did(act.copy(nv3[:, t, :], full("nv", l, t)[:, 0:NWID]), "w_act", "nv", l, t)
                lst = na_list(l)

                def na_exp(n):
                    h, t = lst[n]
                    kn = T if t < NX else CTX
                    b = n % 2
                    act.wait_ge(*past("nmax", l, h, t))
                    if n >= 2:
                        act.wait_ge(*past("w_full", "pt", l, *lst[n - 2]))
                    did(act.activation(na_sc(b)[:, 0:kn], full("s", l, h, t)[:, 0:kn], ACT.Exp,
                                       bias=stat[:, 16 + b:17 + b], accum_out=stat[:, 20 + b:21 + b]),
                        "w_act", "s", l, h, t)

                def na(steps):
                    for n in steps:
                        if n + 1 < len(lst):
                            na_exp(n + 1)

                na_exp(0)
                for n_g, (d, f) in enumerate(GROUPS):
                    act.wait_ge(*past("diffs", l, d, f))
                    qs, ks = (1, 0) if d == 0 else (0, 1)
                    did(act.activation(KI, KI, ACT.Exp, scale=-1.0 / TAU), "kexp", l, d, f)
                    for X, n, h in ((X64, 4, 64), (X32, 8, 32)):
                        X4 = X.rearrange("p (n two h) -> p n two h", two=2, h=h)
                        did(act.activation(X4[:, :, qs, :], X4[:, :, qs, :], ACT.Exp, scale=1.0 / TAU))
                        did(act.activation(X4[:, :, ks, :], X4[:, :, ks, :], ACT.Exp, scale=-1.0 / TAU))
                    did(act.activation(Kd, Qd, ACT.Exp, scale=-1.0 / TAU))
                    own()
                    did(act.activation(Qd, Qd, ACT.Exp, scale=1.0 / TAU))
                    did(act.activation(QI, cum4[:, d, f, :], ACT.Exp, scale=1.0 / TAU))
                    endc = cum4[:, d, f, :].rearrange("p (t n) -> p t n", t=NT)[:, :, P - 1 if d == 0 else 0]
                    did(act.activation(stat[:, 0:NT], endc, ACT.Exp, scale=1.0 / TAU), "factors", l, d, f)
                    na(na_steps(l, n_g, 0))
                    did(act.copy(kit.rearrange("p (t n) -> p t n", t=NT),
                                 full("kt", l, d, f)[:, :].rearrange("p (t n) -> p t n", t=NT)), "w_act", "kt", l, d, f)
                    na(na_steps(l, n_g, 1))
                    na(na_steps(l, n_g, 2))
                act.wait_ge(*past("cvar", l))
                did(act.activation(lnb(2), lnb(2), ACT.Sqrt), "cstd", l)
                for t in tiles_out(l):
                    act.wait_ge(*past("group_done", l, 1, 1))
                    if t:
                        act.wait_ge(*past("gsq_used", l, t - 1))
                    did(act.activation(ST[:, 0:GWID], psum[t][:, 0:GWID], ACT.Square), "gsq", l, t)
                    act.wait_ge(*past("gvar", l, t))
                    did(act.activation(stat[:, 8:12], stat[:, 8:12], ACT.Sqrt), "gstd", l, t)
                n = streams_out(l)
                for ct in range(2):
                    act.wait_ge(*past("cnorm", l, ct))
                    did(act.activation(hT3[:, 6 + ct, 0:n * SEQ], ca4[:, ct, 0:n, :].rearrange("p s n -> p (s n)"),
                                       ACT.Silu, scale=ccol[:, ct, CK + 1:CK + 2], bias=ccol[:, ct, CK + 2:CK + 3]), "cact", l, ct)
                for t in tiles_out(l):
                    did(act.copy(hT3[:, 0:3, t * P:(t + 1) * P],
                                 full("gt", l, t)[:, 0:GWID].rearrange("p (k n) -> p k n", k=3)), "w_act", "gt", l, t)
                norm_act(act, did, own, l, "ffn", tiles_out(l))
                n = len(tiles_out(l)) * E
                did(act.activation(rt[:, 0, 0:n], full("lg", l)[:, 0:n], ACT.Sigmoid), "w_act", "lg", l)
                act.wait_ge(*past("routed", l))
                nb = act.value_load(tabi[0:1, TAB:TAB + 1], min_val=4, max_val=MAXB)
                s = {x: sem(f"m{l}_{x}") for x in ("gused", "dused", "sil", "hf", "he", "yd", "ye", "mul")}
                act.sem_inc(s["yd"], 16)
                act.sem_inc(s["ye"], 2)
                act.wait_ge(*past("ydfill", l))

                def silu(n):
                    act.wait_ge(s["gused"], n * 8 + 8)
                    for c in range(2):
                        act.activation(hb[:, c * 512:(c + 1) * 512], psum[c][:, :], ACT.Silu).then_inc(s["sil"], 1)

                def h_out(n):
                    act.wait_ge(s["hf"], n)
                    for c in range(2):
                        act.copy(hbT[:, c * 512:(c + 1) * 512], psum[6 + c][:, :]).then_inc(s["he"], 1)

                def y_out(n, dst):
                    act.wait_ge(s["dused"], n * 4 + 4)
                    act.wait_ge(s["yd"], n * 16)
                    for c in range(2):
                        act.copy(yb[:, c * 512:(c + 1) * 512], psum[4 + c][:, :]).then_inc(s["ye"], 1)
                    act.wait_ge(s["ye"], n * 2 + 2)
                    act.dma_start(dst, yb[:, :]).then_inc(s["yd"], 16)

                silu(1)
                h_out(1)
                with act.Fori(1, nb) as i:
                    silu(i + 1)
                    y_out(i, yd[l][bass.ds((i - 1) * P, P), :])
                    h_out(i + 1)
                y_out(nb, yd[l][bass.ds((nb - 1) * P, P), :])
            norm_act(act, did, own, DEPTH, "fin", range(NX))
            for t in range(NX):
                act.wait_ge(*past("final", t))
                act.dma_start(io["out"][0, t * P:(t + 1) * P, :], nh[:, t * D:(t + 1) * D]).then_inc(*dma("out", t))
            act.wait_ge(*past("out", NX - 1))

        @block.vector
        def _(dve):
            last = []

            def did(ins, *key):
                ins.then_inc(*up(*(key or ("dve_chain",))))
                last[:] = [(sem(key[0] if key else "dve_chain"), led.count[key[0] if key else "dve_chain"])]

            def own():
                dve.wait_ge(*last[0])

            def mark(*key):
                own()
                did(dve.engine_nop(), *key)

            def full(*key):
                dve.wait_ge(*past("w_full", *key))
                return bank_of(key)

            def norm(l, which, tiles):
                for t in tiles:
                    dve.wait_ge(*past("sumsq", l, which, t))
                    did(dve.tensor_scalar(stat[:, 28 + t:29 + t], stat[:, 24 + t:25 + t], 1.0 / D, EPS, ALU.mult, ALU.add),
                        "nvar", l, which, t)
                    dve.wait_ge(*past("nstd", l, which, t))
                    did(dve.reciprocal(stat[:, 28 + t:29 + t], stat[:, 28 + t:29 + t]))
                    own()
                    s = t // NX
                    buf = nh[:, (t % 2) * D:(t % 2 + 1) * D]
                    if which == "fin":
                        did(dve.scalar_tensor_tensor(buf, xres[:, t, :], stat[:, 28 + t:29 + t], rows[:, 2, :],
                                                     ALU.mult, ALU.mult), "final", t)
                        continue
                    if t == tiles[0]:
                        dve.wait_ge(*past("rows", l, which))
                    did(dve.scalar_tensor_tensor(buf, xres[:, t, :], stat[:, 28 + t:29 + t], rows[:, 2 * s, :],
                                                 ALU.mult, ALU.mult))
                    own()
                    did(dve.tensor_tensor(buf, buf, rows[:, 2 * s + 1, :], ALU.add), "h2" if which == "ffn" else "h1", l, t)
                    for c in range(2):
                        did(dve.tensor_copy(hT3[:, 4 * c:4 * c + 4, t * P:(t + 1) * P],
                                            full("ht", l, which, t, c)[:, :].rearrange("p (k n) -> p k n", k=4)),
                            "w_dve", "ht", l, which, t, c)
                mark("rows_used", l, which)

            dve.wait_ge(*past("csilu"))
            did(dve.tensor_copy(scol[:, :, :], full("scol")[:, 0:2 * KD].rearrange("p (k s) -> p k s", s=2)), "w_dve", "scol")

            def mod_out(ml, part, u):
                if u == 0:
                    dve.wait_ge(*past("mbias", ml, part))
                sl = slice(u * MW, (u + 1) * MW)
                did(dve.tensor_tensor(mrow[:, sl], full("mod", ml, part, u)[0:2, 0:MW], mrow[:, sl], ALU.add),
                    "w_dve", "mod", ml, part, u)
                if u == MU - 1:
                    own()
                    if part in (1, 4):
                        did(dve.scalar_tensor_tensor(mrow, mrow, 1.0, mgain, ALU.add, ALU.mult), "modrow", ml, part)
                    else:
                        did(dve.engine_nop(), "modrow", ml, part)

            for part in range(2):
                for u in range(MU):
                    mod_out(0, part, u)
            for t in range(NT):
                if t % 2 == 0:
                    dve.wait_ge(*past("xin", t // 2))
                mark("xready", 0, "mix", t)

            for l in range(DEPTH):
                last_layer = l == DEPTH - 1
                norm(l, "mix", range(NT))
                if l:
                    dve.wait_ge(*past("arena_free", l))
                n = streams_out(l)
                dve.wait_ge(*past("padded", l, 0))
                for ct in range(2):
                    b = full("ca", l, ct)
                    dve.wait_ge(*emptied("cg", l, ct))
                    did(dve.tensor_tensor(cp4[:, ct, 0:n, HALF:HALF + SEQ],
                                          b[:, 0:n * SEQ].rearrange("p (s n) -> p s n", s=n), ca4[:, ct, 0:n, :], ALU.mult),
                        "w_dve", "ca", l, ct)
                did(dve.tensor_copy(aT[0:2 * LR, :], full("a", l)[0:2 * LR, :]), "w_dve", "a", l)
                for f in range(2):
                    did(dve.tensor_scalar(q3[:, f, :], full("q", l, f)[:, :], DK ** -0.5, None, ALU.mult), "w_dve", "q", l, f)
                for n_g, (d, f) in enumerate(GROUPS):
                    z = cum4[:, d, f, :]
                    did(dve.tensor_scalar(z, full("z", l, d, f)[:, :], bacol[:, d, f:f + 1], None, ALU.add), "w_dve", "z", l, d, f)
                    own()
                    did(dve.tensor_scalar(zbuf(n_g)[0], z, 0.0, None, ALU.min), "zready", l, d, f)
                for t in range(NT):
                    did(dve.tensor_copy(v3[:, t, :], full("v", l, t)[:, 0:GWID]), "w_dve", "v", l, t)
                for nm, X in (("rq", q3), ("rk", k3)):
                    for f in range(2):
                        b = full(nm, l, f)
                        did(dve.tensor_tensor(stat2(f), b[:, 0:SEQ], cst("sin"), ALU.mult), "w_dve", nm, l, f)
                        dve.wait_ge(*emptied("k", l, 1))
                        did(dve.tensor_tensor(X[:, f, 0:SEQ], X[:, f, 0:SEQ], cst("cos"), ALU.mult))
                        own()
                        did(dve.tensor_tensor(X[:, f, 0:SEQ], X[:, f, 0:SEQ], stat2(f), ALU.add), "roped", l, nm, f)
                for n_g, (d, f) in enumerate(GROUPS):
                    dve.wait_ge(*past("zln", l, d, f))
                    g_, sp_ = zbuf(n_g)
                    did(dve.tensor_tensor(g_, g_, sp_, ALU.subtract))
                    own()
                    dst = cum4[:, d, f, :]
                    if d == 0:
                        did(dve.tensor_tensor_scan(dst, cst("notfirst"), g_, 0.0, ALU.mult, ALU.add))
                    else:
                        did(dve.tensor_tensor_scan(dst[:, ::-1], cst("notfirst"), g_[:, ::-1], 0.0, ALU.mult, ALU.add))
                for qt in range(2):
                    if qt == 0:
                        dve.wait_ge(*past("bias", l))
                    bv = bias4[:, qt, :, :].rearrange("p h (i n) -> p (h i) n", i=4)
                    did(dve.tensor_tensor(bv, bv, cst("window").rearrange("p (a n) -> p a n", a=1).to_broadcast([P, NH * 4, GRID_W]),
                                          ALU.add), "masked", l, qt)
                for f in range(3):
                    did(dve.tensor_copy(nk3[:, f, :], full("nk", l, f)[:, :]), "w_dve", "nk", l, f)
                did(dve.tensor_copy(ccol[:, :, :], full("cc", l)[:, 0:2 * (CK + 3)].rearrange("p (c k) -> p c k", c=2)),
                    "w_dve", "cc", l)
                own()
                did(dve.memset(states[:, :], 0.0))
                lst = na_list(l)
                taps = [(j, ct) for j in range(CK) for ct in range(2)]

                def na_max(n):
                    h, t = lst[n]
                    did(dve.tensor_reduce(stat[:, 16 + n % 2:17 + n % 2], full("s", l, h, t)[:, 0:T if t < NX else CTX],
                                          AX.X, ALU.max, negate=True), "nmax", l, h, t)

                def na_finish(n):
                    h, t = lst[n]
                    kn = T if t < NX else CTX
                    b = n % 2
                    if n >= 2:
                        dve.wait_ge(*past("w_full", "no", l, *lst[n - 2]))
                    did(dve.tensor_copy(na_pt(b)[:, 0:kn], full("pt", l, h, t)[:, 0:kn]), "w_dve", "pt", l, h, t)
                    did(dve.reciprocal(stat[:, 20 + b:21 + b], stat[:, 20 + b:21 + b]))
                    own()

                def na_out(n):
                    h, t = lst[n]
                    o_ps = full("no", l, h, t)
                    did(dve.tensor_scalar(nout3[:, t, h * DH:(h + 1) * DH], o_ps[:, 0:DH], stat[:, 20 + n % 2:21 + n % 2], None,
                                          ALU.mult), "w_dve", "no", l, h, t)

                def tap(j, ct):
                    n = streams_out(l)
                    if j == 0:
                        did(dve.tensor_scalar(ca4[:, ct, 0:n, :], cp4[:, ct, 0:n, 0:SEQ], ccol[:, ct, 0:1],
                                              ccol[:, ct, CK:CK + 1], ALU.mult, ALU.add), "tap", l, j, ct)
                    else:
                        dve.wait_ge(*past("tap", l, j - 1, ct))
                        did(dve.scalar_tensor_tensor(ca4[:, ct, 0:n, :], cp4[:, ct, 0:n, j:j + SEQ], ccol[:, ct, j:j + 1],
                                                     ca4[:, ct, 0:n, :], ALU.mult, ALU.add), "tap", l, j, ct)

                def na(steps):
                    for n in steps:
                        mine = share(taps, n, len(lst))
                        if n + 1 < len(lst):
                            na_max(n + 1)
                        for ml, (part, u) in share(mod_units(l), n, len(lst)):
                            mod_out(ml, part, u)
                        for j, ct in mine[:1]:
                            tap(j, ct)
                        na_finish(n)
                        for j, ct in mine[1:]:
                            tap(j, ct)
                        na_out(n)

                na_max(0)
                for n_g, (d, f) in enumerate(GROUPS):
                    if n_g:
                        dve.wait_ge(*past("group_done", l, *GROUPS[n_g - 1]))
                    own()
                    c = cum4[:, d, f, :]
                    refs = ((X64, 128, 63 if d == 0 else 64), (X32, 64, 31 if d == 0 else 32),
                            (Qd, 32, 15 if d == 0 else 16), (KI, 128, 127 if d == 0 else 0))
                    for X, w, r in refs:
                        cv = c.rearrange("p (n w) -> p n w", w=w)
                        did(dve.tensor_tensor(X.rearrange("p (n w) -> p n w", w=w), cv,
                                              cv[:, :, r:r + 1].to_broadcast([P, T // w, w]), ALU.subtract))
                    own()
                    did(dve.tensor_scalar(Qd, Qd, CLAMP, -CLAMP, ALU.min, ALU.max), "diffs", l, d, f)
                    na(na_steps(l, n_g, 0))
                    dve.wait_ge(*past("kexp", l, d, f))
                    did(dve.tensor_tensor(KI, KI, k3[:, f, :], ALU.mult), "kint", l, d, f)
                    dve.wait_ge(*past("factors", l, d, f))
                    qs, ks = (1, 0) if d == 0 else (0, 1)
                    for X, n, h in ((X64, 4, 64), (X32, 8, 32)):
                        X4 = X.rearrange("p (n two h) -> p n two h", two=2, h=h)
                        for side, src in ((qs, q3), (ks, k3)):
                            s4 = src[:, f, :].rearrange("p (n two h) -> p n two h", two=2, h=h)
                            did(dve.tensor_tensor(X4[:, :, side, :], X4[:, :, side, :], s4[:, :, side, :], ALU.mult))
                    did(dve.tensor_tensor(Qd, Qd, q3[:, f, :], ALU.mult))
                    did(dve.tensor_tensor(Kd, Kd, k3[:, f, :], ALU.mult))
                    did(dve.tensor_tensor(QI, QI, q3[:, f, :], ALU.mult), "scaled", l, d, f)
                    na(na_steps(l, n_g, 1))
                    order = gla_order(d)
                    kv = full("kv", l, d, f)
                    for j in range(NT - 1):
                        own()
                        t = order[j]
                        for hh in range(2):
                            key = ("w_dve", "kv", l, d, f) if (j, hh) == (NT - 2, 1) else ()
                            r = slice(hh * DKP, (hh + 1) * DKP)
                            a0, a1 = (2 * j + hh) * DV, (2 * j + 2 + hh) * DV
                            did(dve.scalar_tensor_tensor(states[r, a1:a1 + DV], states[r, a0:a0 + DV],
                                                         stat[r, t:t + 1], kv[r, t * DV:(t + 1) * DV], ALU.mult, ALU.add), *key)
                    for hh in range(2):
                        m = cst(f"causal{d}").rearrange("p (a n) -> p a n", a=1).to_broadcast([P, NT, P])
                        did(dve.tensor_tensor(ST[:, hh * 512:(hh + 1) * 512].rearrange("p (t n) -> p t n", t=NT),
                                              full("sc", l, d, f, hh)[:, :].rearrange("p (t n) -> p t n", t=NT), m, ALU.mult),
                            "w_dve", "sc", l, d, f, hh)
                    na(na_steps(l, n_g, 2))
                dve.wait_ge(*past("group_done", l, *GROUPS[-1]))
                own()
                w = streams_out(l) * SEQ
                for ct in range(2):
                    c2 = ca4[:, ct, 0:streams_out(l), :].rearrange("p s n -> p (s n)")
                    did(dve.tensor_tensor(lnb(ct)[:, 0:w], c2, c2, ALU.mult), "csq", l, ct)
                mean, var = lnb(3)[:, 0:w], lnb(2)
                did(dve.memset(var, 1.0))
                did(dve.tensor_scalar(mean, full("cs", l)[:, 0:w], 1.0 / CW, None, ALU.mult), "w_dve", "cs", l)
                own()
                did(dve.tensor_tensor(lnb(4)[:, 0:w], mean, mean, ALU.mult))
                own()
                did(dve.scalar_tensor_tensor(var[:, 0:w], full("cs2", l)[:, 0:w], 1.0 / CW, lnb(4)[:, 0:w], ALU.mult, ALU.subtract),
                    "w_dve", "cs2", l)
                own()
                did(dve.tensor_scalar(var[:, 0:w], var[:, 0:w], 0.0, EPS, ALU.max, ALU.add), "cvar", l)
                for t in tiles_out(l):
                    did(dve.tensor_copy(hT3[:, 3:6, t * P:(t + 1) * P],
                                        full("nt", l, t)[:, 0:NWID].rearrange("p (k n) -> p k n", k=3)), "w_dve", "nt", l, t)
                dve.wait_ge(*past("cstd", l))
                did(dve.reciprocal(var[:, 0:w], var[:, 0:w]))
                dve.wait_ge(*past("small", l))
                for t in tiles_out(l):
                    dve.wait_ge(*past("gsq", l, t))
                    did(dve.tensor_reduce(stat[:, 8:12], ST[:, 0:GWID].rearrange("p (h e) -> p h e", h=GH), AX.X, ALU.add),
                        "gsq_used", l, t)
                    own()
                    did(dve.tensor_scalar(stat[:, 8:12], stat[:, 8:12], 1.0 / DV, EPS, ALU.mult, ALU.add), "gvar", l, t)
                    if t < 2:
                        c2 = ca4[:, t, 0:streams_out(l), :].rearrange("p s n -> p (s n)")
                        did(dve.tensor_tensor(c2, c2, mean, ALU.subtract))
                        own()
                        did(dve.tensor_tensor(c2, c2, var[:, 0:w], ALU.mult), "cnorm", l, t)
                    dve.wait_ge(*past("gstd", l, t))
                    did(dve.reciprocal(stat[:, 8:12], stat[:, 8:12]))
                    own()
                    g3 = gout3[:, t, :].rearrange("p (h e) -> p h e", h=GH)
                    did(dve.tensor_tensor(g3, psum[t][:, 0:GWID].rearrange("p (h e) -> p h e", h=GH),
                                          stat[:, 8:12].rearrange("p (h a) -> p h a", a=1).to_broadcast([P, GH, DV]), ALU.mult),
                        "o_free", l, t)
                    own()
                    did(dve.tensor_tensor(gout3[:, t, :], gout3[:, t, :], gnrow[:, :], ALU.mult))
                    own()
                    did(dve.tensor_tensor(gout3[:, t, :], gout3[:, t, :], gate3[:, t, :], ALU.mult), "gout", l, t)
                mark("mixed", l)
                dve.wait_ge(*past("rows", l, "gate_mix"))
                for t in tiles_out(l):
                    for c in range(2):
                        b = psum[t % 2 * 2 + c]
                        dve.wait_ge(*past("y_full", l, t, c))
                        sl = slice(c * 512, (c + 1) * 512)
                        did(dve.tensor_tensor(nh[:, sl], b[:, :], rows[:, t // NX, sl], ALU.mult), "y_free", l, t, c)
                        own()
                        did(dve.tensor_tensor(xres[:, t, sl], xres[:, t, sl], nh[:, sl], ALU.add),
                            *(("xmid", l, t, c)))
                mark("rows_used", l, "gate_mix")
                own()
                for t in tiles_out(l):
                    mark("xready", l, "ffn", t)
                norm(l, "ffn", tiles_out(l))
                nt = len(tiles_out(l))
                n = nt * E
                dve.wait_ge(*emptied("lg", l))
                dve.wait_ge(*past("rw", 1))

                def r3(i):
                    return rt[:, i, 0:n].rearrange("p (t e) -> p t e", t=nt)

                def rg(i):
                    return rt[:, i, 0:n].rearrange("p (a e) -> p a e", e=EG)

                def bc(x, w):
                    return x.rearrange("p (a b) -> p a b", b=1).to_broadcast([P, x.shape[1], w])

                def row(x, m):
                    return x.rearrange("p (a e) -> p a e", a=1).to_broadcast([P, m, x.shape[1]])

                def step(ins, *key):
                    did(ins, *key)
                    own()

                AFF, SEL, PR, OH1, OH2, T1, T2, GR, SLOT, RR = 0, 1, 2, 4, 5, 6, 7, 8, 9, 10
                step(dve.tensor_tensor(r3(SEL), r3(AFF), row(rbias[:, :], nt), ALU.add))
                pr = rt[:, PR:PR + 2, :].rearrange("p a b -> p (a b)")[:, 0:nt * NG * 6].rearrange("p (a e) -> p a e", e=6)
                sg = rg(SEL)
                na_ = nt * NG
                step(dve.tensor_tensor(pr[:, :, 0:3], sg[:, :, 1:4], sg[:, :, 0:1].to_broadcast([P, na_, 3]), ALU.add))
                step(dve.tensor_tensor(pr[:, :, 3:5], sg[:, :, 2:4], sg[:, :, 1:2].to_broadcast([P, na_, 2]), ALU.add))
                step(dve.tensor_tensor(pr[:, :, 5:6], sg[:, :, 3:4], sg[:, :, 2:3], ALU.add))
                gs, gm, gt = rt[:, GR, 0:na_], rt[:, GR, 16:16 + nt], rt[:, GR, 32:32 + na_]
                step(dve.tensor_reduce(gs, pr, AX.X, ALU.max))

                def first_of(x3, m, red, t3, iota, out):
                    w = x3.shape[2]
                    step(dve.tensor_reduce(red, x3, AX.X, ALU.max))
                    step(dve.tensor_tensor(t3, x3, bc(red, w), ALU.is_equal))
                    step(dve.tensor_scalar(t3, t3, -100.0, None, ALU.mult))
                    step(dve.tensor_tensor(t3, t3, row(iota, m), ALU.add))
                    step(dve.tensor_reduce(red, t3, AX.X, ALU.min))
                    step(dve.tensor_tensor(out, t3, bc(red, w), ALU.is_equal))

                g3 = gs.rearrange("p (t g) -> p t g", t=nt)
                gt3 = gt.rearrange("p (t g) -> p t g", t=nt)
                first_of(g3, nt, gm, gt3, cst("iota4"), gt3)
                step(dve.tensor_tensor(rg(T2), sg, bc(gt, EG), ALU.mult))
                step(dve.tensor_scalar(gt, gt, 1e30, -1e30, ALU.mult, ALU.add))
                step(dve.tensor_tensor(rg(T2), rg(T2), bc(gt, EG), ALU.add))
                first_of(r3(T2), nt, gm, r3(T1), cst("iota16"), r3(OH1))
                step(dve.scalar_tensor_tensor(rt[:, T2, 0:n], rt[:, OH1, 0:n], -3e30, rt[:, T2, 0:n], ALU.mult, ALU.add))
                first_of(r3(T2), nt, gm, r3(T1), cst("iota16"), r3(OH2))
                step(dve.tensor_tensor(rt[:, RR, 0:n], rt[:, OH1, 0:n], rt[:, OH2, 0:n], ALU.add), "assigned", l)
                for kk, oh in enumerate((OH1, OH2)):
                    step(dve.tensor_tensor(rt[:, T1, 0:n], rt[:, AFF, 0:n], rt[:, oh, 0:n], ALU.mult))
                    step(dve.tensor_reduce(stat[:, 32 + kk * NT:32 + kk * NT + nt], r3(T1), AX.X, ALU.add))
                step(dve.tensor_tensor(stat[:, 40:40 + nt], stat[:, 32:32 + nt], stat[:, 32 + NT:32 + NT + nt], ALU.add))
                step(dve.reciprocal(stat[:, 40:40 + nt], stat[:, 40:40 + nt]))
                for kk in range(2):
                    ww = stat[:, 32 + kk * NT:32 + kk * NT + nt]
                    step(dve.tensor_tensor(ww, ww, stat[:, 40:40 + nt], ALU.mult))
                cnt = rt[:, 11, 0:E]
                step(dve.tensor_copy(cnt, full("count", l)[:, NT * E:NT * E + E]))
                step(dve.tensor_copy(rt[:, SLOT, 0:n], full("count", l)[:, 0:n]), "w_dve", "count", l)
                nbk, inc, tmp16 = rt[:, 11, 16:32], rt[:, 11, 32:48], rt[:, 11, 48:64]
                step(dve.tensor_scalar(nbk, cnt, 0.0, None, ALU.is_gt))
                for j in range(1, nt):
                    step(dve.tensor_scalar(tmp16, cnt, float(j * P), None, ALU.is_gt))
                    step(dve.tensor_tensor(nbk, nbk, tmp16, ALU.add))
                step(dve.tensor_tensor_scan(inc, ones[:, 0:E], nbk, 0.0, ALU.mult, ALU.add))
                step(dve.tensor_tensor(tmp16, inc, nbk, ALU.subtract))
                step(dve.tensor_scalar(tmp16, tmp16, float(P), None, ALU.mult))
                step(dve.tensor_tensor(r3(SLOT), r3(SLOT), row(tmp16, nt), ALU.add))
                for kk, oh in enumerate((OH1, OH2)):
                    step(dve.tensor_tensor(rt[:, T1, 0:n], rt[:, SLOT, 0:n], rt[:, oh, 0:n], ALU.mult))
                    step(dve.tensor_reduce(stat[:, 44 + kk * NT:44 + kk * NT + nt], r3(T1), AX.X, ALU.add))
                dv = stat[:, 44:44 + 2 * NT].rearrange("p (k t) -> p t k", k=2)[:, 0:nt, :]
                if l:
                    dve.wait_ge(*past("comb_last", l - 1))
                step(dve.tensor_copy(rti[:, 0:2 * nt].rearrange("p (t k) -> p t k", k=2), dv), "dest", l)
                tt = tmp[0:1, 0:TAB * E].rearrange("p (b e) -> p b e", b=TAB)
                tt = rt[0:1, 4:10, :].rearrange("p a b -> p (a b)")[:, 0:TAB * E].rearrange("p (b e) -> p b e", b=TAB)
                step(dve.tensor_tensor(tt, inc[0:1, :].rearrange("p (a e) -> p a e", a=1).to_broadcast([1, TAB, E]),
                                       cst("iotab")[0:1, :].rearrange("p (b a) -> p b a", a=1).to_broadcast([1, TAB, E]), ALU.is_le))
                step(dve.tensor_reduce(rt[0:1, 12, 0:TAB], tt, AX.X, ALU.add))
                step(dve.tensor_scalar(rt[0:1, 12, 0:TAB], rt[0:1, 12, 0:TAB], float(E - 1), None, ALU.min))
                step(dve.tensor_copy(rt[0:1, 12, TAB:TAB + 1], inc[0:1, E - 1:E]))
                step(dve.tensor_copy(tabi[0:1, 0:TAB + 1], rt[0:1, 12, 0:TAB + 1]), "routed", l)
                mark("table", l)
                nb = dve.value_load(tabi[0:1, TAB:TAB + 1], min_val=4, max_val=MAXB)
                s = {x: sem(f"m{l}_{x}") for x in ("gused", "sil", "xf", "xe", "mul")}

                def x_out(n):
                    dve.wait_ge(s["xf"], n)
                    for c in range(2):
                        dve.tensor_copy(xT[:, c * 512:(c + 1) * 512], psum[6 + c][:, :]).then_inc(s["xe"], 1)

                def product(n):
                    for c in range(2):
                        dve.wait_ge(s["sil"], n * 2 - (1 - c))
                        dve.tensor_tensor(hb[:, c * 512:(c + 1) * 512], hb[:, c * 512:(c + 1) * 512], psum[2 + c][:, :],
                                          ALU.mult).then_inc(s["mul"], 1)

                x_out(1)
                product(1)
                x_out(2)
                with dve.Fori(1, nb) as i:
                    product(i + 1)
                    x_out(i + 2)
                dve.wait_ge(*past("rows", l, "gate_ffn"))
                for t in tiles_out(l):
                    dve.wait_ge(*past(f"comb{t % 2}", l, t))
                    a, b2 = comb[:, t % 2, 0, :], comb[:, t % 2, 1, :]
                    did(dve.tensor_scalar(a, a, stat[:, 32 + t:33 + t], None, ALU.mult))
                    own()
                    did(dve.scalar_tensor_tensor(a, b2, stat[:, 32 + NT + t:33 + NT + t], a, ALU.mult, ALU.add))
                    own()
                    did(dve.tensor_tensor(a, a, rows[:, t // NX, :], ALU.mult))
                    own()
                    did(dve.tensor_tensor(xres[:, t, :], xres[:, t, :], a, ALU.add), "combined", l, t)
                    own()
                    if not last_layer:
                        mark("xready", l + 1, "mix", t)
                    else:
                        mark("xready", l + 1, "fin", t)
                mark("rows_used", l, "gate_ffn")
                mark("comb_last", l)
                mark("arena_free", l + 1)
            norm(DEPTH, "fin", range(NX))

        @block.tensor
        def _(pe):
            def full(mm, *key):
                mm.then_inc(*up("w_full", *key))

            def slabs(key):
                return dring[:, dslot(key), :]

            pe.wait_ge(*past("const"))
            pe.wait_ge(*past("csilu"))
            b = take(pe, "scol")
            for kk in range(KD):
                mm = pe.transpose(b[:, 2 * kk:2 * kk + 2], nh[0:2, D + kk * P:D + (kk + 1) * P], ident[0:2, 0:2])
            full(mm, "scol")
            pe.wait_ge(*emptied("scol"))

            def mod_unit(ml, part, u):
                b = take(pe, "mod", ml, part, u)
                pe.wait_ge(*landed("mod", ml, (part, u)))
                w = slabs(("mod", ml, (part, u)))
                for kk in range(KD):
                    mm = pe.matmul(b[0:2, 0:MW], scol[:, kk, :], w[:, kk * MW:(kk + 1) * MW], start=kk == 0, stop=kk == KD - 1)
                full(mm, "mod", ml, part, u)

            for part in range(2):
                for u in range(MU):
                    mod_unit(0, part, u)

            def turn_rows(l, which, tiles):
                for t in tiles:
                    pe.wait_ge(*past("h2" if which == "ffn" else "h1", l, t))
                    for c in range(2):
                        b = take(pe, "ht", l, which, t, c)
                        for kk in range(4):
                            o = (t % 2) * D + (4 * c + kk) * P
                            mm = pe.transpose(b[:, kk * P:(kk + 1) * P], nh[:, o:o + P], ident)
                        full(mm, "ht", l, which, t, c)

            def feature_major(l, nm, i, lhs, m, n=T, rows_=P):
                b = take(pe, nm, l, i) if i is not None else take(pe, nm, l)
                for kk in range(KD):
                    mm = pe.matmul(b[0:m, 0:n], lhs(kk), hT3[:, kk, 0:n], start=kk == 0, stop=kk == KD - 1)
                full(mm, *((nm, l, i) if i is not None else (nm, l)))

            def token_major(l, nm, t, w):
                b = take(pe, nm, l, t)
                for kk in range(KD):
                    mm = pe.matmul(b[:, 0:UW], hT3[:, kk, t * P:(t + 1) * P], w[:, kk * UW:(kk + 1) * UW],
                                   start=kk == 0, stop=kk == KD - 1)
                full(mm, nm, l, t)

            for l in range(DEPTH):
                turn_rows(l, "mix", range(NT))
                for t in range(NT):
                    for c in range(2):
                        pe.wait_ge(*emptied("ht", l, "mix", t, c))
                n = streams_out(l) * SEQ
                for nm, u in (("ca", "c0"), ("cg", "c1")):
                    pe.wait_ge(*landed("in", l, u))
                    w = slabs(("in", l, u))
                    for ct in range(2):
                        feature_major(l, nm, ct, lambda kk, w=w, ct=ct: w[:, kk * 256 + ct * P:kk * 256 + (ct + 1) * P], P, n)
                w = slabs(("in", l, "c1"))
                feature_major(l, "a", None, lambda kk: w[:, KD * 256 + kk * 32:KD * 256 + (kk + 1) * 32], 2 * LR)
                pe.wait_ge(*past("wqk", l))
                for nm, h0 in (("q", 0), ("k", GH)):
                    for f in range(2):
                        feature_major(l, nm, f, lambda kk, h0=h0, f=f: wqk[:, kk, h0 + 2 * f:h0 + 2 * f + 2, :], P)
                pe.wait_ge(*emptied("a", l))
                pe.wait_ge(*past("small", l))
                for d, f in GROUPS:
                    b = take(pe, "z", l, d, f)
                    full(pe.matmul(b[:, :], wap[:, d, 2 * f:2 * f + 2, :], aT[0:2 * LR, :], start=True, stop=True), "z", l, d, f)
                pe.wait_ge(*landed("in", l, "v"))
                for t in range(NT):
                    token_major(l, "v", t, slabs(("in", l, "v")))
                for nm, X in (("rq", q3), ("rk", k3)):
                    for f in range(2):
                        pe.wait_ge(*emptied(nm[1], l, f))
                        b = take(pe, nm, l, f)
                        full(pe.matmul(b[:, 0:SEQ], cst("rot"), X[:, f, 0:SEQ], start=True, stop=True), nm, l, f)
                pe.wait_ge(*landed("in", l, "gate"))
                for t in tiles_out(l):
                    token_major(l, "gate", t, slabs(("in", l, "gate")))
                for nm in ("nq", "nk"):
                    pe.wait_ge(*landed("in", l, nm))
                    w = slabs(("in", l, nm))
                    for f in range(3):
                        feature_major(l, nm, f, lambda kk, w=w, f=f: w[:, kk * UW + f * P:kk * UW + (f + 1) * P], P)
                pe.wait_ge(*landed("in", l, "nv"))
                for t in range(NT):
                    token_major(l, "nv", t, slabs(("in", l, "nv")))
                b = take(pe, "cc", l)
                for ct in range(2):
                    mm = pe.transpose(b[:, ct * (CK + 3):(ct + 1) * (CK + 3)], crow[:, ct * P:(ct + 1) * P], ident[0:CK + 3, 0:CK + 3])
                full(mm, "cc", l)
                lst = na_list(l)
                pe.wait_ge(*past("masked", l, 1))
                pe.wait_ge(*emptied("nq", l, 2))
                pe.wait_ge(*emptied("nk", l, 2))

                def scores(n):
                    h, t = lst[n]
                    r = slice((h % 2) * DH, (h % 2 + 1) * DH)
                    b = take(pe, "s", l, h, t)
                    lat = t < NX
                    k0 = 0 if lat else SEQ
                    if lat:
                        pe.matmul(b[:, 0:SEQ], ident, bias4[:, t, h, :], start=True, stop=False, skip_group_check=True)
                    mm = pe.matmul(b[:, 0:T - k0], nq3[r, h // 2, t * P:(t + 1) * P], nk3[r, h // 2, k0:T],
                                   start=not lat, stop=True, skip_group_check=True)
                    full(mm, "s", l, h, t)

                def na(steps):
                    for n in steps:
                        h, t = lst[n]
                        if n + 1 < len(lst):
                            scores(n + 1)
                        for ml, (part, u) in share(mod_units(l), n, len(lst)):
                            mod_unit(ml, part, u)
                        js = range(4) if t < NX else range(2)
                        t0 = 0 if t < NX else NX
                        b = take(pe, "pt", l, h, t)
                        pe.wait_ge(*emptied("s", l, h, t))
                        for j in js:
                            mm = pe.transpose(b[:, j * P:(j + 1) * P], na_sc(n % 2)[:, j * P:(j + 1) * P], ident)
                        full(mm, "pt", l, h, t)
                        b = take(pe, "no", l, h, t)
                        pe.wait_ge(*emptied("pt", l, h, t))
                        for j in js:
                            mm = pe.matmul(b[:, 0:DH], na_pt(n % 2)[:, j * P:(j + 1) * P], nv3[:, t0 + j, h * DH:(h + 1) * DH],
                                           start=j == 0, stop=j == len(js) - 1)
                        full(mm, "no", l, h, t)

                scores(0)
                pe.wait_ge(*emptied("nv", l, NT - 1))
                for n_g, (d, f) in enumerate(GROUPS):
                    na(na_steps(l, n_g, 0))
                    order = gla_order(d)
                    pe.wait_ge(*past("kint", l, d, f))
                    b = take(pe, "kt", l, d, f)
                    for t in range(NT):
                        mm = pe.transpose(b[:, t * P:(t + 1) * P], KI[:, t * P:(t + 1) * P], ident)
                    full(mm, "kt", l, d, f)
                    na(na_steps(l, n_g, 1))
                    b = take(pe, "kv", l, d, f)
                    pe.wait_ge(*emptied("kt", l, d, f))
                    for t in range(NT):
                        for hh in range(2):
                            h = 2 * f + hh
                            mm = pe.matmul(b[hh * DKP:(hh + 1) * DKP, t * DV:(t + 1) * DV],
                                           kit[:, t * P + hh * DKP:t * P + (hh + 1) * DKP], v3[:, t, h * DV:(h + 1) * DV],
                                           start=True, stop=True)
                    full(mm, "kv", l, d, f)
                    pe.wait_ge(*past("scaled", l, d, f))
                    qs, ks = (1, 0) if d == 0 else (0, 1)
                    for hh in range(2):
                        r = slice(hh * DKP, (hh + 1) * DKP)
                        b = take(pe, "sc", l, d, f, hh)
                        pe.matmul(b[:, :], zeros[:, 0:P], zeros[:, :], start=True, stop=True, skip_group_check=True)
                        for t in tiles_out(l):
                            def block_of(s0, t0, w, kx, qx):
                                return pe.matmul(b[s0:s0 + w, t * P + t0:t * P + t0 + w], kx[r, t * P + s0:t * P + s0 + w],
                                                 qx[r, t * P + t0:t * P + t0 + w], start=False, stop=True, skip_group_check=True)
                            block_of(64 * ks, 64 * qs, 64, X64, X64)
                            for i in range(2):
                                block_of(64 * i + 32 * ks, 64 * i + 32 * qs, 32, X32, X32)
                            for i in range(4):
                                mm = block_of(32 * i, 32 * i, 32, Kd, Qd)
                        full(mm, "sc", l, d, f, hh)
                    behind = na_steps(l, n_g, 2)
                    na(behind[:len(behind) // 3])
                    pe.wait_ge(*emptied("kv", l, d, f))
                    for hh in range(2):
                        pe.wait_ge(*emptied("sc", l, d, f, hh))
                        h = 2 * f + hh
                        for t in tiles_out(l):
                            o = psum[t][:, h * DV:(h + 1) * DV]
                            pe.matmul(o, ST[:, hh * 512 + t * P:hh * 512 + (t + 1) * P], v3[:, t, h * DV:(h + 1) * DV],
                                      start=(d, f, hh) == (0, 0, 0), stop=False, skip_group_check=True)
                    for t in tiles_out(l):
                        j = order.index(t)
                        mm = pe.matmul(psum[t][:, 2 * f * DV:(2 * f + 2) * DV], QI[:, t * P:(t + 1) * P],
                                       states[:, 2 * j * DV:(2 * j + 2) * DV], start=False, stop=d == 1,
                                       skip_group_check=True)
                    mm.then_inc(*up("group_done", l, d, f))
                    na(behind[len(behind) // 3:])
                w = streams_out(l) * SEQ
                for nm in ("cs", "cs2"):
                    b = take(pe, nm, l)
                    pe.wait_ge(*past("csq", l, 1))
                    for ct in range(2):
                        src = ca4[:, ct, 0:streams_out(l), :].rearrange("p s n -> p (s n)") if nm == "cs" else lnb(ct)[:, 0:w]
                        mm = pe.matmul(b[:, 0:w], ones[:, :], src, start=ct == 0, stop=ct == 1)
                    full(mm, nm, l)
                for nm, X in (("nt", nout3), ("gt", gout3)):
                    for t in tiles_out(l):
                        b = take(pe, nm, l, t)
                        pe.wait_ge(*(past("gout", l, t) if nm == "gt" else emptied("no", l, NH - 1, t)))
                        for kk in range(3):
                            mm = pe.transpose(b[:, kk * P:(kk + 1) * P], X[:, t, kk * P:(kk + 1) * P], ident)
                        full(mm, nm, l, t)
                pe.wait_ge(*past("cact", l, 1))
                for t in tiles_out(l):
                    pe.wait_ge(*emptied("gt", l, t))
                    pe.wait_ge(*emptied("nt", l, t))
                    pe.wait_ge(*past("o_free", l, t))
                for u in range(3):
                    pe.wait_ge(*landed("out", l, u))
                for t in tiles_out(l):
                    for c in range(2):
                        if t >= 2:
                            pe.wait_ge(*past("y_free", l, t - 2, c))
                        b = psum[t % 2 * 2 + c]
                        for kk in range(KD):
                            mm = pe.matmul(b[:, :], hT3[:, kk, t * P:(t + 1) * P],
                                           slabs(("out", l, kk // 3))[:, (kk % 3) * D + c * 512:(kk % 3) * D + (c + 1) * 512],
                                           start=kk == 0, stop=kk == KD - 1)
                        mm.then_inc(*up("y_full", l, t, c))
                turn_rows(l, "ffn", tiles_out(l))
                b = take(pe, "lg", l)
                pe.wait_ge(*past("rw", 1))
                for t in tiles_out(l):
                    for c in range(2):
                        pe.wait_ge(*emptied("ht", l, "ffn", t, c))
                    for kk in range(KD):
                        mm = pe.matmul(b[:, t * E:(t + 1) * E], hT3[:, kk, t * P:(t + 1) * P], rw[:, kk, :],
                                       start=kk == 0, stop=kk == KD - 1)
                full(mm, "lg", l)
                b = take(pe, "count", l)
                pe.wait_ge(*past("assigned", l))
                n_t = len(tiles_out(l))
                for t in range(n_t):
                    for t2 in range(t + 1):
                        pe.matmul(b[:, t * E:(t + 1) * E], cst("before") if t2 == t else ones[:, :], rt[:, 10, t2 * E:(t2 + 1) * E],
                                  start=t2 == 0, stop=t2 == t)
                for t in range(n_t):
                    mm = pe.matmul(b[:, NT * E:(NT + 1) * E], ones[:, :], rt[:, 10, t * E:(t + 1) * E], start=t == 0, stop=t == n_t - 1)
                full(mm, "count", l)
                pe.wait_ge(*past("routed", l))
                nb = pe.value_load(tabi[0:1, TAB:TAB + 1], min_val=4, max_val=MAXB)
                land = [sem(f"m{l}_land{j}") for j in range(12)]
                s = {x: sem(f"m{l}_{x}") for x in ("gused", "dused", "xg", "xf", "xe", "hf", "he", "mul", "ye")}

                def turn_x(n):
                    pe.wait_ge(s["xg"], n * 16)
                    for kk in range(KD):
                        mm = pe.transpose(psum[6 + kk // 4][:, kk % 4 * P:(kk % 4 + 1) * P], xe[:, kk * P:(kk + 1) * P], ident)
                    mm.then_inc(s["xf"], 1)

                def turn_h(n):
                    pe.wait_ge(s["mul"], n * 2)
                    for kk in range(KD):
                        mm = pe.transpose(psum[6 + kk // 4][:, kk % 4 * P:(kk % 4 + 1) * P], hb[:, kk * P:(kk + 1) * P], ident)
                    mm.then_inc(s["hf"], 1)

                def gate_up(pos, count):
                    for m in range(8):
                        u = pos[m]
                        pe.wait_ge(land[u], count[m])
                        for j in range(2):
                            kk = m // 2 * 2 + j
                            for c in range(2):
                                mm = pe.matmul(psum[(m % 2) * 2 + c][:, :], xT[:, kk * P:(kk + 1) * P],
                                               mring[:, u, j * D + c * 512:j * D + (c + 1) * 512],
                                               start=kk == 0, stop=kk == KD - 1)
                        mm.then_inc(s["gused"], 1)

                def down(pos, count):
                    for m in range(4):
                        u = pos[m]
                        pe.wait_ge(land[u], count)
                        for j in range(2):
                            kk = 2 * m + j
                            for c in range(2):
                                mm = pe.matmul(psum[4 + c][:, :], hbT[:, kk * P:(kk + 1) * P],
                                               mring[:, u, j * D + c * 512:j * D + (c + 1) * 512],
                                               start=kk == 0, stop=kk == KD - 1)
                        mm.then_inc(s["dused"], 1)

                turn_x(1)
                pe.wait_ge(s["xe"], 2)
                pe.wait_ge(sem(f"m{l}_first"), 1)
                gate_up(range(8), [16] * 8)
                turn_x(2)
                pe.wait_ge(s["xe"], 4)
                turn_h(1)
                with pe.Fori(1, nb) as i:
                    pe.wait_ge(s["xe"], i * 2 + 2)
                    pe.wait_ge(s["mul"], i * 2)
                    gate_up([(8 + m) % 12 for m in range(8)], [i * 16] * 4 + [i * 16 + 16] * 4)
                    pe.wait_ge(s["he"], i * 2)
                    turn_x(i + 2)
                    pe.wait_ge(s["ye"], i * 2)
                    down(range(4, 8), i * 16 + 16)
                    pe.wait_ge(s["xe"], i * 2 + 4)
                    turn_h(i + 1)
                pe.wait_ge(s["he"], nb * 2)
                pe.wait_ge(s["ye"], nb * 2)
                down(range(8, 12), nb * 16)
                pe.wait_ge(s["ye"], nb * 2 + 2)

        led.known_now = led.now
        led.now[("order",)] = {k: v for k, v in led.order.items() if k[0] != "d"}
        led.now[("dorder",)] = {k[1:]: v for k, v in led.order.items() if k[0] == "d"}
        return led.now


_INS = ['x', 'c', 'ctx', 'c_ctx', 'w_mod', 'b_mod', 'g_mix', 'g_ffn', 'w_in', 'gla_wa_f', 'gla_ba_f', 'gla_wa_b',
        'gla_ba_b', 'gla_g_norm', 'na_rpb', 'conv_w', 'conv_b', 'conv_ln_g', 'conv_ln_b', 'w_out', 'router_w',
        'router_bias', 'w_gate', 'w_up', 'w_down', 'g_final']


def kernel(**inputs):
    import numpy as _np
    import concourse.bacc as _bacc
    from concourse.bass_utils import run_bass_kernel_spmd as _run

    arrays = {f"in_{n}": _np.ascontiguousarray(inputs[n]) for n in _INS}
    arrays["in_const"] = CONST

    def program(known):
        nc = _bacc.Bacc("TRN2", target_bir_lowering=False, num_devices=1)
        io = {n[3:]: nc.dram_tensor(n, a.shape, mybir.dt.from_np(a.dtype), kind="ExternalInput").ap() for n, a in arrays.items()}
        io["out"] = nc.dram_tensor("out_0", (1, SEQ, D), F32, kind="ExternalOutput").ap()
        return nc, build(nc, io, known)

    _, known = program({})
    nc, _ = program(known)
    r = _run(nc, [arrays], core_ids=[0])
    return r.results[0]["out_0"]
```

```python
from contextlib import ExitStack

import numpy as np

import concourse.bass as bass
import concourse.mybir as mybir
from concourse.alu_op_type import AluOpType as ALU

F32 = mybir.dt.float32
BF16 = mybir.dt.bfloat16
F32R = mybir.dt.float32r
I32 = mybir.dt.int32
ACT = mybir.ActivationFunctionType
AX = mybir.AxisListType

P = 128
D = 1024
KD = D // P
DEPTH = 2
SEQ = 256
CTX = 256
T = SEQ + CTX
NT = T // P
NX = SEQ // P
EPS = 1e-6
GRID_W = 64
GH, DK, DV = 4, 48, 96
DKP = 64
GQK, GWID = GH * DK, GH * DV
LR = 16
TAU = 16.0
NH, DH = 6, 64
NWID = NH * DH
NKH, NKW = 8, 16
CW, CK = 256, 31
COLS = 2848
UW = 384
E, FF = 16, 1024
NG, EG = 4, 4
SLOTS = T * 2
MAXB = SLOTS // P + E - 1
TAB = MAXB + 1
MOD = 6 * D
MW = 256
MU = D // MW
CLAMP = 80.0 * TAU
HALF = CK // 2
PADW = SEQ + 2 * HALF

C_QK, C_V, C_GATE, C_A = 0, 2 * GQK, 2 * GQK + GWID, 2 * GQK + 2 * GWID
C_NQ = C_A + 2 * LR
C_NK, C_NV = C_NQ + NWID, C_NQ + 2 * NWID
C_CONV = C_NQ + 3 * NWID


def constants():
    p = np.arange(P)
    parts = {}
    parts["ident"] = np.eye(P)
    rot = np.zeros((P, P))
    for i in range(0, P, 2):
        rot[i + 1, i] = -1.0
        rot[i, i + 1] = 1.0
    parts["rot"] = rot
    parts["before"] = (p[:, None] < p[None, :]).astype(float)
    parts["causal0"] = (p[:, None] <= p[None, :]).astype(float)
    parts["causal1"] = (p[:, None] >= p[None, :]).astype(float)
    half = DK // 2
    inv = 10000.0 ** (-np.arange(0, half, 2, dtype=np.float32) / half)
    t = np.arange(SEQ)
    ang = np.concatenate([(t // GRID_W)[:, None] * inv, (t % GRID_W)[:, None] * inv], -1).astype(np.float32)
    cos, sin = np.zeros((P, SEQ)), np.zeros((P, SEQ))
    for h in range(2):
        cos[h * DKP:h * DKP + DK] = np.repeat(np.cos(ang).T, 2, axis=0)
        sin[h * DKP:h * DKP + DK] = np.repeat(np.sin(ang).T, 2, axis=0)
    parts["cos"], parts["sin"] = cos, sin
    cq = p % GRID_W
    c0 = np.clip(cq - NKW // 2, 0, GRID_W - NKW)[:, None]
    ck = np.arange(GRID_W)[None, :]
    parts["window"] = np.where((ck >= c0) & (ck < c0 + NKW), 0.0, -1e30)
    parts["iota4"] = np.tile(np.arange(NG), (P, 1))
    parts["iota16"] = np.tile(np.arange(E), (P, 1))
    parts["iotab"] = np.tile(np.arange(TAB), (P, 1))
    first = np.ones((P, T))
    first[:, ::P] = 0.0
    parts["notfirst"] = first
    at, off = {}, 0
    for k, v in parts.items():
        at[k] = (off, off + v.shape[1])
        off += v.shape[1]
    return np.concatenate(list(parts.values()), 1).astype(np.float32), at


CONST, CAT = constants()
NCONST = CONST.shape[1]


class Ledger:

    def __init__(self, known):
        self.known, self.now, self.count, self.order, self.last = known, {}, {}, {}, {}

    def note(self, name, key, by):
        self.count[name] = self.count.get(name, 0) + by
        self.now[(name, key)] = self.count[name]


def build(nc, io, known):
    led = Ledger(known)
    ctx = ExitStack()
    with ctx:
        sems = {}

        def sem(name):
            if name not in sems:
                sems[name] = ctx.enter_context(nc.semaphore(name))
            return sems[name]

        def up(name, *key, by=1):
            led.note(name, key, by)
            return sem(name), by

        def dma(name, *key):
            return up(name, *key, by=16)

        def past(name, *key):
            assert not known or (name, key) in known, (name, key)
            return sem(name), known.get((name, key), 1)

        def sb(name, shape, dt=F32):
            return ctx.enter_context(nc.sbuf_tensor(name, shape, dt))

        const = sb("const", [P, NCONST])

        def cst(name):
            a, b = CAT[name]
            return const[:, a:b]

        ident = cst("ident")
        ones = sb("ones", [P, P])
        zeros = sb("zeros", [P, 512], BF16)
        zeroi = sb("zeroi", [P, TAB], I32)
        tokid = sb("tokid", [P, NT], I32)
        xres = sb("xres", [P, NT, D])
        ND = 3
        dring = sb("dring", [P, ND, KD * UW])
        dring_at = nc.sbuf_base - 4 * ND * KD * UW
        rows = sb("rows", [P, 4, D])
        scol = sb("scol", [P, KD, 2])
        rw = sb("rw", [P, KD, E])
        rbias = sb("rbias", [P, E])
        wap = sb("wap", [2 * LR, 2, GH, DKP])
        bacol = sb("bacol", [P, 2, 2])
        gnrow = sb("gnrow", [P, GWID])
        crow = sb("crow", [CK + 3, CW])
        ccol = sb("ccol", [P, 2, CK + 3])
        stat = sb("stat", [P, 64])
        rt = sb("rt", [P, 14, NT * E])
        rti = sb("rti", [P, 2 * NT], I32)
        tabi = sb("tabi", [P, 64], I32)
        idx = sb("idx", [P, 1], I32)

        NAR = 12 * 2048 + 6144
        arena = sb("arena", [P, NAR])
        arena_at = nc.sbuf_base - 4 * NAR
        ends = {}

        def carve(name, n, at):
            ends[name] = (at, at + n)
            assert at + n <= NAR, name
            return arena[:, at:at + n]

        MR = 12 * 2048
        o = 0
        tmp = carve("tmp", 4096, o); o += 4096
        q = carve("q", 2 * T, o); o += 2 * T
        k = carve("k", 2 * T, o); o += 2 * T
        v = carve("v", NT * GWID, o); o += NT * GWID
        gate = carve("gate", NT * GWID, o); o += NT * GWID
        aT = carve("aT", T, o); o += T
        cum = carve("cum", 4 * T, o); o += 4 * T
        nq = carve("nq", 3 * T, o); o += 3 * T
        nk = carve("nk", 3 * T, o); o += 3 * T
        nv = carve("nv", NT * NWID, o); o += NT * NWID
        bias = carve("bias", 2 * NH * SEQ, o); o += 2 * NH * SEQ
        cpad = carve("cpad", 2 * 2 * PADW, o); o += 2 * 2 * PADW
        ST = carve("ST", 1024, o); o += 1024
        kit = carve("kit", 512, o); o += 512
        states = carve("states", 4 * 2 * DV, o); o += 4 * 2 * DV
        cacc = carve("cacc", 1024, o); o += 1024
        assert o <= MR, o
        hT = carve("hT", KD * T, MR)
        nh = carve("nh", 2048, MR + 4096)
        gout = arena[:, 4096:4096 + NT * GWID]
        mring = arena[:, 0:MR].rearrange("p (u n) -> p u n", u=12)
        hb = carve("hb", D, MR + 4096)
        yb = carve("yb", D, MR + 5120)
        comb = arena[:, MR:MR + 4096].rearrange("p (b k n) -> p b k n", b=2, k=2)

        def split_at(name, at, n):
            return [nc.alloc_sbuf_tensor_at(f"{name}_{part}", [P, n], F32R, offset=at + 4 * n * i) for i, part in enumerate(("hi", "lo"))]

        xTh, xTl = split_at("xT", arena_at + 4 * MR, D)
        hTh, hTl = split_at("hbT", arena_at + 4 * (MR + 2048), D)
        NSP = 4
        wh, wl = split_at("slab", dring_at, NSP * D)
        xe = dring[:, ND - 1, KD * UW - D:]
        assert 2 * NSP * D <= ND * KD * UW - D

        q3 = q.rearrange("p (f t) -> p f t", f=2)
        k3 = k.rearrange("p (f t) -> p f t", f=2)
        v3 = v.rearrange("p (t n) -> p t n", t=NT)
        gate3 = gate.rearrange("p (t n) -> p t n", t=NT)
        cum4 = cum.rearrange("p (d f t) -> p d f t", d=2, f=2)
        nout3 = hT[:, 0:NT * NWID].rearrange("p (t n) -> p t n", t=NT)
        mrow, mgain = rows[0:2, 2, :], rows[0:2, 3, :]
        nq3 = nq.rearrange("p (f t) -> p f t", f=3)
        nk3 = nk.rearrange("p (f t) -> p f t", f=3)
        nv3 = nv.rearrange("p (t n) -> p t n", t=NT)
        bias4 = bias.rearrange("p (q h n) -> p q h n", q=2, h=NH)
        cp4 = cpad.rearrange("p (c s n) -> p c s n", c=2, s=2)
        ca4 = cacc.rearrange("p (c s n) -> p c s n", c=2, s=2)
        wqk = tmp.rearrange("p (k h d) -> p k h d", k=KD, h=2 * GH)
        hT3 = hT.rearrange("p (k t) -> p k t", k=KD)
        gout3 = gout.rearrange("p (t n) -> p t n", t=NT)
        X64, X32, Qd, Kd, QI, KI = (tmp[:, i * T:(i + 1) * T] for i in range(6))
        tb = sb("tb", [42, P])

        psum = [ctx.enter_context(nc.psum_tensor(f"ps{i}", [P, 512], F32)) for i in range(8)]

        modd = nc.dram_tensor("modd", [DEPTH, 2, MOD], F32)
        toep = nc.dram_tensor("toep", [DEPTH * 42 * GRID_W * P], F32)
        h2d = nc.dram_tensor("h2d", [DEPTH, T, D], F32)
        rtok = [nc.dram_tensor(f"rtok{l}", [TAB * P, 1], I32) for l in range(DEPTH)]
        yd = [nc.dram_tensor(f"yd{l}", [TAB * P, D], F32) for l in range(DEPTH)]
        h2l = [nc.dram_tensor(f"h2l{l}", [SEQ if l == DEPTH - 1 else T, D], F32) for l in range(DEPTH)]

        jobs = []

        def bank_of(key):
            return psum[4 + known.get(("order",), {}).get(key, 0) % 4]

        def take(pe, *key):
            jobs.append(key)
            led.order[key] = len(jobs) - 1
            n = len(jobs) - 1
            if n >= 4:
                pe.wait_ge(*emptied(*jobs[n - 4]))
            return psum[4 + n % 4]

        def emptied(*key):
            for name in ("w_act", "w_dve"):
                if (name, key) in known:
                    return sem(name), known[(name, key)]
            assert not known, key
            return sem("w_act"), 1

        dunits = []

        def dslot(key):
            return known.get(("dorder",), {}).get(key, 0) % ND

        def landed(*key):
            return past(f"dense{dslot(key)}", *key)

        def released(key):
            kind, l, u = key
            if kind == "mod":
                return past("w_full", "mod", l, *u)
            if kind == "out":
                return past("y_full", l, tiles_out(l)[-1], 1)
            if u == "qk":
                return past("wqk", l)
            return past("w_full", *{"v": ("v", l, NT - 1), "gate": ("gate", l, tiles_out(l)[-1]), "nq": ("nq", l, 2),
                                    "nk": ("nk", l, 2), "nv": ("nv", l, NT - 1), "c0": ("ca", l, 1), "c1": ("a", l)}[u])

        def tiles_out(l):
            return range(NX if l == DEPTH - 1 else NT)

        def streams_out(l):
            return 1 if l == DEPTH - 1 else 2

        def mod_late(l):
            return [(0, 2), (0, 3), (0, 4), (0, 5), (1, 0), (1, 1)] if l == 0 else [(l, 2), (l, 3), (l, 4), (l, 5)]

        def mod_units(l):
            return [(ml, (part, u)) for ml, part in mod_late(l) for u in range(MU)]

        def share(items, n, of):
            return items[n * len(items) // of:(n + 1) * len(items) // of]

        def na_between(l):
            return (2, 1, 3) if l < DEPTH - 1 else (1, 1, 1)

        GROUPS = [(d, f) for d in range(2) for f in range(2)]

        def na_steps(l, n_g, stage):
            before, between, behind = na_between(l)
            at = n_g * (before + between + behind) + (0, before, before + between)[stage]
            return range(at, at + na_between(l)[stage])

        def zbuf(n_g):
            return tmp[:, n_g * T:(n_g + 1) * T], tmp[:, (4 + n_g) * T:(5 + n_g) * T]

        def rows_load(eng, l, which):
            S = streams_out(l)
            plan = {"mix": [(0, 0, 1), (1, 0, 0), (2, 1, 1), (3, 1, 0)],
                    "gate_mix": [(s, s, 2) for s in range(S)],
                    "ffn": [(2 * s, s, 4) for s in range(S)] + [(2 * s + 1, s, 3) for s in range(S)],
                    "gate_ffn": [(s, s, 5) for s in range(S)]}[which]
            before = {"mix": ("rows_used", l - 1, "gate_ffn") if l else ("modd", 0, 1),
                      "gate_mix": ("rows_used", l, "mix"), "ffn": ("rows_used", l, "gate_mix"),
                      "gate_ffn": ("rows_used", l, "ffn")}[which]
            eng.wait_ge(*past(*before))
            for slot, s, part in plan:
                eng.dma_start(rows[:, slot, :], modd[l, s:s + 1, part * D:(part + 1) * D].to_broadcast([P, D])
                              ).then_inc(*dma("rows", l, which))
            if which == "gate_ffn" and l == DEPTH - 1:
                eng.dma_start(rows[:, 2, :], io["g_final"].rearrange("(a d) -> a d", a=1).to_broadcast([P, D])
                              ).then_inc(*dma("rows", l, which))

        def na_sc(b):
            return nh[:, b * 512:(b + 1) * 512]

        def na_pt(b):
            return nh[:, 1024 + b * 512:1024 + (b + 1) * 512]

        def lnb(i):
            return tmp[:, i * 512:(i + 1) * 512]

        def na_list(l):
            return [(h, t) for t in tiles_out(l) for h in range(NH)]

        def norm_act(act, did, own, l, which, tiles):
            for t in tiles:
                act.wait_ge(*past("xready", l, which, t))
                if t >= 2:
                    act.wait_ge(*past("w_full", "ht", l, which, t - 2, 1))
                    if which == "ffn":
                        act.wait_ge(*past(f"h2d{t - 2}", l, t - 2))
                did(act.activation(nh[:, (t % 2) * D:(t % 2 + 1) * D], xres[:, t, :], ACT.Square,
                                   accum_out=stat[:, 24 + t:25 + t]), "sumsq", l, which, t)
                act.wait_ge(*past("nvar", l, which, t))
                did(act.activation(stat[:, 28 + t:29 + t], stat[:, 28 + t:29 + t], ACT.Sqrt), "nstd", l, which, t)

        def stat2(f):
            return ST[:, f * SEQ:(f + 1) * SEQ]

        def gla_order(d):
            return [2, 3, 0, 1] if d == 0 else [3, 2, 1, 0]

        def gu_pos(m):
            return (8 + m) % 12

        def d_pos(m):
            return 4 + m

        def gu_slab(i, n, ahead=0):
            return 8 + n if isinstance(i, int) and i == 0 else i * 24 + (24 * ahead + n)

        def down_slab(i, n, tail=False):
            return i * 24 + (n if tail else n + 16)

        def gate_ups(i, a, b, ahead=0):
            for n in range(a, b):
                yield gu_slab(i, n, ahead), n, gu_pos(n // 2), n % 2, i * 16 + (16 * ahead + 16)

        def downs(i, a, b, tail=False):
            for n in range(a, b):
                yield down_slab(i, n, tail), n, d_pos(n // 2), n % 2, i * 16

        def split_of(n):
            at = slice(n % NSP * D, (n % NSP + 1) * D)
            return wh[:, at], wl[:, at]

        block = ctx.enter_context(nc.Block())

        @block.sync
        def _(sp):
            def dense_load(key, pieces):
                n = len(dunits)
                dunits.append(key)
                led.order[("d",) + key] = n
                if n >= ND:
                    sp.wait_ge(*released(dunits[n - ND]))
                for i, (dst, src) in enumerate(pieces(dring[:, n % ND, :])):
                    sp.dma_start(dst, src).then_inc(*dma(f"dense{n % ND}", *key))

            def wide(src):
                w = src.shape[1]
                return lambda slot: [(slot[:, 0:KD * w].rearrange("p (k n) -> p k n", k=KD),
                                      src.rearrange("(k p) n -> p k n", p=P))]

            sp.dma_start(const[:, :], io["const"]).then_inc(*dma("const"))
            for s, src in enumerate((io["c"], io["c_ctx"].rearrange("(a d) -> a d", a=1))):
                sp.dma_start(nh[s:s + 1, 0:D], src).then_inc(*dma("crows", s))
            for s, src in enumerate((io["x"], io["ctx"])):
                sp.dma_start(xres[:, 2 * s:2 * s + 2, :], src.rearrange("b (t p) d -> p (b t) d", p=P)).then_inc(*dma("xin", s))
            sp.dma_start(rw[:, :, :], io["router_w"].rearrange("(k p) e -> p k e", p=P)).then_inc(*dma("rw", 0))
            sp.dma_start(rbias[:, :], io["router_bias"].rearrange("(a e) -> a e", a=1).to_broadcast([P, E])).then_inc(*dma("rw", 1))
            def mod_load(l, pu):
                part, u = pu
                c0 = part * D + u * MW
                dense_load(("mod", l, pu), wide(io["w_mod"][l, :, c0:c0 + MW]))

            for part in range(2):
                for u in range(MU):
                    mod_load(0, (part, u))
            for l in range(DEPTH):
                w = io["w_in"][l]
                cols = {"qk": C_QK, "v": C_V, "gate": C_GATE, "nq": C_NQ, "nk": C_NK, "nv": C_NV}
                dense_load(("in", l, "c0"), wide(w[:, C_CONV:C_CONV + 256]))

                def last_unit(slot, w=w):
                    return [(slot[:, 0:KD * 256].rearrange("p (k n) -> p k n", k=KD),
                             w[:, C_CONV + 256:C_CONV + 512].rearrange("(k p) n -> p k n", p=P)),
                            (slot[:, KD * 256:KD * 288].rearrange("p (k n) -> p k n", k=KD),
                             w[:, C_A:C_A + 2 * LR].rearrange("(k p) n -> p k n", p=P))]
                dense_load(("in", l, "c1"), last_unit)
                for nm in ("qk", "v", "gate", "nq", "nk", "nv"):
                    dense_load(("in", l, nm), wide(w[:, cols[nm]:cols[nm] + UW]))
                for ml, pu in mod_units(l):
                    mod_load(ml, pu)
                for u, (a, b) in enumerate(((0, 3), (3, 6), (6, 8))):
                    dense_load(("out", l, u), lambda slot, a=a, b=b, l=l: [
                        (slot[:, 0:(b - a) * D].rearrange("p (k n) -> p k n", n=D),
                         io["w_out"][l, a * P:b * P, :].rearrange("(k p) n -> p k n", p=P))])
                sp.wait_ge(*past("mixed", l))
                sp.wait_ge(*past("cact", l, 1))
                sp.wait_ge(*past("w_full", "gt", l, tiles_out(l)[-1]))
                gsem = [sem(f"m{l}_land{j}") for j in range(12)]
                split = sem(f"m{l}_lo")

                def gu_unit(m, e):
                    src = io["w_gate"] if m % 2 == 0 else io["w_up"]
                    kk = m // 2
                    return (mring[:, gu_pos(m), :].rearrange("p (k n) -> p k n", k=2),
                            src[l, bass.ds(e, 1), kk * 256:(kk + 1) * 256, :].rearrange("a (k p) n -> p (a k) n", p=P))

                def d_unit(m, e):
                    return (mring[:, d_pos(m), :].rearrange("p (k n) -> p k n", k=2),
                            io["w_down"][l, bass.ds(e, 1), m * 256:(m + 1) * 256, :].rearrange("a (k p) n -> p (a k) n", p=P))

                for m in range(8):
                    sp.dma_start(*gu_unit(m, 0)).then_inc(gsem[gu_pos(m)], 16)
                sp.wait_ge(*past("table", l))
                nb = sp.value_load(tabi[0:1, TAB:TAB + 1], min_val=4, max_val=MAXB)
                last_block = sp.value_load(tabi[0:1, 2 * TAB + 1:2 * TAB + 2], min_val=3, max_val=MAXB - 1)
                e0 = sp.value_load(tabi[0:1, 0:1], min_val=0, max_val=E - 1)
                redo = sem(f"m{l}_redo")
                with sp.If(e0 > 0):
                    for m in range(8):
                        sp.wait_ge(gsem[gu_pos(m)], 16)
                    for m in range(8):
                        sp.dma_start(*gu_unit(m, e0)).then_inc(redo, 16)
                    sp.wait_ge(redo, 8 * 16)
                sp.sem_inc(sem(f"m{l}_first"), 1)

                def load_gu(i, seen):
                    e = sp.value_load(tabi[0:1, bass.ds(i, 1)], min_val=0, max_val=E - 1)
                    new = sp.value_load(tabi[0:1, bass.ds(i + TAB + 1, 1)], min_val=0, max_val=1)
                    with sp.If(new > 0):
                        for m in range(8):
                            sp.wait_ge(split, seen + (2 * m + 2))
                            sp.dma_start(*gu_unit(m, e)).then_inc(gsem[gu_pos(m)], 16)
                    with sp.If(new < 1):
                        for m in range(8):
                            sp.wait_ge(split, seen + (2 * m + 2))
                            sp.sem_inc(gsem[gu_pos(m)], 16)

                def load_down(i, seen):
                    e = sp.value_load(tabi[0:1, bass.ds(i, 1)], min_val=0, max_val=E - 1)
                    new = sp.value_load(tabi[0:1, bass.ds(i + TAB + 1, 1)], min_val=0, max_val=1)
                    with sp.If(new > 0):
                        for m in range(4):
                            sp.wait_ge(split, seen + (2 * m + 2))
                            sp.dma_start(*d_unit(m, e)).then_inc(gsem[d_pos(m)], 16)
                    with sp.If(new < 1):
                        for m in range(4):
                            sp.wait_ge(split, seen + (2 * m + 2))
                            sp.sem_inc(gsem[d_pos(m)], 16)

                load_gu(1, gu_slab(0, 0))
                for m in range(4):
                    sp.dma_start(*d_unit(m, e0)).then_inc(gsem[d_pos(m)], 16)
                with sp.Fori(2, nb) as i:
                    load_gu(i, gu_slab(i - 1, 0))
                    load_down(i - 1, down_slab(i - 1, 0))
                load_down(nb - 1, down_slab(last_block, 0))
                if l < DEPTH - 1:
                    sp.wait_ge(sem(f"m{l}_used"), nb * 24 + (8 + NSP))
                    sp.sem_inc(sem("sp_pace"), 1)
                    sp.wait_ge(sem(f"m{l}_xf"), nb + 1)
                    sp.sem_inc(sem("sp_pace"), 1)

        @block.gpsimd
        def _(pool):
            pool.memset(ones[:, :], 1.0).then_inc(*up("fill", "ones"))
            def carry_wait():
                pool.sem_inc(sem("pool_pace"), 1)

            pool.memset(zeros[:, :], 0.0).then_inc(*up("fill", "zeros"))
            pool.memset(zeroi[:, :], 0).then_inc(*up("fill", "zeroi"))
            pool.memset(wap[:, :, :, :], 0.0).then_inc(*up("fill", "wap"))
            pool.memset(bacol[:, :, :], 0.0).then_inc(*up("fill", "bacol"))
            pool.memset(tb[:, :], 0.0).then_inc(*up("fill", "tb"))
            pool.iota(tokid[:, :], [[P, NT]], base=0, channel_multiplier=1).then_inc(*up("fill", "tokid"))
            pool.wait_ge(*past("fill", "zeroi"))
            for l in range(DEPTH):
                pool.dma_start(rtok[l][:, :].rearrange("(p n) a -> p (n a)", p=P), zeroi[:, :]).then_inc(*dma(f"rtok{l}", 0))

            def mod_part(l, part):
                for s_ in range(2):
                    pool.dma_start(mrow[s_:s_ + 1, :], io["b_mod"][l:l + 1, part * D:(part + 1) * D]).then_inc(*dma("mbias", l, part))
                    if part in (1, 4):
                        pool.dma_start(mgain[s_:s_ + 1, :], io["g_mix" if part == 1 else "g_ffn"][l:l + 1, :]
                                       ).then_inc(*dma("mbias", l, part))
                pool.wait_ge(*past("modrow", l, part))
                pool.dma_start(modd[l, :, part * D:(part + 1) * D], mrow).then_inc(*dma("modd", l, part))
                pool.wait_ge(*past("modd", l, part))

            def small(l):
                if l:
                    pool.wait_ge(*past("gout", l - 1, tiles_out(l - 1)[-1]))
                    pool.wait_ge(*emptied("cc", l - 1))
                else:
                    for nm in ("wap", "bacol", "tb"):
                        pool.wait_ge(*past("fill", nm))
                for d, nm in enumerate(("gla_wa_f", "gla_wa_b")):
                    pool.dma_start(wap[d * LR:(d + 1) * LR, d, :, 0:DK],
                                   io[nm][l].rearrange("r (h d) -> r h d", h=GH)).then_inc(*dma("small", l))
                for d, nm in enumerate(("gla_ba_f", "gla_ba_b")):
                    for hh in range(2):
                        for f in range(2):
                            h = 2 * f + hh
                            pool.dma_start(bacol[hh * DKP:hh * DKP + DK, d, f:f + 1],
                                           io[nm][l, h * DK:(h + 1) * DK].rearrange("(d a) -> d a", a=1)
                                           ).then_inc(*dma("small", l))
                pool.dma_start(gnrow[:, :], io["gla_g_norm"][l:l + 1, :].to_broadcast([P, GWID])).then_inc(*dma("small", l))
                pool.dma_start(crow[0:CK, :], io["conv_w"][l]).then_inc(*dma("small", l))
                for j, nm in enumerate(("conv_b", "conv_ln_g", "conv_ln_b")):
                    pool.dma_start(crow[CK + j:CK + j + 1, :], io[nm][l:l + 1, :]).then_inc(*dma("small", l))
                if l:
                    pool.wait_ge(*past("toep", l - 1))
                for h in range(NH):
                    pool.dma_start(tb[7 * h:7 * h + 7, 48:79], io["na_rpb"][l, h, 4:11, :]).then_inc(*dma("tb", l))
                pool.wait_ge(*past("tb", l))
                pool.dma_start(bass.AP(toep, l * 42 * GRID_W * P, [[GRID_W * P, 42], [P, GRID_W], [1, P]]),
                               tb[:, :].rearrange("p (a n) -> p a n", a=1).to_broadcast([42, GRID_W, P])
                               ).then_inc(*dma("toep", l))

            for part in range(2):
                mod_part(0, part)
            rows_load(pool, 0, "mix")
            small(0)
            for l in range(DEPTH):
                if l:
                    pool.wait_ge(*past("arena_free", l))
                pool.memset(cpad, 0.0).then_inc(*up("padded", l, 0))
                pool.memset(wqk[:, :, :, DK:DKP], 0.0).then_inc(*up("padded", l, 1))
                pool.wait_ge(*past("toep", l))
                for qt in range(2):
                    for rl in range(2):
                        r = 2 * qt + rl
                        for h in range(NH):
                            off = (l * 42 + h * 7 + 3 - r) * GRID_W * P + GRID_W - 1
                            pool.dma_start(
                                bias4[64 * rl:64 * rl + 64, qt, h, :].rearrange("p (i n) -> p i n", i=4),
                                bass.AP(toep, off, [[P - 1, GRID_W], [GRID_W * P, 4], [1, GRID_W]])
                            ).then_inc(*dma("bias", l))
                least = (SLOTS if l < DEPTH - 1 else 2 * SEQ) // P
                if l == 0:
                    pool.wait_ge(*past("fill", "zeros"))
                n = (TAB - least) * D // 256
                pool.dma_start(yd[l][least * P:, :].rearrange("(p a) d -> p (a d)", p=P).rearrange("p (a n) -> p a n", a=n),
                               zeros[:, :].bitcast(F32).rearrange("p (a n) -> p a n", a=1).to_broadcast([P, n, 256])
                               ).then_inc(*dma("ydfill", l))
                pool.wait_ge(*past("rows_used", l, "mix"))
                for ml, part in mod_late(l):
                    mod_part(ml, part)
                rows_load(pool, l, "gate_mix")
                rows_load(pool, l, "ffn")
                for t in tiles_out(l):
                    pool.wait_ge(*past("h2", l, t))
                    pool.dma_start(h2l[l][t * P:(t + 1) * P, :], nh[:, (t % 2) * D:(t % 2 + 1) * D]).then_inc(*dma(f"h2d{t}", l, t))
                pool.wait_ge(*past(f"rtok{l}", 0))
                pool.wait_ge(*past("dest", l))
                for t in tiles_out(l):
                    for kk in range(2):
                        pool.indirect_dma_start(
                            out=rtok[l][:, :], out_offset=bass.IndirectOffsetOnAxis(ap=rti[:, 2 * t + kk:2 * t + kk + 1], axis=0),
                            in_=tokid[:, t:t + 1], in_offset=None).then_inc(*dma(f"rtok{l}", 1))
                pool.wait_ge(*past(f"rtok{l}", 1))
                for t in tiles_out(l):
                    pool.wait_ge(*past(f"h2d{t}", l, t))
                pool.wait_ge(*past("routed", l))
                nb = pool.value_load(tabi[0:1, TAB:TAB + 1], min_val=4, max_val=MAXB)
                s_idx, s_xg, s_xf = sem(f"m{l}_idx"), sem(f"m{l}_xg"), sem(f"m{l}_xf")

                def gather(idx_src, n_idx):
                    pool.dma_start(idx[:, :], idx_src).then_inc(s_idx, 16)
                    pool.wait_ge(s_idx, n_idx)
                    carry_wait()
                    pool.indirect_dma_start(out=xe[:, :], out_offset=None, in_=h2l[l][:, :],
                                            in_offset=bass.IndirectOffsetOnAxis(ap=idx[:, 0:1], axis=0)).then_inc(s_xg, 16)

                gather(rtok[l][0:P, :], 16)
                with pool.Fori(1, nb + 1) as i:
                    pool.wait_ge(s_xf, i)
                    carry_wait()
                    gather(rtok[l][bass.ds(i * P, P), :], (i + 1) * 16)
                rows_load(pool, l, "gate_ffn")
                if l < DEPTH - 1:
                    small(l + 1)
                pool.wait_ge(sem(f"m{l}_yd"), nb * 16 + 16)
                pool.wait_ge(s_xf, nb + 1)
                pool.wait_ge(sem(f"m{l}_xe"), nb * 2 + 2)
                pool.wait_ge(sem(f"m{l}_used"), nb * 24 + (8 + NSP))
                carry_wait()
                for t in tiles_out(l):
                    if t >= 2:
                        pool.wait_ge(*past("combined", l, t - 2))
                    for kk in range(2):
                        pool.indirect_dma_start(
                            out=comb[:, t % 2, kk, :], out_offset=None, in_=yd[l][:, :],
                            in_offset=bass.IndirectOffsetOnAxis(ap=rti[:, 2 * t + kk:2 * t + kk + 1], axis=0)
                        ).then_inc(*dma(f"comb{t % 2}", l, t))
                if l < DEPTH - 1:
                    rows_load(pool, l + 1, "mix")

        @block.scalar
        def _(act):
            last = []

            def did(ins, *key):
                ins.then_inc(*up(*(key or ("act_chain",))))
                last[:] = [(sem(key[0] if key else "act_chain"), led.count[key[0] if key else "act_chain"])]

            def own():
                act.wait_ge(*last[0])

            def full(*key):
                act.wait_ge(*past("w_full", *key))
                return bank_of(key)

            act.wait_ge(*past("crows", 1))
            did(act.activation(nh[0:2, D:2 * D], nh[0:2, 0:D], ACT.Silu), "csilu")
            act.wait_ge(*emptied("scol"))
            for l in range(DEPTH):
                norm_act(act, did, own, l, "mix", range(NT))
                act.wait_ge(*landed("in", l, "qk"))
                act.wait_ge(*past("padded", l, 1))
                did(act.copy(wqk[:, :, :, 0:DK], dring[:, dslot(("in", l, "qk")), :].rearrange("p (k h d) -> p k h d", k=KD, h=2 * GH)),
                    "wqk", l)
                for ct in range(2):
                    n = streams_out(l)
                    did(act.activation(ca4[:, ct, 0:n, :],
                                       full("cg", l, ct)[:, 0:n * SEQ].rearrange("p (s n) -> p s n", s=n), ACT.Sigmoid),
                        "w_act", "cg", l, ct)
                for f in range(2):
                    did(act.copy(k3[:, f, :], full("k", l, f)[:, :]), "w_act", "k", l, f)
                for n_g, (d, f) in enumerate(GROUPS):
                    act.wait_ge(*past("zready", l, d, f))
                    did(act.activation(zbuf(n_g)[1], cum4[:, d, f, :], ACT.Abs))
                    own()
                    did(act.activation(zbuf(n_g)[1], zbuf(n_g)[1], ACT.Exp, scale=-1.0))
                own()
                for n_g, (d, f) in enumerate(GROUPS):
                    did(act.activation(zbuf(n_g)[1], zbuf(n_g)[1], ACT.Ln, bias=1.0), "zln", l, d, f)
                for t in tiles_out(l):
                    did(act.activation(gate3[:, t, :], full("gate", l, t)[:, 0:GWID], ACT.Silu), "w_act", "gate", l, t)
                for f in range(3):
                    did(act.mul(nq3[:, f, :], full("nq", l, f)[:, :], DH ** -0.5), "w_act", "nq", l, f)
                for t in range(NT):
                    did(act.copy(nv3[:, t, :], full("nv", l, t)[:, 0:NWID]), "w_act", "nv", l, t)
                lst = na_list(l)

                def na_exp(n):
                    h, t = lst[n]
                    kn = T if t < NX else CTX
                    b = n % 2
                    act.wait_ge(*past("nmax", l, h, t))
                    if n >= 2:
                        act.wait_ge(*past("w_full", "pt", l, *lst[n - 2]))
                    did(act.activation(na_sc(b)[:, 0:kn], full("s", l, h, t)[:, 0:kn], ACT.Exp,
                                       bias=stat[:, 16 + b:17 + b], accum_out=stat[:, 20 + b:21 + b]),
                        "w_act", "s", l, h, t)

                def na(steps):
                    for n in steps:
                        if n + 1 < len(lst):
                            na_exp(n + 1)

                na_exp(0)
                for n_g, (d, f) in enumerate(GROUPS):
                    act.wait_ge(*past("diffs", l, d, f))
                    qs, ks = (1, 0) if d == 0 else (0, 1)
                    did(act.activation(KI, KI, ACT.Exp, scale=-1.0 / TAU), "kexp", l, d, f)
                    for X, n, h in ((X64, 4, 64), (X32, 8, 32)):
                        X4 = X.rearrange("p (n two h) -> p n two h", two=2, h=h)
                        did(act.activation(X4[:, :, qs, :], X4[:, :, qs, :], ACT.Exp, scale=1.0 / TAU))
                        did(act.activation(X4[:, :, ks, :], X4[:, :, ks, :], ACT.Exp, scale=-1.0 / TAU))
                    did(act.activation(Kd, Qd, ACT.Exp, scale=-1.0 / TAU))
                    own()
                    did(act.activation(Qd, Qd, ACT.Exp, scale=1.0 / TAU))
                    did(act.activation(QI, cum4[:, d, f, :], ACT.Exp, scale=1.0 / TAU))
                    endc = cum4[:, d, f, :].rearrange("p (t n) -> p t n", t=NT)[:, :, P - 1 if d == 0 else 0]
                    did(act.activation(stat[:, 0:NT], endc, ACT.Exp, scale=1.0 / TAU), "factors", l, d, f)
                    na(na_steps(l, n_g, 0))
                    did(act.copy(kit.rearrange("p (t n) -> p t n", t=NT),
                                 full("kt", l, d, f)[:, :].rearrange("p (t n) -> p t n", t=NT)), "w_act", "kt", l, d, f)
                    na(na_steps(l, n_g, 1))
                    na(na_steps(l, n_g, 2))
                act.wait_ge(*past("cvar", l))
                did(act.activation(lnb(2), lnb(2), ACT.Sqrt), "cstd", l)
                for t in tiles_out(l):
                    act.wait_ge(*past("group_done", l, 1, 1))
                    if t:
                        act.wait_ge(*past("gsq_used", l, t - 1))
                    did(act.activation(ST[:, 0:GWID], psum[t][:, 0:GWID], ACT.Square), "gsq", l, t)
                    act.wait_ge(*past("gvar", l, t))
                    did(act.activation(stat[:, 8:12], stat[:, 8:12], ACT.Sqrt), "gstd", l, t)
                n = streams_out(l)
                for ct in range(2):
                    act.wait_ge(*past("cnorm", l, ct))
                    did(act.activation(hT3[:, 6 + ct, 0:n * SEQ], ca4[:, ct, 0:n, :].rearrange("p s n -> p (s n)"),
                                       ACT.Silu, scale=ccol[:, ct, CK + 1:CK + 2], bias=ccol[:, ct, CK + 2:CK + 3]), "cact", l, ct)
                for t in tiles_out(l):
                    did(act.copy(hT3[:, 0:3, t * P:(t + 1) * P],
                                 full("gt", l, t)[:, 0:GWID].rearrange("p (k n) -> p k n", k=3)), "w_act", "gt", l, t)
                norm_act(act, did, own, l, "ffn", tiles_out(l))
                n = len(tiles_out(l)) * E
                did(act.activation(rt[:, 0, 0:n], full("lg", l)[:, 0:n], ACT.Sigmoid), "w_act", "lg", l)
                act.wait_ge(*past("routed", l))
                nb = act.value_load(tabi[0:1, TAB:TAB + 1], min_val=4, max_val=MAXB)
                last_block = act.value_load(tabi[0:1, 2 * TAB + 1:2 * TAB + 2], min_val=3, max_val=MAXB - 1)
                s = {x: sem(f"m{l}_{x}") for x in ("first", "hi", "used", "sil", "hf", "he", "yd", "ye", "mul")}
                land = [sem(f"m{l}_land{j}") for j in range(12)]
                act.sem_inc(s["yd"], 16)
                act.sem_inc(s["ye"], 2)
                act.sem_inc(s["hi"], 8)
                act.sem_inc(s["used"], 8 + NSP)
                act.wait_ge(*past("ydfill", l))
                act.wait_ge(s["first"], 1)

                def high(slabs):
                    for before, n, u, half, loads in slabs:
                        if half == 0:
                            act.wait_ge(land[u], loads)
                        act.wait_ge(s["used"], before + 1)
                        act.copy(split_of(n)[0], mring[:, u, half * D:(half + 1) * D]).then_inc(s["hi"], 1)

                def silu(i):
                    act.wait_ge(s["used"], gu_slab(i, 16 + NSP))
                    for c in range(2):
                        act.activation(hb[:, c * 512:(c + 1) * 512], psum[c][:, :], ACT.Silu).then_inc(s["sil"], 1)

                def h_out(i):
                    act.wait_ge(s["hf"], i + 1)
                    for c in range(2):
                        act.copy(hTh[:, c * 512:(c + 1) * 512], psum[6 + c][:, :]).then_inc(s["he"], 1)

                def y_out(i, done, dst):
                    act.wait_ge(s["used"], done)
                    act.wait_ge(s["yd"], i * 16)
                    for c in range(2):
                        act.copy(yb[:, c * 512:(c + 1) * 512], psum[4 + c][:, :]).then_inc(s["ye"], 1)
                    act.wait_ge(s["ye"], i * 2 + 2)
                    act.dma_start(dst, yb[:, :]).then_inc(s["yd"], 16)

                def block_of(i, ahead):
                    high(gate_ups(i, NSP, 16))
                    high(downs(i, 0, NSP))
                    silu(i)
                    high(downs(i, NSP, 8))
                    high(ahead)
                    y_out(i, down_slab(i, 8 + NSP), yd[l][bass.ds((i - 1) * P, P), :])
                    h_out(i)

                high(gate_ups(0, 0, 16))
                silu(0)
                high(gate_ups(1, 0, NSP))
                h_out(0)
                with act.Fori(1, nb - 1) as i:
                    block_of(i, gate_ups(i, 0, NSP, ahead=1))
                block_of(last_block, downs(nb, 0, NSP, tail=True))
                high(downs(nb, NSP, 8, tail=True))
                y_out(nb, down_slab(nb, 8 + NSP, tail=True), yd[l][bass.ds((nb - 1) * P, P), :])
            norm_act(act, did, own, DEPTH, "fin", range(NX))
            for t in range(NX):
                act.wait_ge(*past("final", t))
                act.dma_start(io["out"][0, t * P:(t + 1) * P, :], nh[:, t * D:(t + 1) * D]).then_inc(*dma("out", t))
            act.wait_ge(*past("out", NX - 1))

        @block.vector
        def _(dve):
            last = []

            def did(ins, *key):
                ins.then_inc(*up(*(key or ("dve_chain",))))
                last[:] = [(sem(key[0] if key else "dve_chain"), led.count[key[0] if key else "dve_chain"])]

            def own():
                dve.wait_ge(*last[0])

            def mark(*key):
                own()
                did(dve.engine_nop(), *key)

            def full(*key):
                dve.wait_ge(*past("w_full", *key))
                return bank_of(key)

            def norm(l, which, tiles):
                for t in tiles:
                    dve.wait_ge(*past("sumsq", l, which, t))
                    did(dve.tensor_scalar(stat[:, 28 + t:29 + t], stat[:, 24 + t:25 + t], 1.0 / D, EPS, ALU.mult, ALU.add),
                        "nvar", l, which, t)
                    dve.wait_ge(*past("nstd", l, which, t))
                    did(dve.reciprocal(stat[:, 28 + t:29 + t], stat[:, 28 + t:29 + t]))
                    own()
                    s = t // NX
                    buf = nh[:, (t % 2) * D:(t % 2 + 1) * D]
                    if which == "fin":
                        did(dve.scalar_tensor_tensor(buf, xres[:, t, :], stat[:, 28 + t:29 + t], rows[:, 2, :],
                                                     ALU.mult, ALU.mult), "final", t)
                        continue
                    if t == tiles[0]:
                        dve.wait_ge(*past("rows", l, which))
                    did(dve.scalar_tensor_tensor(buf, xres[:, t, :], stat[:, 28 + t:29 + t], rows[:, 2 * s, :],
                                                 ALU.mult, ALU.mult))
                    own()
                    did(dve.tensor_tensor(buf, buf, rows[:, 2 * s + 1, :], ALU.add), "h2" if which == "ffn" else "h1", l, t)
                    for c in range(2):
                        did(dve.tensor_copy(hT3[:, 4 * c:4 * c + 4, t * P:(t + 1) * P],
                                            full("ht", l, which, t, c)[:, :].rearrange("p (k n) -> p k n", k=4)),
                            "w_dve", "ht", l, which, t, c)
                mark("rows_used", l, which)

            dve.wait_ge(*past("csilu"))
            did(dve.tensor_copy(scol[:, :, :], full("scol")[:, 0:2 * KD].rearrange("p (k s) -> p k s", s=2)), "w_dve", "scol")

            def mod_out(ml, part, u):
                if u == 0:
                    dve.wait_ge(*past("mbias", ml, part))
                sl = slice(u * MW, (u + 1) * MW)
                did(dve.tensor_tensor(mrow[:, sl], full("mod", ml, part, u)[0:2, 0:MW], mrow[:, sl], ALU.add),
                    "w_dve", "mod", ml, part, u)
                if u == MU - 1:
                    own()
                    if part in (1, 4):
                        did(dve.scalar_tensor_tensor(mrow, mrow, 1.0, mgain, ALU.add, ALU.mult), "modrow", ml, part)
                    else:
                        did(dve.engine_nop(), "modrow", ml, part)

            for part in range(2):
                for u in range(MU):
                    mod_out(0, part, u)
            for t in range(NT):
                if t % 2 == 0:
                    dve.wait_ge(*past("xin", t // 2))
                mark("xready", 0, "mix", t)

            for l in range(DEPTH):
                last_layer = l == DEPTH - 1
                norm(l, "mix", range(NT))
                if l:
                    dve.wait_ge(*past("arena_free", l))
                n = streams_out(l)
                dve.wait_ge(*past("padded", l, 0))
                for ct in range(2):
                    b = full("ca", l, ct)
                    dve.wait_ge(*emptied("cg", l, ct))
                    did(dve.tensor_tensor(cp4[:, ct, 0:n, HALF:HALF + SEQ],
                                          b[:, 0:n * SEQ].rearrange("p (s n) -> p s n", s=n), ca4[:, ct, 0:n, :], ALU.mult),
                        "w_dve", "ca", l, ct)
                did(dve.tensor_copy(aT[0:2 * LR, :], full("a", l)[0:2 * LR, :]), "w_dve", "a", l)
                for f in range(2):
                    did(dve.tensor_scalar(q3[:, f, :], full("q", l, f)[:, :], DK ** -0.5, None, ALU.mult), "w_dve", "q", l, f)
                for n_g, (d, f) in enumerate(GROUPS):
                    z = cum4[:, d, f, :]
                    did(dve.tensor_scalar(z, full("z", l, d, f)[:, :], bacol[:, d, f:f + 1], None, ALU.add), "w_dve", "z", l, d, f)
                    own()
                    did(dve.tensor_scalar(zbuf(n_g)[0], z, 0.0, None, ALU.min), "zready", l, d, f)
                for t in range(NT):
                    did(dve.tensor_copy(v3[:, t, :], full("v", l, t)[:, 0:GWID]), "w_dve", "v", l, t)
                for nm, X in (("rq", q3), ("rk", k3)):
                    for f in range(2):
                        b = full(nm, l, f)
                        did(dve.tensor_tensor(stat2(f), b[:, 0:SEQ], cst("sin"), ALU.mult), "w_dve", nm, l, f)
                        dve.wait_ge(*emptied("k", l, 1))
                        did(dve.tensor_tensor(X[:, f, 0:SEQ], X[:, f, 0:SEQ], cst("cos"), ALU.mult))
                        own()
                        did(dve.tensor_tensor(X[:, f, 0:SEQ], X[:, f, 0:SEQ], stat2(f), ALU.add), "roped", l, nm, f)
                for n_g, (d, f) in enumerate(GROUPS):
                    dve.wait_ge(*past("zln", l, d, f))
                    g_, sp_ = zbuf(n_g)
                    did(dve.tensor_tensor(g_, g_, sp_, ALU.subtract))
                    own()
                    dst = cum4[:, d, f, :]
                    if d == 0:
                        did(dve.tensor_tensor_scan(dst, cst("notfirst"), g_, 0.0, ALU.mult, ALU.add))
                    else:
                        did(dve.tensor_tensor_scan(dst[:, ::-1], cst("notfirst"), g_[:, ::-1], 0.0, ALU.mult, ALU.add))
                for qt in range(2):
                    if qt == 0:
                        dve.wait_ge(*past("bias", l))
                    bv = bias4[:, qt, :, :].rearrange("p h (i n) -> p (h i) n", i=4)
                    did(dve.tensor_tensor(bv, bv, cst("window").rearrange("p (a n) -> p a n", a=1).to_broadcast([P, NH * 4, GRID_W]),
                                          ALU.add), "masked", l, qt)
                for f in range(3):
                    did(dve.tensor_copy(nk3[:, f, :], full("nk", l, f)[:, :]), "w_dve", "nk", l, f)
                did(dve.tensor_copy(ccol[:, :, :], full("cc", l)[:, 0:2 * (CK + 3)].rearrange("p (c k) -> p c k", c=2)),
                    "w_dve", "cc", l)
                own()
                did(dve.memset(states[:, :], 0.0))
                lst = na_list(l)
                taps = [(j, ct) for j in range(CK) for ct in range(2)]

                def na_max(n):
                    h, t = lst[n]
                    did(dve.tensor_reduce(stat[:, 16 + n % 2:17 + n % 2], full("s", l, h, t)[:, 0:T if t < NX else CTX],
                                          AX.X, ALU.max, negate=True), "nmax", l, h, t)

                def na_finish(n):
                    h, t = lst[n]
                    kn = T if t < NX else CTX
                    b = n % 2
                    if n >= 2:
                        dve.wait_ge(*past("w_full", "no", l, *lst[n - 2]))
                    did(dve.tensor_copy(na_pt(b)[:, 0:kn], full("pt", l, h, t)[:, 0:kn]), "w_dve", "pt", l, h, t)
                    did(dve.reciprocal(stat[:, 20 + b:21 + b], stat[:, 20 + b:21 + b]))
                    own()

                def na_out(n):
                    h, t = lst[n]
                    o_ps = full("no", l, h, t)
                    did(dve.tensor_scalar(nout3[:, t, h * DH:(h + 1) * DH], o_ps[:, 0:DH], stat[:, 20 + n % 2:21 + n % 2], None,
                                          ALU.mult), "w_dve", "no", l, h, t)

                def tap(j, ct):
                    n = streams_out(l)
                    if j == 0:
                        did(dve.tensor_scalar(ca4[:, ct, 0:n, :], cp4[:, ct, 0:n, 0:SEQ], ccol[:, ct, 0:1],
                                              ccol[:, ct, CK:CK + 1], ALU.mult, ALU.add), "tap", l, j, ct)
                    else:
                        dve.wait_ge(*past("tap", l, j - 1, ct))
                        did(dve.scalar_tensor_tensor(ca4[:, ct, 0:n, :], cp4[:, ct, 0:n, j:j + SEQ], ccol[:, ct, j:j + 1],
                                                     ca4[:, ct, 0:n, :], ALU.mult, ALU.add), "tap", l, j, ct)

                def na(steps):
                    for n in steps:
                        mine = share(taps, n, len(lst))
                        if n + 1 < len(lst):
                            na_max(n + 1)
                        for ml, (part, u) in share(mod_units(l), n, len(lst)):
                            mod_out(ml, part, u)
                        for j, ct in mine[:1]:
                            tap(j, ct)
                        na_finish(n)
                        for j, ct in mine[1:]:
                            tap(j, ct)
                        na_out(n)

                na_max(0)
                for n_g, (d, f) in enumerate(GROUPS):
                    if n_g:
                        dve.wait_ge(*past("group_done", l, *GROUPS[n_g - 1]))
                    own()
                    c = cum4[:, d, f, :]
                    refs = ((X64, 128, 63 if d == 0 else 64), (X32, 64, 31 if d == 0 else 32),
                            (Qd, 32, 15 if d == 0 else 16), (KI, 128, 127 if d == 0 else 0))
                    for X, w, r in refs:
                        cv = c.rearrange("p (n w) -> p n w", w=w)
                        did(dve.tensor_tensor(X.rearrange("p (n w) -> p n w", w=w), cv,
                                              cv[:, :, r:r + 1].to_broadcast([P, T // w, w]), ALU.subtract))
                    own()
                    did(dve.tensor_scalar(Qd, Qd, CLAMP, -CLAMP, ALU.min, ALU.max), "diffs", l, d, f)
                    na(na_steps(l, n_g, 0))
                    dve.wait_ge(*past("kexp", l, d, f))
                    did(dve.tensor_tensor(KI, KI, k3[:, f, :], ALU.mult), "kint", l, d, f)
                    dve.wait_ge(*past("factors", l, d, f))
                    qs, ks = (1, 0) if d == 0 else (0, 1)
                    for X, n, h in ((X64, 4, 64), (X32, 8, 32)):
                        X4 = X.rearrange("p (n two h) -> p n two h", two=2, h=h)
                        for side, src in ((qs, q3), (ks, k3)):
                            s4 = src[:, f, :].rearrange("p (n two h) -> p n two h", two=2, h=h)
                            did(dve.tensor_tensor(X4[:, :, side, :], X4[:, :, side, :], s4[:, :, side, :], ALU.mult))
                    did(dve.tensor_tensor(Qd, Qd, q3[:, f, :], ALU.mult))
                    did(dve.tensor_tensor(Kd, Kd, k3[:, f, :], ALU.mult))
                    did(dve.tensor_tensor(QI, QI, q3[:, f, :], ALU.mult), "scaled", l, d, f)
                    na(na_steps(l, n_g, 1))
                    order = gla_order(d)
                    kv = full("kv", l, d, f)
                    for j in range(NT - 1):
                        own()
                        t = order[j]
                        for hh in range(2):
                            key = ("w_dve", "kv", l, d, f) if (j, hh) == (NT - 2, 1) else ()
                            r = slice(hh * DKP, (hh + 1) * DKP)
                            a0, a1 = (2 * j + hh) * DV, (2 * j + 2 + hh) * DV
                            did(dve.scalar_tensor_tensor(states[r, a1:a1 + DV], states[r, a0:a0 + DV],
                                                         stat[r, t:t + 1], kv[r, t * DV:(t + 1) * DV], ALU.mult, ALU.add), *key)
                    for hh in range(2):
                        m = cst(f"causal{d}").rearrange("p (a n) -> p a n", a=1).to_broadcast([P, NT, P])
                        did(dve.tensor_tensor(ST[:, hh * 512:(hh + 1) * 512].rearrange("p (t n) -> p t n", t=NT),
                                              full("sc", l, d, f, hh)[:, :].rearrange("p (t n) -> p t n", t=NT), m, ALU.mult),
                            "w_dve", "sc", l, d, f, hh)
                    na(na_steps(l, n_g, 2))
                dve.wait_ge(*past("group_done", l, *GROUPS[-1]))
                own()
                w = streams_out(l) * SEQ
                for ct in range(2):
                    c2 = ca4[:, ct, 0:streams_out(l), :].rearrange("p s n -> p (s n)")
                    did(dve.tensor_tensor(lnb(ct)[:, 0:w], c2, c2, ALU.mult), "csq", l, ct)
                mean, var = lnb(3)[:, 0:w], lnb(2)
                did(dve.memset(var, 1.0))
                did(dve.tensor_scalar(mean, full("cs", l)[:, 0:w], 1.0 / CW, None, ALU.mult), "w_dve", "cs", l)
                own()
                did(dve.tensor_tensor(lnb(4)[:, 0:w], mean, mean, ALU.mult))
                own()
                did(dve.scalar_tensor_tensor(var[:, 0:w], full("cs2", l)[:, 0:w], 1.0 / CW, lnb(4)[:, 0:w], ALU.mult, ALU.subtract),
                    "w_dve", "cs2", l)
                own()
                did(dve.tensor_scalar(var[:, 0:w], var[:, 0:w], 0.0, EPS, ALU.max, ALU.add), "cvar", l)
                for t in tiles_out(l):
                    did(dve.tensor_copy(hT3[:, 3:6, t * P:(t + 1) * P],
                                        full("nt", l, t)[:, 0:NWID].rearrange("p (k n) -> p k n", k=3)), "w_dve", "nt", l, t)
                dve.wait_ge(*past("cstd", l))
                did(dve.reciprocal(var[:, 0:w], var[:, 0:w]))
                dve.wait_ge(*past("small", l))
                for t in tiles_out(l):
                    dve.wait_ge(*past("gsq", l, t))
                    did(dve.tensor_reduce(stat[:, 8:12], ST[:, 0:GWID].rearrange("p (h e) -> p h e", h=GH), AX.X, ALU.add),
                        "gsq_used", l, t)
                    own()
                    did(dve.tensor_scalar(stat[:, 8:12], stat[:, 8:12], 1.0 / DV, EPS, ALU.mult, ALU.add), "gvar", l, t)
                    if t < 2:
                        c2 = ca4[:, t, 0:streams_out(l), :].rearrange("p s n -> p (s n)")
                        did(dve.tensor_tensor(c2, c2, mean, ALU.subtract))
                        own()
                        did(dve.tensor_tensor(c2, c2, var[:, 0:w], ALU.mult), "cnorm", l, t)
                    dve.wait_ge(*past("gstd", l, t))
                    did(dve.reciprocal(stat[:, 8:12], stat[:, 8:12]))
                    own()
                    g3 = gout3[:, t, :].rearrange("p (h e) -> p h e", h=GH)
                    did(dve.tensor_tensor(g3, psum[t][:, 0:GWID].rearrange("p (h e) -> p h e", h=GH),
                                          stat[:, 8:12].rearrange("p (h a) -> p h a", a=1).to_broadcast([P, GH, DV]), ALU.mult),
                        "o_free", l, t)
                    own()
                    did(dve.tensor_tensor(gout3[:, t, :], gout3[:, t, :], gnrow[:, :], ALU.mult))
                    own()
                    did(dve.tensor_tensor(gout3[:, t, :], gout3[:, t, :], gate3[:, t, :], ALU.mult), "gout", l, t)
                mark("mixed", l)
                dve.wait_ge(*past("rows", l, "gate_mix"))
                for t in tiles_out(l):
                    for c in range(2):
                        b = psum[t % 2 * 2 + c]
                        dve.wait_ge(*past("y_full", l, t, c))
                        sl = slice(c * 512, (c + 1) * 512)
                        did(dve.tensor_tensor(nh[:, sl], b[:, :], rows[:, t // NX, sl], ALU.mult), "y_free", l, t, c)
                        own()
                        did(dve.tensor_tensor(xres[:, t, sl], xres[:, t, sl], nh[:, sl], ALU.add),
                            *(("xmid", l, t, c)))
                mark("rows_used", l, "gate_mix")
                own()
                for t in tiles_out(l):
                    mark("xready", l, "ffn", t)
                norm(l, "ffn", tiles_out(l))
                nt = len(tiles_out(l))
                n = nt * E
                dve.wait_ge(*emptied("lg", l))
                dve.wait_ge(*past("rw", 1))

                def r3(i):
                    return rt[:, i, 0:n].rearrange("p (t e) -> p t e", t=nt)

                def rg(i):
                    return rt[:, i, 0:n].rearrange("p (a e) -> p a e", e=EG)

                def bc(x, w):
                    return x.rearrange("p (a b) -> p a b", b=1).to_broadcast([P, x.shape[1], w])

                def row(x, m):
                    return x.rearrange("p (a e) -> p a e", a=1).to_broadcast([P, m, x.shape[1]])

                def step(ins, *key):
                    did(ins, *key)
                    own()

                AFF, SEL, PR, OH1, OH2, T1, T2, GR, SLOT, RR = 0, 1, 2, 4, 5, 6, 7, 8, 9, 10
                step(dve.tensor_tensor(r3(SEL), r3(AFF), row(rbias[:, :], nt), ALU.add))
                pr = rt[:, PR:PR + 2, :].rearrange("p a b -> p (a b)")[:, 0:nt * NG * 6].rearrange("p (a e) -> p a e", e=6)
                sg = rg(SEL)
                na_ = nt * NG
                step(dve.tensor_tensor(pr[:, :, 0:3], sg[:, :, 1:4], sg[:, :, 0:1].to_broadcast([P, na_, 3]), ALU.add))
                step(dve.tensor_tensor(pr[:, :, 3:5], sg[:, :, 2:4], sg[:, :, 1:2].to_broadcast([P, na_, 2]), ALU.add))
                step(dve.tensor_tensor(pr[:, :, 5:6], sg[:, :, 3:4], sg[:, :, 2:3], ALU.add))
                gs, gm, gt = rt[:, GR, 0:na_], rt[:, GR, 16:16 + nt], rt[:, GR, 32:32 + na_]
                step(dve.tensor_reduce(gs, pr, AX.X, ALU.max))

                def first_of(x3, m, red, t3, iota, out):
                    w = x3.shape[2]
                    step(dve.tensor_reduce(red, x3, AX.X, ALU.max))
                    step(dve.tensor_tensor(t3, x3, bc(red, w), ALU.is_equal))
                    step(dve.tensor_scalar(t3, t3, -100.0, None, ALU.mult))
                    step(dve.tensor_tensor(t3, t3, row(iota, m), ALU.add))
                    step(dve.tensor_reduce(red, t3, AX.X, ALU.min))
                    step(dve.tensor_tensor(out, t3, bc(red, w), ALU.is_equal))

                g3 = gs.rearrange("p (t g) -> p t g", t=nt)
                gt3 = gt.rearrange("p (t g) -> p t g", t=nt)
                first_of(g3, nt, gm, gt3, cst("iota4"), gt3)
                step(dve.tensor_tensor(rg(T2), sg, bc(gt, EG), ALU.mult))
                step(dve.tensor_scalar(gt, gt, 1e30, -1e30, ALU.mult, ALU.add))
                step(dve.tensor_tensor(rg(T2), rg(T2), bc(gt, EG), ALU.add))
                first_of(r3(T2), nt, gm, r3(T1), cst("iota16"), r3(OH1))
                step(dve.scalar_tensor_tensor(rt[:, T2, 0:n], rt[:, OH1, 0:n], -3e30, rt[:, T2, 0:n], ALU.mult, ALU.add))
                first_of(r3(T2), nt, gm, r3(T1), cst("iota16"), r3(OH2))
                step(dve.tensor_tensor(rt[:, RR, 0:n], rt[:, OH1, 0:n], rt[:, OH2, 0:n], ALU.add), "assigned", l)
                for kk, oh in enumerate((OH1, OH2)):
                    step(dve.tensor_tensor(rt[:, T1, 0:n], rt[:, AFF, 0:n], rt[:, oh, 0:n], ALU.mult))
                    step(dve.tensor_reduce(stat[:, 32 + kk * NT:32 + kk * NT + nt], r3(T1), AX.X, ALU.add))
                step(dve.tensor_tensor(stat[:, 40:40 + nt], stat[:, 32:32 + nt], stat[:, 32 + NT:32 + NT + nt], ALU.add))
                step(dve.reciprocal(stat[:, 40:40 + nt], stat[:, 40:40 + nt]))
                for kk in range(2):
                    ww = stat[:, 32 + kk * NT:32 + kk * NT + nt]
                    step(dve.tensor_tensor(ww, ww, stat[:, 40:40 + nt], ALU.mult))
                cnt = rt[:, 11, 0:E]
                step(dve.tensor_copy(cnt, full("count", l)[:, NT * E:NT * E + E]))
                step(dve.tensor_copy(rt[:, SLOT, 0:n], full("count", l)[:, 0:n]), "w_dve", "count", l)
                nbk, inc, tmp16 = rt[:, 11, 16:32], rt[:, 11, 32:48], rt[:, 11, 48:64]
                step(dve.tensor_scalar(nbk, cnt, 0.0, None, ALU.is_gt))
                for j in range(1, nt):
                    step(dve.tensor_scalar(tmp16, cnt, float(j * P), None, ALU.is_gt))
                    step(dve.tensor_tensor(nbk, nbk, tmp16, ALU.add))
                step(dve.tensor_tensor_scan(inc, ones[:, 0:E], nbk, 0.0, ALU.mult, ALU.add))
                step(dve.tensor_tensor(tmp16, inc, nbk, ALU.subtract))
                step(dve.tensor_scalar(tmp16, tmp16, float(P), None, ALU.mult))
                step(dve.tensor_tensor(r3(SLOT), r3(SLOT), row(tmp16, nt), ALU.add))
                for kk, oh in enumerate((OH1, OH2)):
                    step(dve.tensor_tensor(rt[:, T1, 0:n], rt[:, SLOT, 0:n], rt[:, oh, 0:n], ALU.mult))
                    step(dve.tensor_reduce(stat[:, 44 + kk * NT:44 + kk * NT + nt], r3(T1), AX.X, ALU.add))
                dv = stat[:, 44:44 + 2 * NT].rearrange("p (k t) -> p t k", k=2)[:, 0:nt, :]
                if l:
                    dve.wait_ge(*past("comb_last", l - 1))
                step(dve.tensor_copy(rti[:, 0:2 * nt].rearrange("p (t k) -> p t k", k=2), dv), "dest", l)
                tt = tmp[0:1, 0:TAB * E].rearrange("p (b e) -> p b e", b=TAB)
                tt = rt[0:1, 4:10, :].rearrange("p a b -> p (a b)")[:, 0:TAB * E].rearrange("p (b e) -> p b e", b=TAB)
                step(dve.tensor_tensor(tt, inc[0:1, :].rearrange("p (a e) -> p a e", a=1).to_broadcast([1, TAB, E]),
                                       cst("iotab")[0:1, :].rearrange("p (b a) -> p b a", a=1).to_broadcast([1, TAB, E]), ALU.is_le))
                step(dve.tensor_reduce(rt[0:1, 12, 0:TAB], tt, AX.X, ALU.add))
                step(dve.tensor_scalar(rt[0:1, 12, 0:TAB], rt[0:1, 12, 0:TAB], float(E - 1), None, ALU.min))
                step(dve.tensor_copy(rt[0:1, 12, TAB:TAB + 1], inc[0:1, E - 1:E]))
                step(dve.memset(rt[0:1, 12, TAB + 1:TAB + 2], 1.0))
                step(dve.tensor_tensor(rt[0:1, 12, TAB + 2:2 * TAB + 1], rt[0:1, 12, 1:TAB], rt[0:1, 12, 0:TAB - 1], ALU.is_gt))
                step(dve.tensor_scalar(rt[0:1, 12, 2 * TAB + 1:2 * TAB + 2], inc[0:1, E - 1:E], -1.0, None, ALU.add))
                step(dve.tensor_copy(tabi[0:1, 0:2 * TAB + 2], rt[0:1, 12, 0:2 * TAB + 2]), "routed", l)
                mark("table", l)
                nb = dve.value_load(tabi[0:1, TAB:TAB + 1], min_val=4, max_val=MAXB)
                last_block = dve.value_load(tabi[0:1, 2 * TAB + 1:2 * TAB + 2], min_val=3, max_val=MAXB - 1)
                s = {x: sem(f"m{l}_{x}") for x in ("hi", "lo", "sil", "xf", "xh", "xe", "mul", "he", "hl")}

                dve.sem_inc(s["lo"], 8)

                def low(slabs):
                    for before, n, u, half, _ in slabs:
                        dve.wait_ge(s["hi"], before + 1)
                        hi, lo = split_of(n)
                        dve.tensor_tensor(lo, mring[:, u, half * D:(half + 1) * D], hi.bitcast(F32), ALU.subtract).then_inc(s["lo"], 1)

                def x_out(i):
                    dve.wait_ge(s["xf"], i + 1)
                    for c in range(2):
                        dve.tensor_copy(xTh[:, c * 512:(c + 1) * 512], psum[6 + c][:, :]).then_inc(s["xh"], 1)
                    for c in range(2):
                        dve.wait_ge(s["xh"], i * 2 + (c + 1))
                        dve.tensor_tensor(xTl[:, c * 512:(c + 1) * 512], psum[6 + c][:, :],
                                          xTh[:, c * 512:(c + 1) * 512].bitcast(F32), ALU.subtract).then_inc(s["xe"], 1)

                def product(i):
                    for c in range(2):
                        dve.wait_ge(s["sil"], i * 2 + (c + 1))
                        dve.tensor_tensor(hb[:, c * 512:(c + 1) * 512], hb[:, c * 512:(c + 1) * 512], psum[2 + c][:, :],
                                          ALU.mult).then_inc(s["mul"], 1)

                def h_low(i):
                    for c in range(2):
                        dve.wait_ge(s["he"], i * 2 + (c + 1))
                        dve.tensor_tensor(hTl[:, c * 512:(c + 1) * 512], psum[6 + c][:, :],
                                          hTh[:, c * 512:(c + 1) * 512].bitcast(F32), ALU.subtract).then_inc(s["hl"], 1)

                def block_of(i, ahead):
                    low(gate_ups(i, NSP, 16))
                    low(downs(i, 0, NSP))
                    x_out(i + 1)
                    product(i)
                    low(downs(i, NSP, 8))
                    low(ahead)
                    h_low(i)

                x_out(0)
                low(gate_ups(0, 0, 16))
                x_out(1)
                product(0)
                low(gate_ups(1, 0, NSP))
                h_low(0)
                with dve.Fori(1, nb - 1) as i:
                    block_of(i, gate_ups(i, 0, NSP, ahead=1))
                block_of(last_block, downs(nb, 0, NSP, tail=True))
                low(downs(nb, NSP, 8, tail=True))
                dve.wait_ge(*past("rows", l, "gate_ffn"))
                for t in tiles_out(l):
                    dve.wait_ge(*past(f"comb{t % 2}", l, t))
                    a, b2 = comb[:, t % 2, 0, :], comb[:, t % 2, 1, :]
                    did(dve.tensor_scalar(a, a, stat[:, 32 + t:33 + t], None, ALU.mult))
                    own()
                    did(dve.scalar_tensor_tensor(a, b2, stat[:, 32 + NT + t:33 + NT + t], a, ALU.mult, ALU.add))
                    own()
                    did(dve.tensor_tensor(a, a, rows[:, t // NX, :], ALU.mult))
                    own()
                    did(dve.tensor_tensor(xres[:, t, :], xres[:, t, :], a, ALU.add), "combined", l, t)
                    own()
                    if not last_layer:
                        mark("xready", l + 1, "mix", t)
                    else:
                        mark("xready", l + 1, "fin", t)
                mark("rows_used", l, "gate_ffn")
                mark("comb_last", l)
                mark("arena_free", l + 1)
            norm(DEPTH, "fin", range(NX))

        @block.tensor
        def _(pe):
            def full(mm, *key):
                mm.then_inc(*up("w_full", *key))

            def slabs(key):
                return dring[:, dslot(key), :]

            pe.wait_ge(*past("const"))
            pe.wait_ge(*past("csilu"))
            b = take(pe, "scol")
            for kk in range(KD):
                mm = pe.transpose(b[:, 2 * kk:2 * kk + 2], nh[0:2, D + kk * P:D + (kk + 1) * P], ident[0:2, 0:2])
            full(mm, "scol")
            pe.wait_ge(*emptied("scol"))

            def mod_unit(ml, part, u):
                b = take(pe, "mod", ml, part, u)
                pe.wait_ge(*landed("mod", ml, (part, u)))
                w = slabs(("mod", ml, (part, u)))
                for kk in range(KD):
                    mm = pe.matmul(b[0:2, 0:MW], scol[:, kk, :], w[:, kk * MW:(kk + 1) * MW], start=kk == 0, stop=kk == KD - 1)
                full(mm, "mod", ml, part, u)

            for part in range(2):
                for u in range(MU):
                    mod_unit(0, part, u)

            def turn_rows(l, which, tiles):
                for t in tiles:
                    pe.wait_ge(*past("h2" if which == "ffn" else "h1", l, t))
                    for c in range(2):
                        b = take(pe, "ht", l, which, t, c)
                        for kk in range(4):
                            o = (t % 2) * D + (4 * c + kk) * P
                            mm = pe.transpose(b[:, kk * P:(kk + 1) * P], nh[:, o:o + P], ident)
                        full(mm, "ht", l, which, t, c)

            def feature_major(l, nm, i, lhs, m, n=T, rows_=P):
                b = take(pe, nm, l, i) if i is not None else take(pe, nm, l)
                for kk in range(KD):
                    mm = pe.matmul(b[0:m, 0:n], lhs(kk), hT3[:, kk, 0:n], start=kk == 0, stop=kk == KD - 1)
                full(mm, *((nm, l, i) if i is not None else (nm, l)))

            def token_major(l, nm, t, w):
                b = take(pe, nm, l, t)
                for kk in range(KD):
                    mm = pe.matmul(b[:, 0:UW], hT3[:, kk, t * P:(t + 1) * P], w[:, kk * UW:(kk + 1) * UW],
                                   start=kk == 0, stop=kk == KD - 1)
                full(mm, nm, l, t)

            for l in range(DEPTH):
                turn_rows(l, "mix", range(NT))
                for t in range(NT):
                    for c in range(2):
                        pe.wait_ge(*emptied("ht", l, "mix", t, c))
                n = streams_out(l) * SEQ
                for nm, u in (("ca", "c0"), ("cg", "c1")):
                    pe.wait_ge(*landed("in", l, u))
                    w = slabs(("in", l, u))
                    for ct in range(2):
                        feature_major(l, nm, ct, lambda kk, w=w, ct=ct: w[:, kk * 256 + ct * P:kk * 256 + (ct + 1) * P], P, n)
                w = slabs(("in", l, "c1"))
                feature_major(l, "a", None, lambda kk: w[:, KD * 256 + kk * 32:KD * 256 + (kk + 1) * 32], 2 * LR)
                pe.wait_ge(*past("wqk", l))
                for nm, h0 in (("q", 0), ("k", GH)):
                    for f in range(2):
                        feature_major(l, nm, f, lambda kk, h0=h0, f=f: wqk[:, kk, h0 + 2 * f:h0 + 2 * f + 2, :], P)
                pe.wait_ge(*emptied("a", l))
                pe.wait_ge(*past("small", l))
                for d, f in GROUPS:
                    b = take(pe, "z", l, d, f)
                    full(pe.matmul(b[:, :], wap[:, d, 2 * f:2 * f + 2, :], aT[0:2 * LR, :], start=True, stop=True), "z", l, d, f)
                pe.wait_ge(*landed("in", l, "v"))
                for t in range(NT):
                    token_major(l, "v", t, slabs(("in", l, "v")))
                for nm, X in (("rq", q3), ("rk", k3)):
                    for f in range(2):
                        pe.wait_ge(*emptied(nm[1], l, f))
                        b = take(pe, nm, l, f)
                        full(pe.matmul(b[:, 0:SEQ], cst("rot"), X[:, f, 0:SEQ], start=True, stop=True), nm, l, f)
                pe.wait_ge(*landed("in", l, "gate"))
                for t in tiles_out(l):
                    token_major(l, "gate", t, slabs(("in", l, "gate")))
                for nm in ("nq", "nk"):
                    pe.wait_ge(*landed("in", l, nm))
                    w = slabs(("in", l, nm))
                    for f in range(3):
                        feature_major(l, nm, f, lambda kk, w=w, f=f: w[:, kk * UW + f * P:kk * UW + (f + 1) * P], P)
                pe.wait_ge(*landed("in", l, "nv"))
                for t in range(NT):
                    token_major(l, "nv", t, slabs(("in", l, "nv")))
                b = take(pe, "cc", l)
                for ct in range(2):
                    mm = pe.transpose(b[:, ct * (CK + 3):(ct + 1) * (CK + 3)], crow[:, ct * P:(ct + 1) * P], ident[0:CK + 3, 0:CK + 3])
                full(mm, "cc", l)
                lst = na_list(l)
                pe.wait_ge(*past("masked", l, 1))
                pe.wait_ge(*emptied("nq", l, 2))
                pe.wait_ge(*emptied("nk", l, 2))

                def scores(n):
                    h, t = lst[n]
                    r = slice((h % 2) * DH, (h % 2 + 1) * DH)
                    b = take(pe, "s", l, h, t)
                    lat = t < NX
                    k0 = 0 if lat else SEQ
                    if lat:
                        pe.matmul(b[:, 0:SEQ], ident, bias4[:, t, h, :], start=True, stop=False, skip_group_check=True)
                    mm = pe.matmul(b[:, 0:T - k0], nq3[r, h // 2, t * P:(t + 1) * P], nk3[r, h // 2, k0:T],
                                   start=not lat, stop=True, skip_group_check=True)
                    full(mm, "s", l, h, t)

                def na(steps):
                    for n in steps:
                        h, t = lst[n]
                        if n + 1 < len(lst):
                            scores(n + 1)
                        for ml, (part, u) in share(mod_units(l), n, len(lst)):
                            mod_unit(ml, part, u)
                        js = range(4) if t < NX else range(2)
                        t0 = 0 if t < NX else NX
                        b = take(pe, "pt", l, h, t)
                        pe.wait_ge(*emptied("s", l, h, t))
                        for j in js:
                            mm = pe.transpose(b[:, j * P:(j + 1) * P], na_sc(n % 2)[:, j * P:(j + 1) * P], ident)
                        full(mm, "pt", l, h, t)
                        b = take(pe, "no", l, h, t)
                        pe.wait_ge(*emptied("pt", l, h, t))
                        for j in js:
                            mm = pe.matmul(b[:, 0:DH], na_pt(n % 2)[:, j * P:(j + 1) * P], nv3[:, t0 + j, h * DH:(h + 1) * DH],
                                           start=j == 0, stop=j == len(js) - 1)
                        full(mm, "no", l, h, t)

                scores(0)
                pe.wait_ge(*emptied("nv", l, NT - 1))
                for n_g, (d, f) in enumerate(GROUPS):
                    na(na_steps(l, n_g, 0))
                    order = gla_order(d)
                    pe.wait_ge(*past("kint", l, d, f))
                    b = take(pe, "kt", l, d, f)
                    for t in range(NT):
                        mm = pe.transpose(b[:, t * P:(t + 1) * P], KI[:, t * P:(t + 1) * P], ident)
                    full(mm, "kt", l, d, f)
                    na(na_steps(l, n_g, 1))
                    b = take(pe, "kv", l, d, f)
                    pe.wait_ge(*emptied("kt", l, d, f))
                    for t in range(NT):
                        for hh in range(2):
                            h = 2 * f + hh
                            mm = pe.matmul(b[hh * DKP:(hh + 1) * DKP, t * DV:(t + 1) * DV],
                                           kit[:, t * P + hh * DKP:t * P + (hh + 1) * DKP], v3[:, t, h * DV:(h + 1) * DV],
                                           start=True, stop=True)
                    full(mm, "kv", l, d, f)
                    pe.wait_ge(*past("scaled", l, d, f))
                    qs, ks = (1, 0) if d == 0 else (0, 1)
                    for hh in range(2):
                        r = slice(hh * DKP, (hh + 1) * DKP)
                        b = take(pe, "sc", l, d, f, hh)
                        pe.matmul(b[:, :], zeros[:, 0:P], zeros[:, :], start=True, stop=True, skip_group_check=True)
                        for t in tiles_out(l):
                            def block_of(s0, t0, w, kx, qx):
                                return pe.matmul(b[s0:s0 + w, t * P + t0:t * P + t0 + w], kx[r, t * P + s0:t * P + s0 + w],
                                                 qx[r, t * P + t0:t * P + t0 + w], start=False, stop=True, skip_group_check=True)
                            block_of(64 * ks, 64 * qs, 64, X64, X64)
                            for i in range(2):
                                block_of(64 * i + 32 * ks, 64 * i + 32 * qs, 32, X32, X32)
                            for i in range(4):
                                mm = block_of(32 * i, 32 * i, 32, Kd, Qd)
                        full(mm, "sc", l, d, f, hh)
                    behind = na_steps(l, n_g, 2)
                    na(behind[:len(behind) // 3])
                    pe.wait_ge(*emptied("kv", l, d, f))
                    for hh in range(2):
                        pe.wait_ge(*emptied("sc", l, d, f, hh))
                        h = 2 * f + hh
                        for t in tiles_out(l):
                            o = psum[t][:, h * DV:(h + 1) * DV]
                            pe.matmul(o, ST[:, hh * 512 + t * P:hh * 512 + (t + 1) * P], v3[:, t, h * DV:(h + 1) * DV],
                                      start=(d, f, hh) == (0, 0, 0), stop=False, skip_group_check=True)
                    for t in tiles_out(l):
                        j = order.index(t)
                        mm = pe.matmul(psum[t][:, 2 * f * DV:(2 * f + 2) * DV], QI[:, t * P:(t + 1) * P],
                                       states[:, 2 * j * DV:(2 * j + 2) * DV], start=False, stop=d == 1,
                                       skip_group_check=True)
                    mm.then_inc(*up("group_done", l, d, f))
                    na(behind[len(behind) // 3:])
                w = streams_out(l) * SEQ
                for nm in ("cs", "cs2"):
                    b = take(pe, nm, l)
                    pe.wait_ge(*past("csq", l, 1))
                    for ct in range(2):
                        src = ca4[:, ct, 0:streams_out(l), :].rearrange("p s n -> p (s n)") if nm == "cs" else lnb(ct)[:, 0:w]
                        mm = pe.matmul(b[:, 0:w], ones[:, :], src, start=ct == 0, stop=ct == 1)
                    full(mm, nm, l)
                for nm, X in (("nt", nout3), ("gt", gout3)):
                    for t in tiles_out(l):
                        b = take(pe, nm, l, t)
                        pe.wait_ge(*(past("gout", l, t) if nm == "gt" else emptied("no", l, NH - 1, t)))
                        for kk in range(3):
                            mm = pe.transpose(b[:, kk * P:(kk + 1) * P], X[:, t, kk * P:(kk + 1) * P], ident)
                        full(mm, nm, l, t)
                pe.wait_ge(*past("cact", l, 1))
                for t in tiles_out(l):
                    pe.wait_ge(*emptied("gt", l, t))
                    pe.wait_ge(*emptied("nt", l, t))
                    pe.wait_ge(*past("o_free", l, t))
                for u in range(3):
                    pe.wait_ge(*landed("out", l, u))
                for t in tiles_out(l):
                    for c in range(2):
                        if t >= 2:
                            pe.wait_ge(*past("y_free", l, t - 2, c))
                        b = psum[t % 2 * 2 + c]
                        for kk in range(KD):
                            mm = pe.matmul(b[:, :], hT3[:, kk, t * P:(t + 1) * P],
                                           slabs(("out", l, kk // 3))[:, (kk % 3) * D + c * 512:(kk % 3) * D + (c + 1) * 512],
                                           start=kk == 0, stop=kk == KD - 1)
                        mm.then_inc(*up("y_full", l, t, c))
                turn_rows(l, "ffn", tiles_out(l))
                b = take(pe, "lg", l)
                pe.wait_ge(*past("rw", 1))
                for t in tiles_out(l):
                    for c in range(2):
                        pe.wait_ge(*emptied("ht", l, "ffn", t, c))
                    for kk in range(KD):
                        mm = pe.matmul(b[:, t * E:(t + 1) * E], hT3[:, kk, t * P:(t + 1) * P], rw[:, kk, :],
                                       start=kk == 0, stop=kk == KD - 1)
                full(mm, "lg", l)
                b = take(pe, "count", l)
                pe.wait_ge(*past("assigned", l))
                n_t = len(tiles_out(l))
                for t in range(n_t):
                    for t2 in range(t + 1):
                        pe.matmul(b[:, t * E:(t + 1) * E], cst("before") if t2 == t else ones[:, :], rt[:, 10, t2 * E:(t2 + 1) * E],
                                  start=t2 == 0, stop=t2 == t)
                for t in range(n_t):
                    mm = pe.matmul(b[:, NT * E:(NT + 1) * E], ones[:, :], rt[:, 10, t * E:(t + 1) * E], start=t == 0, stop=t == n_t - 1)
                full(mm, "count", l)
                pe.wait_ge(*past("routed", l))
                nb = pe.value_load(tabi[0:1, TAB:TAB + 1], min_val=4, max_val=MAXB)
                s = {x: sem(f"m{l}_{x}") for x in ("lo", "used", "xg", "xf", "xe", "hf", "he", "hl", "mul", "ye")}

                def turn_x(i):
                    pe.wait_ge(s["xg"], i * 16 + 16)
                    for kk in range(KD):
                        mm = pe.transpose(psum[6 + kk // 4][:, kk % 4 * P:(kk % 4 + 1) * P], xe[:, kk * P:(kk + 1) * P], ident)
                    mm.then_inc(s["xf"], 1)

                def turn_h(i):
                    pe.wait_ge(s["mul"], i * 2 + 2)
                    for kk in range(KD):
                        mm = pe.transpose(psum[6 + kk // 4][:, kk % 4 * P:(kk % 4 + 1) * P], hb[:, kk * P:(kk + 1) * P], ident)
                    mm.then_inc(s["hf"], 1)

                def slab_products(slabs, hi, lo, bank):
                    for before, n, _, _, _ in slabs:
                        pe.wait_ge(s["lo"], before + 1)
                        kk, base = bank(n)
                        f, g_ = split_of(n)
                        at = slice(kk * P, (kk + 1) * P)
                        for x, w, first, last in ((hi, f, True, False), (hi, g_, False, False), (lo, f, False, True)):
                            for c in range(2):
                                mm = pe.matmul(psum[base + c][:, :], x[:, at], w[:, c * 512:(c + 1) * 512],
                                               start=first and kk == 0, stop=last and kk == KD - 1)
                        mm.then_inc(s["used"], 1)

                def gate_up(slabs):
                    slab_products(slabs, xTh, xTl, lambda n: (n // 4 * 2 + n % 2, n // 2 % 2 * 2))

                def down(slabs):
                    slab_products(slabs, hTh, hTl, lambda n: (n, 4))

                turn_x(0)
                pe.wait_ge(s["xe"], 2)
                gate_up(gate_ups(0, 0, 16))
                turn_x(1)
                pe.wait_ge(s["xe"], 4)
                turn_h(0)
                with pe.Fori(1, nb) as i:
                    pe.wait_ge(s["mul"], i * 2)
                    gate_up(gate_ups(i, 0, 16))
                    pe.wait_ge(s["hl"], i * 2)
                    turn_x(i + 1)
                    pe.wait_ge(s["ye"], i * 2)
                    down(downs(i, 0, 8))
                    pe.wait_ge(s["xe"], i * 2 + 4)
                    turn_h(i)
                pe.wait_ge(s["hl"], nb * 2)
                pe.wait_ge(s["ye"], nb * 2)
                down(downs(nb, 0, 8, tail=True))
                pe.wait_ge(s["ye"], nb * 2 + 2)

        led.known_now = led.now
        led.now[("order",)] = {k: v for k, v in led.order.items() if k[0] != "d"}
        led.now[("dorder",)] = {k[1:]: v for k, v in led.order.items() if k[0] == "d"}
        return led.now


_INS = ['x', 'c', 'ctx', 'c_ctx', 'w_mod', 'b_mod', 'g_mix', 'g_ffn', 'w_in', 'gla_wa_f', 'gla_ba_f', 'gla_wa_b',
        'gla_ba_b', 'gla_g_norm', 'na_rpb', 'conv_w', 'conv_b', 'conv_ln_g', 'conv_ln_b', 'w_out', 'router_w',
        'router_bias', 'w_gate', 'w_up', 'w_down', 'g_final']


def kernel(**inputs):
    import numpy as _np
    import concourse.bacc as _bacc
    from concourse.bass_utils import run_bass_kernel_spmd as _run

    arrays = {f"in_{n}": _np.ascontiguousarray(inputs[n]) for n in _INS}
    arrays["in_const"] = CONST

    def program(known):
        nc = _bacc.Bacc("TRN2", target_bir_lowering=False, num_devices=1)
        io = {n[3:]: nc.dram_tensor(n, a.shape, mybir.dt.from_np(a.dtype), kind="ExternalInput").ap() for n, a in arrays.items()}
        io["out"] = nc.dram_tensor("out_0", (1, SEQ, D), F32, kind="ExternalOutput").ap()
        return nc, build(nc, io, known)

    _, known = program({})
    nc, _ = program(known)
    r = _run(nc, [arrays], core_ids=[0])
    return r.results[0]["out_0"]
```

```python
from contextlib import ExitStack

import numpy as np

import concourse.bass as bass
import concourse.mybir as mybir
from concourse.alu_op_type import AluOpType as ALU

F32 = mybir.dt.float32
BF16 = mybir.dt.bfloat16
F32R = mybir.dt.float32r
I32 = mybir.dt.int32
ACT = mybir.ActivationFunctionType
AX = mybir.AxisListType

P = 128
D = 1024
KD = D // P
DEPTH = 2
SEQ = 256
CTX = 256
T = SEQ + CTX
NT = T // P
NX = SEQ // P
EPS = 1e-6
GRID_W = 64
GH, DK, DV = 4, 48, 96
DKP = 64
GQK, GWID = GH * DK, GH * DV
LR = 16
TAU = 16.0
NH, DH = 6, 64
NWID = NH * DH
NKH, NKW = 8, 16
CW, CK = 256, 31
COLS = 2848
UW = 384
E, FF = 16, 1024
NG, EG = 4, 4
SLOTS = T * 2
MAXB = SLOTS // P + E - 1
TAB = MAXB + 1
MOD = 6 * D
MW = 256
MU = D // MW
CLAMP = 80.0 * TAU
HALF = CK // 2
PADW = SEQ + 2 * HALF

C_QK, C_V, C_GATE, C_A = 0, 2 * GQK, 2 * GQK + GWID, 2 * GQK + 2 * GWID
C_NQ = C_A + 2 * LR
C_NK, C_NV = C_NQ + NWID, C_NQ + 2 * NWID
C_CONV = C_NQ + 3 * NWID


def constants():
    p = np.arange(P)
    parts = {}
    parts["ident"] = np.eye(P)
    rot = np.zeros((P, P))
    for i in range(0, P, 2):
        rot[i + 1, i] = -1.0
        rot[i, i + 1] = 1.0
    parts["rot"] = rot
    parts["before"] = (p[:, None] < p[None, :]).astype(float)
    parts["causal0"] = (p[:, None] <= p[None, :]).astype(float)
    parts["causal1"] = (p[:, None] >= p[None, :]).astype(float)
    half = DK // 2
    inv = 10000.0 ** (-np.arange(0, half, 2, dtype=np.float32) / half)
    t = np.arange(SEQ)
    ang = np.concatenate([(t // GRID_W)[:, None] * inv, (t % GRID_W)[:, None] * inv], -1).astype(np.float32)
    cos, sin = np.zeros((P, SEQ)), np.zeros((P, SEQ))
    for h in range(2):
        cos[h * DKP:h * DKP + DK] = np.repeat(np.cos(ang).T, 2, axis=0)
        sin[h * DKP:h * DKP + DK] = np.repeat(np.sin(ang).T, 2, axis=0)
    parts["cos"], parts["sin"] = cos, sin
    cq = p % GRID_W
    c0 = np.clip(cq - NKW // 2, 0, GRID_W - NKW)[:, None]
    ck = np.arange(GRID_W)[None, :]
    parts["window"] = np.where((ck >= c0) & (ck < c0 + NKW), 0.0, -1e30)
    parts["iota4"] = np.tile(np.arange(NG), (P, 1))
    parts["iota16"] = np.tile(np.arange(E), (P, 1))
    parts["iotab"] = np.tile(np.arange(TAB), (P, 1))
    first = np.ones((P, T))
    first[:, ::P] = 0.0
    parts["notfirst"] = first
    at, off = {}, 0
    for k, v in parts.items():
        at[k] = (off, off + v.shape[1])
        off += v.shape[1]
    return np.concatenate(list(parts.values()), 1).astype(np.float32), at


CONST, CAT = constants()
NCONST = CONST.shape[1]


class Ledger:

    def __init__(self, known):
        self.known, self.now, self.count, self.order, self.last = known, {}, {}, {}, {}

    def note(self, name, key, by):
        self.count[name] = self.count.get(name, 0) + by
        self.now[(name, key)] = self.count[name]


def build(nc, io, known):
    led = Ledger(known)
    ctx = ExitStack()
    with ctx:
        sems = {}

        def sem(name):
            if name not in sems:
                sems[name] = ctx.enter_context(nc.semaphore(name))
            return sems[name]

        def up(name, *key, by=1):
            led.note(name, key, by)
            return sem(name), by

        def dma(name, *key):
            return up(name, *key, by=16)

        def past(name, *key):
            assert not known or (name, key) in known, (name, key)
            return sem(name), known.get((name, key), 1)

        def sb(name, shape, dt=F32):
            return ctx.enter_context(nc.sbuf_tensor(name, shape, dt))

        const = sb("const", [P, NCONST])

        def cst(name):
            a, b = CAT[name]
            return const[:, a:b]

        ident = cst("ident")
        ones = sb("ones", [P, P])
        zeros = sb("zeros", [P, 512], BF16)
        zeroi = sb("zeroi", [P, TAB], I32)
        tokid = sb("tokid", [P, NT], I32)
        xres = sb("xres", [P, NT, D])
        ND = 3
        dring = sb("dring", [P, ND, KD * UW])
        dring_at = nc.sbuf_base - 4 * ND * KD * UW
        rows = sb("rows", [P, 4, D])
        scol = sb("scol", [P, KD, 2])
        rw = sb("rw", [P, KD, E])
        rbias = sb("rbias", [P, E])
        wap = sb("wap", [2 * LR, 2, GH, DKP])
        bacol = sb("bacol", [P, 2, 2])
        gnrow = sb("gnrow", [P, GWID])
        crow = sb("crow", [CK + 3, CW])
        ccol = sb("ccol", [P, 2, CK + 3])
        stat = sb("stat", [P, 64])
        rt = sb("rt", [P, 14, NT * E])
        rti = sb("rti", [P, 2 * NT], I32)
        tabi = sb("tabi", [P, 64], I32)
        idx = sb("idx", [P, 1 + TAB], I32)
        junk = rt[:, 0:8, :].rearrange("p a b -> p (a b)").bitcast(BF16)

        NAR = 12 * 2048 + 6144
        arena = sb("arena", [P, NAR])
        arena_at = nc.sbuf_base - 4 * NAR
        ends = {}

        def carve(name, n, at):
            ends[name] = (at, at + n)
            assert at + n <= NAR, name
            return arena[:, at:at + n]

        MR = 12 * 2048
        o = 0
        tmp = carve("tmp", 4096, o); o += 4096
        q = carve("q", 2 * T, o); o += 2 * T
        k = carve("k", 2 * T, o); o += 2 * T
        v = carve("v", NT * GWID, o); o += NT * GWID
        gate = carve("gate", NT * GWID, o); o += NT * GWID
        aT = carve("aT", T, o); o += T
        cum = carve("cum", 4 * T, o); o += 4 * T
        nq = carve("nq", 3 * T, o); o += 3 * T
        nk = carve("nk", 3 * T, o); o += 3 * T
        nv = carve("nv", NT * NWID, o); o += NT * NWID
        bias = carve("bias", 2 * NH * SEQ, o); o += 2 * NH * SEQ
        cpad = carve("cpad", 2 * 2 * PADW, o); o += 2 * 2 * PADW
        ST = carve("ST", 1024, o); o += 1024
        kit = carve("kit", 512, o); o += 512
        states = carve("states", 4 * 2 * DV, o); o += 4 * 2 * DV
        cacc = carve("cacc", 1024, o); o += 1024
        assert o <= MR, o
        hT = carve("hT", KD * T, MR)
        nh = carve("nh", 2048, MR + 4096)
        gout = arena[:, 4096:4096 + NT * GWID]
        mring = arena[:, 0:MR].rearrange("p (u n) -> p u n", u=12)
        hb = carve("hb", D, MR + 4096)
        yb = carve("yb", D, MR + 5120)
        comb = arena[:, 0:NT * 2 * D].rearrange("p (t k n) -> p t k n", t=NT, k=2)

        def split_at(name, at, n):
            return [nc.alloc_sbuf_tensor_at(f"{name}_{part}", [P, n], F32R, offset=at + 4 * n * i) for i, part in enumerate(("hi", "lo"))]

        xTh, xTl = split_at("xT", arena_at + 4 * MR, D)
        gTh, gTl = split_at("hbT", arena_at + 4 * (MR + 2048), D)
        NSP = 4
        wh, wl = split_at("slab", dring_at, NSP * D)
        hTh = nc.alloc_sbuf_tensor_at("hT_hi", [P, KD, T], F32R, offset=arena_at + 4 * MR)
        hTl = nc.alloc_sbuf_tensor_at("hT_lo", [P, KD, T], F32R, offset=arena_at)
        sub_ring = [split_at(f"sub{i}", arena_at + 4 * at, KD * P) for i, at in enumerate((ends["nh"][0], ends["ST"][0]))]
        assert ends["states"][1] - ends["ST"][0] >= 2 * KD * P
        xe = dring[:, ND - 1, KD * UW - D:]
        assert 2 * NSP * D <= ND * KD * UW - D

        q3 = q.rearrange("p (f t) -> p f t", f=2)
        k3 = k.rearrange("p (f t) -> p f t", f=2)
        v3 = v.rearrange("p (t n) -> p t n", t=NT)
        gate3 = gate.rearrange("p (t n) -> p t n", t=NT)
        cum4 = cum.rearrange("p (d f t) -> p d f t", d=2, f=2)
        nout3 = hT[:, 0:NT * NWID].rearrange("p (t n) -> p t n", t=NT)
        nq3 = nq.rearrange("p (f t) -> p f t", f=3)
        nk3 = nk.rearrange("p (f t) -> p f t", f=3)
        nv3 = nv.rearrange("p (t n) -> p t n", t=NT)
        bias4 = bias.rearrange("p (q h n) -> p q h n", q=2, h=NH)
        cp4 = cpad.rearrange("p (c s n) -> p c s n", c=2, s=2)
        ca4 = cacc.rearrange("p (c s n) -> p c s n", c=2, s=2)
        hT3 = hT.rearrange("p (k t) -> p k t", k=KD)
        gout3 = gout.rearrange("p (t n) -> p t n", t=NT)
        X64, X32, Qd, Kd, QI, KI = (tmp[:, i * T:(i + 1) * T] for i in range(6))
        tb = sb("tb", [42, P])

        psum = [ctx.enter_context(nc.psum_tensor(f"ps{i}", [P, 512], F32)) for i in range(8)]

        modd = nc.dram_tensor("modd", [DEPTH, 2, MOD], F32)
        toep = nc.dram_tensor("toep", [DEPTH * 42 * GRID_W * P], F32)
        rtok = [nc.dram_tensor(f"rtok{l}", [TAB * P, 1], I32) for l in range(DEPTH)]
        yd = [nc.dram_tensor(f"yd{l}", [TAB * P, D], F32) for l in range(DEPTH)]
        h2l = [nc.dram_tensor(f"h2l{l}", [SEQ if l == DEPTH - 1 else T, D], F32) for l in range(DEPTH)]

        jobs = []

        def bank_of(key):
            return psum[4 + known.get(("order",), {}).get(key, 0) % 4]

        def take(pe, *key):
            jobs.append(key)
            led.order[key] = len(jobs) - 1
            n = len(jobs) - 1
            if n >= 4:
                pe.wait_ge(*emptied(*jobs[n - 4]))
            return psum[4 + n % 4]

        def emptied(*key):
            for name in ("w_act", "w_dve"):
                if (name, key) in known:
                    return sem(name), known[(name, key)]
            assert not known, key
            return sem("w_act"), 1

        dunits = []

        def dslot(key):
            return known.get(("dorder",), {}).get(key, 0) % ND

        def landed(*key):
            return past(f"dense{dslot(key)}", *key)

        def released(key):
            kind, l, u = key
            if kind == "mod":
                return past("w_full", "mod", l, *u)
            if kind == "out":
                return past("y_full", l, tiles_out(l)[-1], 1)
            return past("sub_lo", l, max(n for n, sub in enumerate(SUBS) if sub[2] == u))

        def tiles_out(l):
            return range(NX if l == DEPTH - 1 else NT)

        def streams_out(l):
            return 1 if l == DEPTH - 1 else 2

        def mod_late(l):
            return [(0, 2), (0, 3), (0, 4), (0, 5), (1, 0), (1, 1)] if l == 0 else [(l, 2), (l, 3), (l, 4), (l, 5)]

        MOD_EARLY = [(0, 1), (0, 0)]

        def mod_rows(ml, part):
            seq = next(x for x in [MOD_EARLY] + [mod_late(l) for l in range(DEPTH)] if (ml, part) in x)
            at = 2 + seq.index((ml, part)) % 2
            return rows[0:2, at, :], rows[0:2, 5 - at, :], at, 5 - at

        def mod_units(l):
            return [(ml, (part, u)) for ml, part in mod_late(l) for u in range(MU)]

        def share(items, n, of):
            return items[n * len(items) // of:(n + 1) * len(items) // of]

        def na_between(l):
            return (1, 1, 2) if l < DEPTH - 1 else (1, 0, 1)

        TAIL = 5

        def tail_steps(l):
            n = len(tiles_out(l)) * NH
            at = len(GROUPS) * sum(na_between(l))
            return [(at + j, share(range(TAIL), j, n - at)) for j in range(n - at)]

        GROUPS = [(d, f) for d in range(2) for f in range(2)]

        def na_steps(l, n_g, stage):
            before, between, behind = na_between(l)
            at = n_g * (before + between + behind) + (0, before, before + between)[stage]
            return range(at, at + na_between(l)[stage])

        def zbuf(n_g):
            flat = rows[:, :, :].rearrange("p a d -> p (a d)")
            return flat[:, n_g * T:(n_g + 1) * T], flat[:, (4 + n_g) * T:(5 + n_g) * T]

        SUBS = [("q", 0, "qk"), ("q", 1, "qk"), ("k", 0, "qk"), ("k", 1, "qk"), ("cg", 0, "c1"), ("cg", 1, "c1"),
                ("a", None, "c1"), ("ca", 0, "c0"), ("ca", 1, "c0")]
        SUBS += [(nm, i, nm) for nm in ("v", "nq", "gate", "nk", "nv") for i in range(3 if nm in ("nq", "nk") else KD // 2)]

        def sub_key(l, n):
            nm, i, _ = SUBS[n]
            return (nm, l) if i is None else (nm, l, i)

        def sub_views(l, n):
            nm, i, unit = SUBS[n]
            raw = dring[:, dslot(("in", l, unit)), :]
            hi, lo = sub_ring[n % 2]
            if unit == "qk":
                h0 = 2 * i + (GH if nm == "k" else 0)
                src = raw.rearrange("p (k h d) -> p k h d", k=KD, h=2 * GH)[:, :, h0:h0 + 2, :]
                return [x[:, :].rearrange("p (k h d) -> p k h d", k=KD, h=2)[:, :, :, 0:DK] for x in (hi, lo)] + [src]
            if nm in ("v", "gate", "nv"):
                src, w = raw.rearrange("p (k n) -> p k n", k=KD)[:, 2 * i:2 * i + 2, :], UW
                return [x[:, 0:2 * w].rearrange("p (k n) -> p k n", k=2) for x in (hi, lo)] + [src]
            if nm == "a":
                src, w = raw[:, KD * 256:KD * (256 + 2 * LR)].rearrange("p (k n) -> p k n", k=KD), 2 * LR
            else:
                full_w = 256 if unit in ("c0", "c1") else UW
                w = P
                src = raw[:, 0:KD * full_w].rearrange("p (k n) -> p k n", k=KD)[:, :, i * P:(i + 1) * P]
            return [x[:, 0:KD * w].rearrange("p (k n) -> p k n", k=KD) for x in (hi, lo)] + [src]

        def norm_slots(l, which, s):
            return (s, 2 + s) if (l, which) == (0, "mix") else (2, 3)

        def rows_load(eng, l, which, s):
            if which in ("mix", "ffn"):
                scale, shift = norm_slots(l, which, s)
                plan = [(scale, {"mix": 1, "ffn": 4}[which]), (shift, {"mix": 0, "ffn": 3}[which])]
                if s and (l or which == "ffn"):
                    before = ("rows_used", l, which, 0)
                elif which == "ffn":
                    before = ("rows_used", l, "mix", NT // NX - 1)
                else:
                    before = ("rows_used", l - 1, "ffn", streams_out(l - 1) - 1)
            else:
                plan = [(s, {"gate_mix": 2, "gate_ffn": 5}[which])]
                before = ("rows_used", l, "gate_mix") if which == "gate_ffn" else \
                    ("rows_used", l - 1, "gate_ffn") if l else ("rows_used", l, "mix", NT // NX - 1)
            eng.wait_ge(*past(*before))
            for slot, part in plan:
                eng.dma_start(rows[:, slot, :], modd[l, s:s + 1, part * D:(part + 1) * D].to_broadcast([P, D])
                              ).then_inc(*dma(f"rows_{which}{s}", l))

        def na_sc(b):
            return nh[:, b * 512:(b + 1) * 512]

        def na_pt(b):
            return nh[:, 1024 + b * 512:1024 + (b + 1) * 512]

        def lnb(i):
            return tmp[:, i * 512:(i + 1) * 512]

        def na_list(l):
            return [(h, t) for t in tiles_out(l) for h in range(NH)]

        def norm_act(act, did, own, l, which, tiles, work=lambda t: None):
            def sumsq(t):
                if t + 1 < len(tiles):
                    work(t + 1)
                act.wait_ge(*past("xready", l, which, t))
                own()
                did(act.activation(junk, xres[:, t, :], ACT.Square, accum_out=stat[:, 24 + t:25 + t]),
                    "sumsq", l, which, t)

            def deviation(s):
                act.wait_ge(*past("nvar", l, which, s))
                sl = slice(28 + 2 * s, 30 + 2 * s)
                did(act.activation(stat[:, sl], stat[:, sl], ACT.Sqrt), "nstd", l, which, s)

            def turned(t):
                if which == "mix":
                    for c in range(2):
                        act.wait_ge(*past("w_full", "ht", l, which, t, c))
                        did(act.copy(hTh[:, 4 * c:4 * c + 4, t * P:(t + 1) * P],
                                     bank_of(("ht", l, which, t, c))[:, :].rearrange("p (k n) -> p k n", k=4)), "ht_hi", l, t, c)
                    return
                act.wait_ge(*past("w_full", "ht", l, which, t, 1))
                did(act.copy(hT3[:, 4:8, t * P:(t + 1) * P],
                             bank_of(("ht", l, which, t, 1))[:, :].rearrange("p (k n) -> p k n", k=4)),
                    "w_act", "ht", l, which, t, 1)

            work(0)
            sumsq(0)
            sumsq(1)
            deviation(0)
            if len(tiles) > 2:
                sumsq(2)
                turned(0)
                sumsq(3)
                turned(1)
                deviation(1)
            if which != "fin":
                turned(tiles[-2])
                turned(tiles[-1])

        def stat2(f):
            return cacc[:, f * SEQ:(f + 1) * SEQ]

        def gla_order(d):
            return [2, 3, 0, 1] if d == 0 else [3, 2, 1, 0]

        def gu_pos(m):
            return (8 + m) % 12

        def d_pos(m):
            return 4 + m

        def gu_slab(i, n, ahead=0):
            return 8 + n if isinstance(i, int) and i == 0 else i * 24 + (24 * ahead + n)

        def down_slab(i, n, tail=False):
            return i * 24 + (n if tail else n + 16)

        def gate_ups(i, a, b, ahead=0):
            for n in range(a, b):
                yield gu_slab(i, n, ahead), n, gu_pos(n // 2), n % 2, i * 16 + (16 * ahead + 16)

        def downs(i, a, b, tail=False):
            for n in range(a, b):
                yield down_slab(i, n, tail), n, d_pos(n // 2), n % 2, i * 16

        def split_of(n):
            at = slice(n % NSP * D, (n % NSP + 1) * D)
            return wh[:, at], wl[:, at]

        block = ctx.enter_context(nc.Block())

        @block.sync
        def _(sp):
            def dense_load(key, pieces):
                n = len(dunits)
                dunits.append(key)
                led.order[("d",) + key] = n
                if n >= ND:
                    sp.wait_ge(*released(dunits[n - ND]))
                for i, (dst, src) in enumerate(pieces(dring[:, n % ND, :])):
                    sp.dma_start(dst, src).then_inc(*dma(f"dense{n % ND}", *key))

            def wide(src):
                w = src.shape[1]
                return lambda slot: [(slot[:, 0:KD * w].rearrange("p (k n) -> p k n", k=KD),
                                      src.rearrange("(k p) n -> p k n", p=P))]

            sp.dma_start(const[:, :], io["const"]).then_inc(*dma("const"))
            for s, src in enumerate((io["c"], io["c_ctx"].rearrange("(a d) -> a d", a=1))):
                sp.dma_start(nh[s:s + 1, 0:D], src).then_inc(*dma("crows", s))
            def mod_load(l, pu):
                part, u = pu
                c0 = part * D + u * MW
                dense_load(("mod", l, pu), wide(io["w_mod"][l, :, c0:c0 + MW]))

            early = [(part, u) for _, part in MOD_EARLY for u in range(MU)]
            for pu in early[:ND]:
                mod_load(0, pu)
            for s, src in enumerate((io["x"], io["ctx"])):
                sp.dma_start(xres[:, 2 * s:2 * s + 2, :], src.rearrange("b (t p) d -> p (b t) d", p=P)).then_inc(*dma("xin", s))
            sp.dma_start(rw[:, :, :], io["router_w"].rearrange("(k p) e -> p k e", p=P)).then_inc(*dma("rw", 0))
            sp.dma_start(rbias[:, :], io["router_bias"].rearrange("(a e) -> a e", a=1).to_broadcast([P, E])).then_inc(*dma("rw", 1))
            for pu in early[ND:]:
                mod_load(0, pu)
            for l in range(DEPTH):
                w = io["w_in"][l]
                cols = {"v": C_V, "gate": C_GATE, "nq": C_NQ, "nk": C_NK, "nv": C_NV}
                sp.wait_ge(*(past(f"comb{NT - 1}", l - 1) if l else past("rows_mix1", 0)))
                dense_load(("in", l, "qk"), wide(w[:, C_QK:C_QK + UW]))

                def last_unit(slot, w=w):
                    return [(slot[:, 0:KD * 256].rearrange("p (k n) -> p k n", k=KD),
                             w[:, C_CONV + 256:C_CONV + 512].rearrange("(k p) n -> p k n", p=P)),
                            (slot[:, KD * 256:KD * 288].rearrange("p (k n) -> p k n", k=KD),
                             w[:, C_A:C_A + 2 * LR].rearrange("(k p) n -> p k n", p=P))]
                dense_load(("in", l, "c1"), last_unit)
                dense_load(("in", l, "c0"), wide(w[:, C_CONV:C_CONV + 256]))
                for nm in ("v", "nq", "gate", "nk", "nv"):
                    dense_load(("in", l, nm), wide(w[:, cols[nm]:cols[nm] + UW]))
                for ml, pu in mod_units(l):
                    mod_load(ml, pu)
                for u, (a, b) in enumerate(((0, 3), (3, 6), (6, 8))):
                    dense_load(("out", l, u), lambda slot, a=a, b=b, l=l: [
                        (slot[:, 0:(b - a) * D].rearrange("p (k n) -> p k n", n=D),
                         io["w_out"][l, a * P:b * P, :].rearrange("(k p) n -> p k n", p=P))])
                sp.wait_ge(*past("mixed", l))
                sp.wait_ge(*past("cact", l, 1))
                sp.wait_ge(*past("w_full", "gt", l, tiles_out(l)[-1]))
                gsem = [sem(f"m{l}_land{j}") for j in range(12)]
                split = sem(f"m{l}_lo")

                def gu_unit(m, e):
                    src = io["w_gate"] if m % 2 == 0 else io["w_up"]
                    kk = m // 2
                    return (mring[:, gu_pos(m), :].rearrange("p (k n) -> p k n", k=2),
                            src[l, bass.ds(e, 1), kk * 256:(kk + 1) * 256, :].rearrange("a (k p) n -> p (a k) n", p=P))

                def d_unit(m, e):
                    return (mring[:, d_pos(m), :].rearrange("p (k n) -> p k n", k=2),
                            io["w_down"][l, bass.ds(e, 1), m * 256:(m + 1) * 256, :].rearrange("a (k p) n -> p (a k) n", p=P))

                for m in range(8):
                    sp.dma_start(*gu_unit(m, 0)).then_inc(gsem[gu_pos(m)], 16)
                for m in range(4):
                    sp.dma_start(*d_unit(m, 0)).then_inc(gsem[d_pos(m)], 16)
                sp.wait_ge(*past("table", l))
                nb = sp.value_load(tabi[0:1, TAB:TAB + 1], min_val=4, max_val=MAXB)
                last_block = sp.value_load(tabi[0:1, 2 * TAB + 1:2 * TAB + 2], min_val=3, max_val=MAXB - 1)
                e0 = sp.value_load(tabi[0:1, 0:1], min_val=0, max_val=E - 1)
                redo = sem(f"m{l}_redo")
                with sp.If(e0 > 0):
                    for u in range(12):
                        sp.wait_ge(gsem[u], 16)
                    for m in range(8):
                        sp.dma_start(*gu_unit(m, e0)).then_inc(redo, 16)
                    for m in range(4):
                        sp.dma_start(*d_unit(m, e0)).then_inc(redo, 16)
                    sp.wait_ge(redo, 12 * 16)
                sp.sem_inc(sem(f"m{l}_first"), 1)

                def load_gu(i, seen):
                    e = sp.value_load(tabi[0:1, bass.ds(i, 1)], min_val=0, max_val=E - 1)
                    new = sp.value_load(tabi[0:1, bass.ds(i + TAB + 1, 1)], min_val=0, max_val=1)
                    with sp.If(new > 0):
                        for m in range(8):
                            sp.wait_ge(split, seen + (2 * m + 2))
                            sp.dma_start(*gu_unit(m, e)).then_inc(gsem[gu_pos(m)], 16)
                    with sp.If(new < 1):
                        for m in range(8):
                            sp.wait_ge(split, seen + (2 * m + 2))
                            sp.sem_inc(gsem[gu_pos(m)], 16)

                def load_down(i, seen):
                    e = sp.value_load(tabi[0:1, bass.ds(i, 1)], min_val=0, max_val=E - 1)
                    new = sp.value_load(tabi[0:1, bass.ds(i + TAB + 1, 1)], min_val=0, max_val=1)
                    with sp.If(new > 0):
                        for m in range(4):
                            sp.wait_ge(split, seen + (2 * m + 2))
                            sp.dma_start(*d_unit(m, e)).then_inc(gsem[d_pos(m)], 16)
                    with sp.If(new < 1):
                        for m in range(4):
                            sp.wait_ge(split, seen + (2 * m + 2))
                            sp.sem_inc(gsem[d_pos(m)], 16)

                load_gu(1, gu_slab(0, 0))
                with sp.Fori(2, nb) as i:
                    load_gu(i, gu_slab(i - 1, 0))
                    load_down(i - 1, down_slab(i - 1, 0))
                load_down(nb - 1, down_slab(last_block, 0))

        @block.gpsimd
        def _(pool):
            pool.memset(ones[:, :], 1.0).then_inc(*up("fill", "ones"))
            def carry_wait():
                pool.sem_inc(sem("pool_pace"), 1)

            pool.memset(zeros[:, :], 0.0).then_inc(*up("fill", "zeros"))
            pool.memset(zeroi[:, :], 0).then_inc(*up("fill", "zeroi"))
            pool.memset(wap[:, :, :, :], 0.0).then_inc(*up("fill", "wap"))
            pool.memset(bacol[:, :, :], 0.0).then_inc(*up("fill", "bacol"))
            pool.memset(tb[:, :], 0.0).then_inc(*up("fill", "tb"))
            pool.iota(tokid[:, :], [[P, NT]], base=0, channel_multiplier=1).then_inc(*up("fill", "tokid"))
            pool.wait_ge(*past("fill", "zeroi"))
            for l in range(DEPTH):
                pool.dma_start(rtok[l][:, :].rearrange("(p n) a -> p (n a)", p=P), zeroi[:, :]).then_inc(*dma(f"rtok{l}", 0))

            def mod_load(ml, part, what):
                row, gain, at, gain_at = mod_rows(ml, part)
                dst, at, src = {"bias": (row, at, io["b_mod"][ml:ml + 1, part * D:(part + 1) * D]),
                                "gain": (gain, gain_at, io["g_mix" if part == 1 else "g_ffn"][ml:ml + 1, :])}[what]
                for s_ in range(2):
                    pool.dma_start(dst[s_:s_ + 1, :], src).then_inc(*dma(f"mrow{at}", ml, part, what))

            def mod_parts(seq, behind=lambda j: None, meanwhile=lambda: None):
                def gained(j):
                    return j < len(seq) and seq[j][1] in (1, 4)

                mod_load(*seq[0], "bias")
                if gained(0):
                    mod_load(*seq[0], "gain")
                else:
                    mod_load(*seq[1], "bias")
                meanwhile()
                for j, (ml, part) in enumerate(seq):
                    pool.wait_ge(*past("modrow", ml, part))
                    pool.dma_start(modd[ml, :, part * D:(part + 1) * D], mod_rows(ml, part)[0]).then_inc(*dma("modd", ml, part))
                    if gained(j) and j + 1 < len(seq):
                        mod_load(*seq[j + 1], "bias")
                    pool.wait_ge(*past("modd", ml, part))
                    if gained(j + 1):
                        mod_load(*seq[j + 1], "gain")
                    elif j + 2 < len(seq):
                        mod_load(*seq[j + 2], "bias")
                    behind(j)

            def small(l):
                if l:
                    pool.wait_ge(*past("gout", l - 1, tiles_out(l - 1)[-1]))
                    pool.wait_ge(*emptied("cc", l - 1))
                else:
                    for nm in ("wap", "bacol", "tb"):
                        pool.wait_ge(*past("fill", nm))
                for d, nm in enumerate(("gla_wa_f", "gla_wa_b")):
                    pool.dma_start(wap[d * LR:(d + 1) * LR, d, :, 0:DK],
                                   io[nm][l].rearrange("r (h d) -> r h d", h=GH)).then_inc(*dma("small", l))
                for d, nm in enumerate(("gla_ba_f", "gla_ba_b")):
                    for hh in range(2):
                        for f in range(2):
                            h = 2 * f + hh
                            pool.dma_start(bacol[hh * DKP:hh * DKP + DK, d, f:f + 1],
                                           io[nm][l, h * DK:(h + 1) * DK].rearrange("(d a) -> d a", a=1)
                                           ).then_inc(*dma("small", l))
                pool.dma_start(gnrow[:, :], io["gla_g_norm"][l:l + 1, :].to_broadcast([P, GWID])).then_inc(*dma("small", l))
                pool.dma_start(crow[0:CK, :], io["conv_w"][l]).then_inc(*dma("small", l))
                for j, nm in enumerate(("conv_b", "conv_ln_g", "conv_ln_b")):
                    pool.dma_start(crow[CK + j:CK + j + 1, :], io[nm][l:l + 1, :]).then_inc(*dma("small", l))
                if l:
                    pool.wait_ge(*past("toep", l - 1))
                for h in range(NH):
                    pool.dma_start(tb[7 * h:7 * h + 7, 48:79], io["na_rpb"][l, h, 4:11, :]).then_inc(*dma("tb", l))
                pool.wait_ge(*past("tb", l))
                pool.dma_start(bass.AP(toep, l * 42 * GRID_W * P, [[GRID_W * P, 42], [P, GRID_W], [1, P]]),
                               tb[:, :].rearrange("p (a n) -> p a n", a=1).to_broadcast([42, GRID_W, P])
                               ).then_inc(*dma("toep", l))

            def first_rows(j):
                for s_ in range(2):
                    part = MOD_EARLY[j][1]
                    pool.dma_start(rows[:, norm_slots(0, "mix", s_)[j], :],
                                   modd[0, s_:s_ + 1, part * D:(part + 1) * D].to_broadcast([P, D])
                                   ).then_inc(*dma(f"rows_mix{s_}", 0) if j else dma(f"rows_scale{s_}", 0))

            mod_parts(MOD_EARLY, first_rows, lambda: small(0))
            for l in range(DEPTH):
                if l:
                    pool.wait_ge(*past("arena_free", l))
                pool.memset(cpad, 0.0).then_inc(*up("padded", l, 0))
                pool.wait_ge(*past("w_full", "ht", l, "mix", NT - 1, 1))
                for parts in sub_ring:
                    for x in parts:
                        pool.memset(x[:, :].rearrange("p (k h d) -> p k h d", k=KD, h=2)[:, :, :, DK:DKP].bitcast(F32), 0.0
                                    ).then_inc(*up("padded", l, 1))
                if l:
                    small(l)
                pool.wait_ge(*past("toep", l))
                for qt in range(2):
                    for rl in range(2):
                        r = 2 * qt + rl
                        for h in range(NH):
                            off = (l * 42 + h * 7 + 3 - r) * GRID_W * P + GRID_W - 1
                            pool.dma_start(
                                bias4[64 * rl:64 * rl + 64, qt, h, :].rearrange("p (i n) -> p i n", i=4),
                                bass.AP(toep, off, [[P - 1, GRID_W], [GRID_W * P, 4], [1, GRID_W]])
                            ).then_inc(*dma("bias", l))
                least = (SLOTS if l < DEPTH - 1 else 2 * SEQ) // P
                if l == 0:
                    pool.wait_ge(*past("fill", "zeros"))
                n = (TAB - least) * D // 256
                pool.dma_start(yd[l][least * P:, :].rearrange("(p a) d -> p (a d)", p=P).rearrange("p (a n) -> p a n", a=n),
                               zeros[:, :].bitcast(F32).rearrange("p (a n) -> p a n", a=1).to_broadcast([P, n, 256])
                               ).then_inc(*dma("ydfill", l))
                pool.wait_ge(*past("scanned", l))
                def gates(j):
                    if mod_late(l)[j] == (l, 2):
                        for s_ in range(streams_out(l)):
                            rows_load(pool, l, "gate_mix", s_)

                mod_parts(mod_late(l), gates)
                for s_ in range(streams_out(l)):
                    rows_load(pool, l, "ffn", s_)
                for t in tiles_out(l):
                    pool.wait_ge(*past("h2", l, t))
                    pool.dma_start(h2l[l][t * P:(t + 1) * P, :], nh[:, (t % 2) * D:(t % 2 + 1) * D]).then_inc(*dma(f"h2d{t}", l, t))
                pool.wait_ge(*past(f"rtok{l}", 0))
                pool.wait_ge(*past("dest", l))
                for t in tiles_out(l):
                    for kk in range(2):
                        pool.indirect_dma_start(
                            out=rtok[l][:, :], out_offset=bass.IndirectOffsetOnAxis(ap=rti[:, 2 * t + kk:2 * t + kk + 1], axis=0),
                            in_=tokid[:, t:t + 1], in_offset=None).then_inc(*dma(f"rtok{l}", 1))
                pool.wait_ge(*past(f"rtok{l}", 1))
                for t in tiles_out(l):
                    pool.wait_ge(*past(f"h2d{t}", l, t))
                pool.wait_ge(*past("routed", l))
                nb = pool.value_load(tabi[0:1, TAB:TAB + 1], min_val=4, max_val=MAXB)
                s_idx, s_xg, s_xf = sem(f"m{l}_idx"), sem(f"m{l}_xg"), sem(f"m{l}_xf")

                def gather(at):
                    pool.indirect_dma_start(out=xe[:, :], out_offset=None, in_=h2l[l][:, :],
                                            in_offset=bass.IndirectOffsetOnAxis(ap=at, axis=0)).then_inc(s_xg, 16)

                pool.dma_start(idx[:, 0:1], rtok[l][0:P, :]).then_inc(s_idx, 16)
                pool.wait_ge(s_idx, 16)
                gather(idx[:, 0:1])
                pool.dma_start(idx[:, 1:1 + TAB], rtok[l][:, :].rearrange("(b p) a -> p (b a)", p=P), allow_slow_non_contiguous=True).then_inc(s_idx, 16)
                pool.wait_ge(s_idx, 32)
                with pool.Fori(1, nb + 1) as i:
                    pool.wait_ge(s_xf, i)
                    carry_wait()
                    pool.tensor_copy(idx[:, 0:1], idx[:, bass.ds(i + 1, 1)]).then_inc(sem(f"m{l}_col"), 1)
                    pool.wait_ge(sem(f"m{l}_col"), i)
                    carry_wait()
                    gather(idx[:, 0:1])
                for s_ in range(streams_out(l)):
                    rows_load(pool, l, "gate_ffn", s_)
                if l < DEPTH - 1:
                    rows_load(pool, l + 1, "mix", 0)
                else:
                    pool.wait_ge(*past("rows_used", l, "ffn", 0))
                    pool.dma_start(rows[:, 2, :], io["g_final"].rearrange("(a d) -> a d", a=1).to_broadcast([P, D])
                                   ).then_inc(*dma("rows_final"))
                pool.wait_ge(sem(f"m{l}_yd"), nb * 16 + 16)
                pool.wait_ge(s_xf, nb + 1)
                pool.wait_ge(sem(f"m{l}_xe"), nb * 2 + 2)
                pool.wait_ge(sem(f"m{l}_used"), nb * 24 + (8 + NSP))
                carry_wait()
                for t in tiles_out(l):
                    for kk in range(2):
                        pool.indirect_dma_start(
                            out=comb[:, t, kk, :], out_offset=None, in_=yd[l][:, :],
                            in_offset=bass.IndirectOffsetOnAxis(ap=rti[:, 2 * t + kk:2 * t + kk + 1], axis=0)
                        ).then_inc(*dma(f"comb{t}", l))
                if l < DEPTH - 1:
                    rows_load(pool, l + 1, "mix", 1)

        @block.scalar
        def _(act):
            last = []

            def did(ins, *key):
                ins.then_inc(*up(*(key or ("act_chain",))))
                last[:] = [(sem(key[0] if key else "act_chain"), led.count[key[0] if key else "act_chain"])]

            def own():
                act.wait_ge(*last[0])

            def full(*key):
                act.wait_ge(*past("w_full", *key))
                return bank_of(key)

            def weigh(l):
                def work(t):
                    act.wait_ge(*past(f"comb{t}", l))
                    did(act.activation(comb[:, t, 0, :], comb[:, t, 0, :], ACT.Identity, scale=stat[:, 32 + t:33 + t]), "weighed", l, t)
                return work

            act.wait_ge(*past("crows", 1))
            did(act.activation(nh[0:2, D:2 * D], nh[0:2, 0:D], ACT.Silu), "csilu")
            act.wait_ge(*emptied("scol"))
            for l in range(DEPTH):
                norm_act(act, did, own, l, "mix", range(NT), weigh(l - 1) if l else lambda t: None)
                def sub_high(n):
                    if n >= len(SUBS):
                        return
                    if n == 0 or SUBS[n - 1][2] != SUBS[n][2]:
                        act.wait_ge(*landed("in", l, SUBS[n][2]))
                    if n >= 2:
                        act.wait_ge(*past("w_full", *sub_key(l, n - 2)))
                    else:
                        act.wait_ge(*past("padded", l, 1))
                    hi, _, src = sub_views(l, n)
                    did(act.copy(hi, src), "sub_hi", l, n)

                def softplus(part, groups):
                    for n_g in groups:
                        d, f = GROUPS[n_g]
                        x = zbuf(n_g)[1]
                        if part == 0:
                            act.wait_ge(*past("zready", l, d, f))
                            did(act.activation(x, cum4[:, d, f, :], ACT.Abs))
                            own()
                            did(act.activation(x, x, ACT.Exp, scale=-1.0))
                            own()
                        else:
                            did(act.activation(x, x, ACT.Ln, bias=1.0), "zln", l, d, f)

                sub_high(0)
                sub_high(1)
                for n, (nm, i, _) in enumerate(SUBS):
                    sub_high(n + 2)
                    key = sub_key(l, n)
                    if nm == "cg":
                        w = streams_out(l)
                        did(act.activation(ca4[:, i, 0:w, :], full(*key)[:, 0:w * SEQ].rearrange("p (s n) -> p s n", s=w),
                                           ACT.Sigmoid), "w_act", *key)
                    elif nm == "k":
                        did(act.copy(k3[:, i, :], full(*key)[:, :]), "w_act", *key)
                    elif nm == "gate" and i == KD // 2 - 1:
                        act.wait_ge(*past("w_full", *key))
                        for t in tiles_out(l):
                            did(act.activation(gate3[:, t, :], psum[t][:, 0:GWID], ACT.Silu), "w_act", "gate_t", l, t)
                    elif nm == "nq":
                        did(act.mul(nq3[:, i, :], full(*key)[:, :], DH ** -0.5), "w_act", *key)
                    elif nm == "nv" and i == KD // 2 - 1:
                        act.wait_ge(*past("w_full", *key))
                        for t in range(NT):
                            did(act.copy(nv3[:, t, :], psum[t][:, 0:NWID]), "w_act", "nv_t", l, t)
                    if nm == "v" and i < 3:
                        softplus(*((0, (0, 1)), (0, (2, 3)), (1, range(4)))[i])
                lst = na_list(l)

                def na_exp(n):
                    h, t = lst[n]
                    kn = T if t < NX else CTX
                    b = n % 2
                    act.wait_ge(*past("nmax", l, h, t))
                    if n >= 2:
                        act.wait_ge(*past("w_full", "pt", l, *lst[n - 2]))
                    did(act.activation(na_sc(b)[:, 0:kn], full("s", l, h, t)[:, 0:kn], ACT.Exp,
                                       bias=stat[:, 16 + b:17 + b], accum_out=stat[:, 20 + b:21 + b]),
                        "w_act", "s", l, h, t)

                def na(steps):
                    for n in steps:
                        if n + 1 < len(lst):
                            na_exp(n + 1)

                na_exp(0)
                for n_g, (d, f) in enumerate(GROUPS):
                    act.wait_ge(*past("diffs", l, d, f))
                    qs, ks = (1, 0) if d == 0 else (0, 1)
                    did(act.activation(KI, KI, ACT.Exp, scale=-1.0 / TAU), "kexp", l, d, f)
                    for X, n, h in ((X64, 4, 64), (X32, 8, 32)):
                        X4 = X.rearrange("p (n two h) -> p n two h", two=2, h=h)
                        did(act.activation(X4[:, :, qs, :], X4[:, :, qs, :], ACT.Exp, scale=1.0 / TAU))
                        did(act.activation(X4[:, :, ks, :], X4[:, :, ks, :], ACT.Exp, scale=-1.0 / TAU))
                    did(act.activation(Kd, Qd, ACT.Exp, scale=-1.0 / TAU))
                    own()
                    did(act.activation(Qd, Qd, ACT.Exp, scale=1.0 / TAU))
                    did(act.activation(QI, cum4[:, d, f, :], ACT.Exp, scale=1.0 / TAU))
                    endc = cum4[:, d, f, :].rearrange("p (t n) -> p t n", t=NT)[:, :, P - 1 if d == 0 else 0]
                    did(act.activation(stat[:, 0:NT], endc, ACT.Exp, scale=1.0 / TAU), "factors", l, d, f)
                    na(na_steps(l, n_g, 0))
                    did(act.copy(kit.rearrange("p (t n) -> p t n", t=NT),
                                 full("kt", l, d, f)[:, :].rearrange("p (t n) -> p t n", t=NT)), "w_act", "kt", l, d, f)
                    na(na_steps(l, n_g, 1))
                    na(na_steps(l, n_g, 2))
                def tail(part):
                    nt = len(tiles_out(l))
                    if part < 2:
                        for t in (2 * part, 2 * part + 1):
                            if t < nt:
                                if t < 2:
                                    act.wait_ge(*past("group_done", l, *GROUPS[-1]))
                                else:
                                    act.wait_ge(*past("gsq_used", l, t - 2))
                                did(act.activation(ST[:, t % 2 * 512:t % 2 * 512 + GWID], psum[t][:, 0:GWID], ACT.Square), "gsq", l, t)
                    elif part == 2:
                        act.wait_ge(*past("cvar", l))
                        did(act.activation(lnb(2), lnb(2), ACT.Sqrt), "cstd", l)
                        act.wait_ge(*past("gvar", l))
                        did(act.activation(stat[:, 44:44 + nt * GH], stat[:, 44:44 + nt * GH], ACT.Sqrt), "gstd", l)

                for n_, parts in tail_steps(l):
                    for part in parts:
                        tail(part)
                    na([n_])
                n = streams_out(l)
                for ct in range(2):
                    act.wait_ge(*past("cnorm", l, ct))
                    did(act.activation(hT3[:, 6 + ct, 0:n * SEQ], ca4[:, ct, 0:n, :].rearrange("p s n -> p (s n)"),
                                       ACT.Silu, scale=ccol[:, ct, CK + 1:CK + 2], bias=ccol[:, ct, CK + 2:CK + 3]), "cact", l, ct)
                for t in tiles_out(l):
                    did(act.copy(hT3[:, 0:3, t * P:(t + 1) * P],
                                 full("gt", l, t)[:, 0:GWID].rearrange("p (k n) -> p k n", k=3)), "w_act", "gt", l, t)
                norm_act(act, did, own, l, "ffn", tiles_out(l))
                n = len(tiles_out(l)) * E
                act.wait_ge(*past("w_full", "lg", l))
                did(act.activation(rt[:, 0, 0:n], psum[0][:, 0:n], ACT.Sigmoid), "w_act", "lg", l)
                act.wait_ge(*past("routed", l))
                nb = act.value_load(tabi[0:1, TAB:TAB + 1], min_val=4, max_val=MAXB)
                last_block = act.value_load(tabi[0:1, 2 * TAB + 1:2 * TAB + 2], min_val=3, max_val=MAXB - 1)
                s = {x: sem(f"m{l}_{x}") for x in ("first", "hi", "used", "sil", "hf", "he", "yd", "ye", "mul")}
                land = [sem(f"m{l}_land{j}") for j in range(12)]
                act.sem_inc(s["yd"], 16)
                act.sem_inc(s["ye"], 2)
                act.sem_inc(s["hi"], 8)
                act.sem_inc(s["used"], 8 + NSP)
                act.wait_ge(*past("ydfill", l))
                act.wait_ge(s["first"], 1)

                def high(slabs):
                    for before, n, u, half, loads in slabs:
                        if half == 0:
                            act.wait_ge(land[u], loads)
                        act.wait_ge(s["used"], before + 1)
                        act.copy(split_of(n)[0], mring[:, u, half * D:(half + 1) * D]).then_inc(s["hi"], 1)

                def silu(i):
                    act.wait_ge(s["used"], gu_slab(i, 16 + NSP))
                    for c in range(2):
                        act.activation(hb[:, c * 512:(c + 1) * 512], psum[c][:, :], ACT.Silu).then_inc(s["sil"], 1)

                def h_out(i):
                    act.wait_ge(s["hf"], i + 1)
                    for c in range(2):
                        act.copy(gTh[:, c * 512:(c + 1) * 512], psum[6 + c][:, :]).then_inc(s["he"], 1)

                def y_out(i, done, dst):
                    act.wait_ge(s["used"], done)
                    act.wait_ge(s["yd"], i * 16)
                    for c in range(2):
                        act.copy(yb[:, c * 512:(c + 1) * 512], psum[4 + c][:, :]).then_inc(s["ye"], 1)
                    act.wait_ge(s["ye"], i * 2 + 2)
                    act.dma_start(dst, yb[:, :]).then_inc(s["yd"], 16)

                def block_of(i, ahead):
                    high(gate_ups(i, NSP, 16))
                    high(downs(i, 0, NSP))
                    silu(i)
                    high(downs(i, NSP, 8))
                    high(ahead)
                    y_out(i, down_slab(i, 8 + NSP), yd[l][bass.ds((i - 1) * P, P), :])
                    h_out(i)

                high(gate_ups(0, 0, 16))
                silu(0)
                high(gate_ups(1, 0, NSP))
                h_out(0)
                with act.Fori(1, nb - 1) as i:
                    block_of(i, gate_ups(i, 0, NSP, ahead=1))
                block_of(last_block, downs(nb, 0, NSP, tail=True))
                high(downs(nb, NSP, 8, tail=True))
                y_out(nb, down_slab(nb, 8 + NSP, tail=True), yd[l][bass.ds((nb - 1) * P, P), :])
            norm_act(act, did, own, DEPTH, "fin", range(NX), weigh(DEPTH - 1))
            for t in range(NX):
                act.wait_ge(*past("final", t))
                act.dma_start(io["out"][0, t * P:(t + 1) * P, :], nh[:, t * D:(t + 1) * D]).then_inc(*dma("out", t))
            act.wait_ge(*past("out", NX - 1))

        @block.vector
        def _(dve):
            last = []

            def did(ins, *key):
                ins.then_inc(*up(*(key or ("dve_chain",))))
                last[:] = [(sem(key[0] if key else "dve_chain"), led.count[key[0] if key else "dve_chain"])]

            def own():
                dve.wait_ge(*last[0])

            def mark(*key):
                own()
                did(dve.engine_nop(), *key)

            def full(*key):
                dve.wait_ge(*past("w_full", *key))
                return bank_of(key)

            def norm(l, which, tiles, work):
                def stats(s):
                    for t in (2 * s, 2 * s + 1):
                        dve.wait_ge(*past("sumsq", l, which, t))
                    var = stat[:, 28 + 2 * s:30 + 2 * s]
                    did(dve.tensor_scalar(var, stat[:, 24 + 2 * s:26 + 2 * s], 1.0 / D, EPS, ALU.mult, ALU.add), "nvar", l, which, s)
                    dve.wait_ge(*past("nstd", l, which, s))
                    did(dve.reciprocal(var, var))
                    own()

                def apply(t):
                    buf = nh[:, (t % 2) * D:(t % 2 + 1) * D]
                    if which == "fin":
                        if t == 0:
                            dve.wait_ge(*past("rows_final"))
                        did(dve.scalar_tensor_tensor(buf, xres[:, t, :], stat[:, 28 + t:29 + t], rows[:, 2, :],
                                                     ALU.mult, ALU.mult), "final", t)
                        return
                    s = t // NX
                    scale, shift = norm_slots(l, which, s)
                    if t % NX == 0:
                        dve.wait_ge(*(past(f"rows_scale{s}", 0) if (l, which) == (0, "mix") else past(f"rows_{which}{s}", l)))
                    if t >= 2:
                        dve.wait_ge(*past("w_full", "ht", l, which, t - 2, 1))
                        if which == "ffn":
                            dve.wait_ge(*past(f"h2d{t - 2}", l, t - 2))
                    did(dve.scalar_tensor_tensor(buf, xres[:, t, :], stat[:, 28 + t:29 + t], rows[:, scale, :], ALU.mult, ALU.mult))
                    own()
                    if t % NX == 0 and (l, which) == (0, "mix"):
                        dve.wait_ge(*past(f"rows_mix{s}", 0))
                    did(dve.tensor_tensor(buf, buf, rows[:, shift, :], ALU.add), "h2" if which == "ffn" else "h1", l, t)
                    if t % NX == NX - 1:
                        mark("rows_used", l, which, s)

                def turned(t):
                    if which == "mix":
                        for c in range(2):
                            dve.wait_ge(*past("ht_hi", l, t, c))
                            at = (slice(None), slice(4 * c, 4 * c + 4), slice(t * P, (t + 1) * P))
                            did(dve.tensor_tensor(hTl[at], full("ht", l, which, t, c)[:, :].rearrange("p (k n) -> p k n", k=4),
                                                  hTh[at].bitcast(F32), ALU.subtract), "w_dve", "ht", l, which, t, c)
                        return
                    did(dve.tensor_copy(hT3[:, 0:4, t * P:(t + 1) * P],
                                        full("ht", l, which, t, 0)[:, :].rearrange("p (k n) -> p k n", k=4)),
                        "w_dve", "ht", l, which, t, 0)

                def ready(t):
                    work(t)
                    mark("xready", l, which, t)

                ready(0)
                ready(1)
                stats(0)
                apply(0)
                apply(1)
                if len(tiles) > 2:
                    ready(2)
                    turned(0)
                    ready(3)
                    turned(1)
                    stats(1)
                    apply(2)
                    apply(3)
                if which != "fin":
                    turned(tiles[-2])
                    turned(tiles[-1])

            def residual(l):
                def work(t):
                    if t % NX == 0:
                        dve.wait_ge(*past(f"rows_gate_mix{t // NX}", l))
                    for c in range(2):
                        b = psum[t % 2 * 2 + c]
                        dve.wait_ge(*past("y_full", l, t, c))
                        sl = slice(c * 512, (c + 1) * 512)
                        did(dve.tensor_tensor(b[:, :], b[:, :], rows[:, t // NX, sl], ALU.mult))
                        own()
                        did(dve.tensor_tensor(xres[:, t, sl], xres[:, t, sl], b[:, :], ALU.add), "y_free", l, t, c)
                    if t == tiles_out(l)[-1]:
                        mark("rows_used", l, "gate_mix")
                return work

            def combine(l):
                def work(t):
                    if l < 0:
                        if t % NX == 0:
                            dve.wait_ge(*past("xin", t // NX))
                        return
                    if t % NX == 0 and t in tiles_out(l):
                        dve.wait_ge(*past(f"rows_gate_ffn{t // NX}", l))
                    a, b = comb[:, t, 0, :], comb[:, t, 1, :]
                    dve.wait_ge(*past(f"comb{t}", l))
                    dve.wait_ge(*past("weighed", l, t))
                    did(dve.scalar_tensor_tensor(a, b, stat[:, 32 + NT + t:33 + NT + t], a, ALU.mult, ALU.add))
                    own()
                    did(dve.tensor_tensor(a, a, rows[:, t // NX, :], ALU.mult))
                    own()
                    did(dve.tensor_tensor(xres[:, t, :], xres[:, t, :], a, ALU.add))
                    if t == tiles_out(l)[-1]:
                        mark("rows_used", l, "gate_ffn")
                        mark("comb_last", l)
                        mark("arena_free", l + 1)
                return work

            dve.wait_ge(*past("csilu"))
            did(dve.tensor_copy(scol[:, :, :], full("scol")[:, 0:2 * KD].rearrange("p (k s) -> p k s", s=2)), "w_dve", "scol")

            def mod_out(ml, part, u):
                row, gain, at, gain_at = mod_rows(ml, part)
                if u == 0:
                    dve.wait_ge(*past(f"mrow{at}", ml, part, "bias"))
                sl = slice(u * MW, (u + 1) * MW)
                did(dve.tensor_tensor(row[:, sl], full("mod", ml, part, u)[0:2, 0:MW], row[:, sl], ALU.add),
                    "w_dve", "mod", ml, part, u)
                if u == MU - 1:
                    own()
                    if part in (1, 4):
                        dve.wait_ge(*past(f"mrow{gain_at}", ml, part, "gain"))
                        did(dve.scalar_tensor_tensor(row, row, 1.0, gain, ALU.add, ALU.mult), "modrow", ml, part)
                    else:
                        did(dve.engine_nop(), "modrow", ml, part)

            for ml, part in MOD_EARLY:
                for u in range(MU):
                    mod_out(ml, part, u)
            for l in range(DEPTH):
                norm(l, "mix", range(NT), combine(l - 1))
                if l:
                    dve.wait_ge(*past("arena_free", l))
                def sub_low(n):
                    if n >= len(SUBS):
                        return
                    dve.wait_ge(*past("sub_hi", l, n))
                    hi, lo, src = sub_views(l, n)
                    did(dve.tensor_tensor(lo, src, hi.bitcast(F32), ALU.subtract), "sub_lo", l, n)

                def decay_argument(n_g):
                    d, f = GROUPS[n_g]
                    z = cum4[:, d, f, :]
                    did(dve.tensor_scalar(z, full("z", l, d, f)[:, :], bacol[:, d, f:f + 1], None, ALU.add), "w_dve", "z", l, d, f)
                    own()
                    did(dve.tensor_scalar(zbuf(n_g)[0], z, 0.0, None, ALU.min), "zready", l, d, f)

                def decay_sum(n_g):
                    d, f = GROUPS[n_g]
                    dve.wait_ge(*past("zln", l, d, f))
                    g_, sp_ = zbuf(n_g)
                    did(dve.tensor_tensor(g_, g_, sp_, ALU.subtract))
                    own()
                    dst = cum4[:, d, f, :]
                    if d == 0:
                        did(dve.tensor_tensor_scan(dst, cst("notfirst"), g_, 0.0, ALU.mult, ALU.add))
                    else:
                        did(dve.tensor_tensor_scan(dst[:, ::-1], cst("notfirst"), g_[:, ::-1], 0.0, ALU.mult, ALU.add))

                def rope(nm, X):
                    for f in range(2):
                        b = full(nm, l, f)
                        did(dve.tensor_tensor(stat2(f), b[:, 0:SEQ], cst("sin"), ALU.mult), "w_dve", nm, l, f)
                        dve.wait_ge(*emptied("k", l, 1))
                        did(dve.tensor_tensor(X[:, f, 0:SEQ], X[:, f, 0:SEQ], cst("cos"), ALU.mult))
                        own()
                        did(dve.tensor_tensor(X[:, f, 0:SEQ], X[:, f, 0:SEQ], stat2(f), ALU.add), "roped", l, nm, f)

                def mask(qt):
                    dve.wait_ge(*past("bias", l))
                    bv = bias4[:, qt, :, :].rearrange("p h (i n) -> p (h i) n", i=4)
                    did(dve.tensor_tensor(bv, bv, cst("window").rearrange("p (a n) -> p a n", a=1).to_broadcast([P, NH * 4, GRID_W]),
                                          ALU.add), "masked", l, qt)

                sub_low(0)
                sub_low(1)
                for n, (nm, i, _) in enumerate(SUBS):
                    sub_low(n + 2)
                    key = sub_key(l, n)
                    if nm == "q":
                        did(dve.tensor_scalar(q3[:, i, :], full(*key)[:, :], DK ** -0.5, None, ALU.mult), "w_dve", *key)
                    elif nm == "a":
                        did(dve.tensor_copy(aT[0:2 * LR, :], full(*key)[0:2 * LR, :]), "w_dve", *key)
                    elif nm == "ca":
                        w = streams_out(l)
                        b = full(*key)
                        dve.wait_ge(*emptied("cg", l, i))
                        dve.wait_ge(*past("padded", l, 0))
                        did(dve.tensor_tensor(cp4[:, i, 0:w, HALF:HALF + SEQ],
                                              b[:, 0:w * SEQ].rearrange("p (s n) -> p s n", s=w), ca4[:, i, 0:w, :], ALU.mult),
                            "w_dve", *key)
                        for n_g in (2 * i, 2 * i + 1):
                            decay_argument(n_g)
                    elif nm == "v":
                        if i < 2:
                            own()
                            rope(*(("rq", q3), ("rk", k3))[i])
                        if i == KD // 2 - 1:
                            dve.wait_ge(*past("w_full", *key))
                            for t in range(NT):
                                did(dve.tensor_copy(v3[:, t, :], psum[t][:, 0:GWID]), "w_dve", "v_t", l, t)
                    elif nm == "nq":
                        decay_sum(i)
                    elif nm == "gate" and i == 0:
                        decay_sum(3)
                        mark("scanned", l)
                    elif nm == "nk":
                        did(dve.tensor_copy(nk3[:, i, :], full(*key)[:, :]), "w_dve", *key)
                    elif nm == "nv" and i < 2:
                        mask(i)
                did(dve.tensor_copy(ccol[:, :, :], full("cc", l)[:, 0:2 * (CK + 3)].rearrange("p (c k) -> p c k", c=2)),
                    "w_dve", "cc", l)
                own()
                lst = na_list(l)
                taps = [(j, ct) for j in range(CK) for ct in range(2)]

                def na_max(n):
                    h, t = lst[n]
                    did(dve.tensor_reduce(stat[:, 16 + n % 2:17 + n % 2], full("s", l, h, t)[:, 0:T if t < NX else CTX],
                                          AX.X, ALU.max, negate=True), "nmax", l, h, t)

                def na_finish(n):
                    h, t = lst[n]
                    kn = T if t < NX else CTX
                    b = n % 2
                    if n >= 2:
                        dve.wait_ge(*past("w_full", "no", l, *lst[n - 2]))
                    did(dve.tensor_copy(na_pt(b)[:, 0:kn], full("pt", l, h, t)[:, 0:kn]), "w_dve", "pt", l, h, t)
                    did(dve.reciprocal(stat[:, 20 + b:21 + b], stat[:, 20 + b:21 + b]))
                    own()

                def na_out(n):
                    h, t = lst[n]
                    o_ps = full("no", l, h, t)
                    did(dve.tensor_scalar(nout3[:, t, h * DH:(h + 1) * DH], o_ps[:, 0:DH], stat[:, 20 + n % 2:21 + n % 2], None,
                                          ALU.mult), "w_dve", "no", l, h, t)

                def tap(j, ct):
                    n = streams_out(l)
                    if j == 0:
                        did(dve.tensor_scalar(ca4[:, ct, 0:n, :], cp4[:, ct, 0:n, 0:SEQ], ccol[:, ct, 0:1],
                                              ccol[:, ct, CK:CK + 1], ALU.mult, ALU.add), "tap", l, j, ct)
                    else:
                        dve.wait_ge(*past("tap", l, j - 1, ct))
                        did(dve.scalar_tensor_tensor(ca4[:, ct, 0:n, :], cp4[:, ct, 0:n, j:j + SEQ], ccol[:, ct, j:j + 1],
                                                     ca4[:, ct, 0:n, :], ALU.mult, ALU.add), "tap", l, j, ct)

                def na(steps):
                    for n in steps:
                        before_tail = len(GROUPS) * sum(na_between(l))
                        mine = share(taps, n, before_tail) if n < before_tail else []
                        if n + 1 < len(lst):
                            na_max(n + 1)
                        for j, ct in mine[:1]:
                            tap(j, ct)
                        na_finish(n)
                        for ml, (part, u) in share(mod_units(l), n, len(lst)):
                            mod_out(ml, part, u)
                        for j, ct in mine[1:]:
                            tap(j, ct)
                        na_out(n)

                na_max(0)
                own()
                did(dve.memset(states[:, :], 0.0))
                for n_g, (d, f) in enumerate(GROUPS):
                    if n_g:
                        dve.wait_ge(*past("group_done", l, *GROUPS[n_g - 1]))
                    own()
                    c = cum4[:, d, f, :]
                    refs = ((X64, 128, 63 if d == 0 else 64), (X32, 64, 31 if d == 0 else 32),
                            (Qd, 32, 15 if d == 0 else 16), (KI, 128, 127 if d == 0 else 0))
                    for X, w, r in refs:
                        cv = c.rearrange("p (n w) -> p n w", w=w)
                        did(dve.tensor_tensor(X.rearrange("p (n w) -> p n w", w=w), cv,
                                              cv[:, :, r:r + 1].to_broadcast([P, T // w, w]), ALU.subtract))
                    own()
                    did(dve.tensor_scalar(Qd, Qd, CLAMP, -CLAMP, ALU.min, ALU.max), "diffs", l, d, f)
                    na(na_steps(l, n_g, 0))
                    dve.wait_ge(*past("kexp", l, d, f))
                    did(dve.tensor_tensor(KI, KI, k3[:, f, :], ALU.mult), "kint", l, d, f)
                    dve.wait_ge(*past("factors", l, d, f))
                    qs, ks = (1, 0) if d == 0 else (0, 1)
                    for X, n, h in ((X64, 4, 64), (X32, 8, 32)):
                        X4 = X.rearrange("p (n two h) -> p n two h", two=2, h=h)
                        for side, src in ((qs, q3), (ks, k3)):
                            s4 = src[:, f, :].rearrange("p (n two h) -> p n two h", two=2, h=h)
                            did(dve.tensor_tensor(X4[:, :, side, :], X4[:, :, side, :], s4[:, :, side, :], ALU.mult))
                    did(dve.tensor_tensor(Qd, Qd, q3[:, f, :], ALU.mult))
                    did(dve.tensor_tensor(Kd, Kd, k3[:, f, :], ALU.mult))
                    did(dve.tensor_tensor(QI, QI, q3[:, f, :], ALU.mult), "scaled", l, d, f)
                    na(na_steps(l, n_g, 1))
                    order = gla_order(d)
                    kv = full("kv", l, d, f)
                    for j in range(NT - 1):
                        own()
                        t = order[j]
                        for hh in range(2):
                            key = ("w_dve", "kv", l, d, f) if (j, hh) == (NT - 2, 1) else ()
                            r = slice(hh * DKP, (hh + 1) * DKP)
                            a0, a1 = (2 * j + hh) * DV, (2 * j + 2 + hh) * DV
                            did(dve.scalar_tensor_tensor(states[r, a1:a1 + DV], states[r, a0:a0 + DV],
                                                         stat[r, t:t + 1], kv[r, t * DV:(t + 1) * DV], ALU.mult, ALU.add), *key)
                    for hh in range(2):
                        m = cst(f"causal{d}").rearrange("p (a n) -> p a n", a=1).to_broadcast([P, NT, P])
                        did(dve.tensor_tensor(ST[:, hh * 512:(hh + 1) * 512].rearrange("p (t n) -> p t n", t=NT),
                                              full("sc", l, d, f, hh)[:, :].rearrange("p (t n) -> p t n", t=NT), m, ALU.mult),
                            "w_dve", "sc", l, d, f, hh)
                    na(na_steps(l, n_g, 2))
                w = streams_out(l) * SEQ
                mean, var = lnb(3)[:, 0:w], lnb(2)
                nt = len(tiles_out(l))
                gst = stat[:, 44:44 + nt * GH]

                def conv_half(ct):
                    return ca4[:, ct, 0:streams_out(l), :].rearrange("p s n -> p (s n)")

                def sums_of_squares(tiles):
                    for t in tiles:
                        dve.wait_ge(*past("gsq", l, t))
                        did(dve.tensor_reduce(stat[:, 44 + t * GH:44 + (t + 1) * GH],
                                              ST[:, t % 2 * 512:t % 2 * 512 + GWID].rearrange("p (h e) -> p h e", h=GH),
                                              AX.X, ALU.add), "gsq_used", l, t)

                def tail(part):
                    if part == 0:
                        dve.wait_ge(*past("group_done", l, *GROUPS[-1]))
                        own()
                        for ct in range(2):
                            did(dve.tensor_tensor(lnb(ct)[:, 0:w], conv_half(ct), conv_half(ct), ALU.mult), "csq", l, ct)
                        did(dve.memset(var, 1.0))
                    elif part == 1:
                        did(dve.tensor_scalar(mean, full("cs", l)[:, 0:w], 1.0 / CW, None, ALU.mult), "w_dve", "cs", l)
                        own()
                        did(dve.tensor_tensor(lnb(4)[:, 0:w], mean, mean, ALU.mult))
                        own()
                        did(dve.scalar_tensor_tensor(var[:, 0:w], full("cs2", l)[:, 0:w], 1.0 / CW, lnb(4)[:, 0:w],
                                                     ALU.mult, ALU.subtract), "w_dve", "cs2", l)
                        own()
                        did(dve.tensor_scalar(var[:, 0:w], var[:, 0:w], 0.0, EPS, ALU.max, ALU.add), "cvar", l)
                        sums_of_squares((0, 1))
                    elif part == 2:
                        sums_of_squares(range(2, nt))
                        own()
                        did(dve.tensor_scalar(gst, gst, 1.0 / DV, EPS, ALU.mult, ALU.add), "gvar", l)
                    elif part == 3:
                        dve.wait_ge(*past("cstd", l))
                        did(dve.reciprocal(var[:, 0:w], var[:, 0:w]))
                        for ct in range(2):
                            did(dve.tensor_tensor(conv_half(ct), conv_half(ct), mean, ALU.subtract))
                            own()
                            did(dve.tensor_tensor(conv_half(ct), conv_half(ct), var[:, 0:w], ALU.mult), "cnorm", l, ct)
                        dve.wait_ge(*past("gstd", l))
                        did(dve.reciprocal(gst, gst))
                    else:
                        dve.wait_ge(*past("small", l))
                        own()
                        for t in tiles_out(l):
                            g3 = gout3[:, t, :].rearrange("p (h e) -> p h e", h=GH)
                            did(dve.tensor_tensor(g3, psum[t][:, 0:GWID].rearrange("p (h e) -> p h e", h=GH),
                                                  stat[:, 44 + t * GH:44 + (t + 1) * GH].rearrange("p (h a) -> p h a", a=1)
                                                  .to_broadcast([P, GH, DV]), ALU.mult), "o_free", l, t)
                            own()
                            did(dve.tensor_tensor(gout3[:, t, :], gout3[:, t, :], gnrow[:, :], ALU.mult))
                            own()
                            did(dve.tensor_tensor(gout3[:, t, :], gout3[:, t, :], gate3[:, t, :], ALU.mult), "gout", l, t)

                for n_, parts in tail_steps(l):
                    for part in parts:
                        tail(part)
                    na([n_])
                for t in tiles_out(l):
                    did(dve.tensor_copy(hT3[:, 3:6, t * P:(t + 1) * P],
                                        full("nt", l, t)[:, 0:NWID].rearrange("p (k n) -> p k n", k=3)), "w_dve", "nt", l, t)
                mark("mixed", l)
                norm(l, "ffn", tiles_out(l), residual(l))
                nt = len(tiles_out(l))
                n = nt * E
                dve.wait_ge(*emptied("lg", l))
                dve.wait_ge(*past("rw", 1))

                def r3(i):
                    return rt[:, i, 0:n].rearrange("p (t e) -> p t e", t=nt)

                def rg(i):
                    return rt[:, i, 0:n].rearrange("p (a e) -> p a e", e=EG)

                def bc(x, w):
                    return x.rearrange("p (a b) -> p a b", b=1).to_broadcast([P, x.shape[1], w])

                def row(x, m):
                    return x.rearrange("p (a e) -> p a e", a=1).to_broadcast([P, m, x.shape[1]])

                def step(ins, *key):
                    did(ins, *key)
                    own()

                AFF, SEL, PR, OH1, OH2, T1, T2, GR, SLOT, RR = 0, 1, 2, 4, 5, 6, 7, 8, 9, 10
                step(dve.tensor_tensor(r3(SEL), r3(AFF), row(rbias[:, :], nt), ALU.add))
                pr = rt[:, PR:PR + 2, :].rearrange("p a b -> p (a b)")[:, 0:nt * NG * 6].rearrange("p (a e) -> p a e", e=6)
                sg = rg(SEL)
                na_ = nt * NG
                step(dve.tensor_tensor(pr[:, :, 0:3], sg[:, :, 1:4], sg[:, :, 0:1].to_broadcast([P, na_, 3]), ALU.add))
                step(dve.tensor_tensor(pr[:, :, 3:5], sg[:, :, 2:4], sg[:, :, 1:2].to_broadcast([P, na_, 2]), ALU.add))
                step(dve.tensor_tensor(pr[:, :, 5:6], sg[:, :, 3:4], sg[:, :, 2:3], ALU.add))
                gs, gm, gt = rt[:, GR, 0:na_], rt[:, GR, 16:16 + nt], rt[:, GR, 32:32 + na_]
                step(dve.tensor_reduce(gs, pr, AX.X, ALU.max))

                def first_of(x3, m, red, t3, iota, out):
                    w = x3.shape[2]
                    step(dve.tensor_reduce(red, x3, AX.X, ALU.max))
                    step(dve.tensor_tensor(t3, x3, bc(red, w), ALU.is_equal))
                    step(dve.tensor_scalar(t3, t3, -100.0, None, ALU.mult))
                    step(dve.tensor_tensor(t3, t3, row(iota, m), ALU.add))
                    step(dve.tensor_reduce(red, t3, AX.X, ALU.min))
                    step(dve.tensor_tensor(out, t3, bc(red, w), ALU.is_equal))

                g3 = gs.rearrange("p (t g) -> p t g", t=nt)
                gt3 = gt.rearrange("p (t g) -> p t g", t=nt)
                first_of(g3, nt, gm, gt3, cst("iota4"), gt3)
                step(dve.tensor_tensor(rg(T2), sg, bc(gt, EG), ALU.mult))
                step(dve.tensor_scalar(gt, gt, 1e30, -1e30, ALU.mult, ALU.add))
                step(dve.tensor_tensor(rg(T2), rg(T2), bc(gt, EG), ALU.add))
                first_of(r3(T2), nt, gm, r3(T1), cst("iota16"), r3(OH1))
                step(dve.scalar_tensor_tensor(rt[:, T2, 0:n], rt[:, OH1, 0:n], -3e30, rt[:, T2, 0:n], ALU.mult, ALU.add))
                first_of(r3(T2), nt, gm, r3(T1), cst("iota16"), r3(OH2))
                step(dve.tensor_tensor(rt[:, RR, 0:n], rt[:, OH1, 0:n], rt[:, OH2, 0:n], ALU.add))
                run = rt[:, 12:14, :].rearrange("p a b -> p (a b)")
                step(dve.tensor_copy(run[:, 0:E], rt[:, RR, 0:E]))
                for t in range(1, nt):
                    step(dve.tensor_tensor(run[:, t * E:(t + 1) * E], run[:, (t - 1) * E:t * E], rt[:, RR, t * E:(t + 1) * E], ALU.add),
                         *(("assigned", l) if t == nt - 1 else ()))
                for kk, oh in enumerate((OH1, OH2)):
                    step(dve.tensor_tensor(rt[:, T1, 0:n], rt[:, AFF, 0:n], rt[:, oh, 0:n], ALU.mult))
                    step(dve.tensor_reduce(stat[:, 32 + kk * NT:32 + kk * NT + nt], r3(T1), AX.X, ALU.add))
                step(dve.tensor_tensor(stat[:, 40:40 + nt], stat[:, 32:32 + nt], stat[:, 32 + NT:32 + NT + nt], ALU.add))
                step(dve.reciprocal(stat[:, 40:40 + nt], stat[:, 40:40 + nt]))
                for kk in range(2):
                    ww = stat[:, 32 + kk * NT:32 + kk * NT + nt]
                    step(dve.tensor_tensor(ww, ww, stat[:, 40:40 + nt], ALU.mult))
                cnt = rt[:, 11, 0:E]
                step(dve.tensor_copy(cnt, full("count", l)[:, NT * E:NT * E + E]))
                step(dve.tensor_copy(rt[:, SLOT, 0:n], full("count", l)[:, 0:n]), "w_dve", "count", l)
                nbk, inc, tmp16 = rt[:, 11, 16:32], rt[:, 11, 32:48], rt[:, 11, 48:64]
                step(dve.tensor_scalar(nbk, cnt, 0.0, None, ALU.is_gt))
                for j in range(1, nt):
                    step(dve.tensor_scalar(tmp16, cnt, float(j * P), None, ALU.is_gt))
                    step(dve.tensor_tensor(nbk, nbk, tmp16, ALU.add))
                step(dve.tensor_tensor_scan(inc, ones[:, 0:E], nbk, 0.0, ALU.mult, ALU.add))
                step(dve.tensor_tensor(tmp16, inc, nbk, ALU.subtract))
                step(dve.tensor_scalar(tmp16, tmp16, float(P), None, ALU.mult))
                step(dve.tensor_tensor(r3(SLOT), r3(SLOT), row(tmp16, nt), ALU.add))
                for kk, oh in enumerate((OH1, OH2)):
                    step(dve.tensor_tensor(rt[:, T1, 0:n], rt[:, SLOT, 0:n], rt[:, oh, 0:n], ALU.mult))
                    step(dve.tensor_reduce(stat[:, 44 + kk * NT:44 + kk * NT + nt], r3(T1), AX.X, ALU.add))
                dv = stat[:, 44:44 + 2 * NT].rearrange("p (k t) -> p t k", k=2)[:, 0:nt, :]
                if l:
                    dve.wait_ge(*past("comb_last", l - 1))
                step(dve.tensor_copy(rti[:, 0:2 * nt].rearrange("p (t k) -> p t k", k=2), dv), "dest", l)
                tt = tmp[0:1, 0:TAB * E].rearrange("p (b e) -> p b e", b=TAB)
                tt = rt[0:1, 4:10, :].rearrange("p a b -> p (a b)")[:, 0:TAB * E].rearrange("p (b e) -> p b e", b=TAB)
                step(dve.tensor_tensor(tt, inc[0:1, :].rearrange("p (a e) -> p a e", a=1).to_broadcast([1, TAB, E]),
                                       cst("iotab")[0:1, :].rearrange("p (b a) -> p b a", a=1).to_broadcast([1, TAB, E]), ALU.is_le))
                step(dve.tensor_reduce(rt[0:1, 12, 0:TAB], tt, AX.X, ALU.add))
                step(dve.tensor_scalar(rt[0:1, 12, 0:TAB], rt[0:1, 12, 0:TAB], float(E - 1), None, ALU.min))
                step(dve.tensor_copy(rt[0:1, 12, TAB:TAB + 1], inc[0:1, E - 1:E]))
                step(dve.memset(rt[0:1, 12, TAB + 1:TAB + 2], 1.0))
                step(dve.tensor_tensor(rt[0:1, 12, TAB + 2:2 * TAB + 1], rt[0:1, 12, 1:TAB], rt[0:1, 12, 0:TAB - 1], ALU.is_gt))
                step(dve.tensor_scalar(rt[0:1, 12, 2 * TAB + 1:2 * TAB + 2], inc[0:1, E - 1:E], -1.0, None, ALU.add))
                step(dve.tensor_copy(tabi[0:1, 0:2 * TAB + 2], rt[0:1, 12, 0:2 * TAB + 2]), "routed", l)
                mark("table", l)
                nb = dve.value_load(tabi[0:1, TAB:TAB + 1], min_val=4, max_val=MAXB)
                last_block = dve.value_load(tabi[0:1, 2 * TAB + 1:2 * TAB + 2], min_val=3, max_val=MAXB - 1)
                s = {x: sem(f"m{l}_{x}") for x in ("hi", "lo", "sil", "xf", "xh", "xe", "mul", "he", "hl")}

                dve.sem_inc(s["lo"], 8)

                def low(slabs):
                    for before, n, u, half, _ in slabs:
                        dve.wait_ge(s["hi"], before + 1)
                        hi, lo = split_of(n)
                        dve.tensor_tensor(lo, mring[:, u, half * D:(half + 1) * D], hi.bitcast(F32), ALU.subtract).then_inc(s["lo"], 1)

                def x_out(i):
                    dve.wait_ge(s["xf"], i + 1)
                    for c in range(2):
                        dve.tensor_copy(xTh[:, c * 512:(c + 1) * 512], psum[6 + c][:, :]).then_inc(s["xh"], 1)
                    for c in range(2):
                        dve.wait_ge(s["xh"], i * 2 + (c + 1))
                        dve.tensor_tensor(xTl[:, c * 512:(c + 1) * 512], psum[6 + c][:, :],
                                          xTh[:, c * 512:(c + 1) * 512].bitcast(F32), ALU.subtract).then_inc(s["xe"], 1)

                def product(i):
                    for c in range(2):
                        dve.wait_ge(s["sil"], i * 2 + (c + 1))
                        dve.tensor_tensor(hb[:, c * 512:(c + 1) * 512], hb[:, c * 512:(c + 1) * 512], psum[2 + c][:, :],
                                          ALU.mult).then_inc(s["mul"], 1)

                def h_low(i):
                    for c in range(2):
                        dve.wait_ge(s["he"], i * 2 + (c + 1))
                        dve.tensor_tensor(gTl[:, c * 512:(c + 1) * 512], psum[6 + c][:, :],
                                          gTh[:, c * 512:(c + 1) * 512].bitcast(F32), ALU.subtract).then_inc(s["hl"], 1)

                def block_of(i, ahead):
                    low(gate_ups(i, NSP, 16))
                    low(downs(i, 0, NSP))
                    x_out(i + 1)
                    product(i)
                    low(downs(i, NSP, 8))
                    low(ahead)
                    h_low(i)

                low(gate_ups(0, 0, NSP))
                x_out(0)
                low(gate_ups(0, NSP, 16))
                x_out(1)
                product(0)
                low(gate_ups(1, 0, NSP))
                h_low(0)
                with dve.Fori(1, nb - 1) as i:
                    block_of(i, gate_ups(i, 0, NSP, ahead=1))
                block_of(last_block, downs(nb, 0, NSP, tail=True))
                low(downs(nb, NSP, 8, tail=True))
            norm(DEPTH, "fin", range(NX), combine(DEPTH - 1))

        @block.tensor
        def _(pe):
            def full(mm, *key):
                mm.then_inc(*up("w_full", *key))

            def slabs(key):
                return dring[:, dslot(key), :]

            pe.wait_ge(*past("const"))
            pe.wait_ge(*past("csilu"))
            b = take(pe, "scol")
            for kk in range(KD):
                mm = pe.transpose(b[:, 2 * kk:2 * kk + 2], nh[0:2, D + kk * P:D + (kk + 1) * P], ident[0:2, 0:2])
            full(mm, "scol")
            pe.wait_ge(*emptied("scol"))

            def mod_unit(ml, part, u):
                b = take(pe, "mod", ml, part, u)
                pe.wait_ge(*landed("mod", ml, (part, u)))
                w = slabs(("mod", ml, (part, u)))
                for kk in range(KD):
                    mm = pe.matmul(b[0:2, 0:MW], scol[:, kk, :], w[:, kk * MW:(kk + 1) * MW], start=kk == 0, stop=kk == KD - 1)
                full(mm, "mod", ml, part, u)

            for ml, part in MOD_EARLY:
                for u in range(MU):
                    mod_unit(ml, part, u)

            def turn_rows(l, which, t):
                pe.wait_ge(*past("h2" if which == "ffn" else "h1", l, t))
                for c in range(2):
                    b = take(pe, "ht", l, which, t, c)
                    for kk in range(4):
                        o = (t % 2) * D + (4 * c + kk) * P
                        mm = pe.transpose(b[:, kk * P:(kk + 1) * P], nh[:, o:o + P], ident)
                    full(mm, "ht", l, which, t, c)

            for l in range(DEPTH):
                for t in range(NT):
                    turn_rows(l, "mix", t)
                for t in range(NT):
                    for c in range(2):
                        pe.wait_ge(*emptied("ht", l, "mix", t, c))
                def sub_job(n):
                    nm, i, _ = SUBS[n]
                    b = None if nm in ("v", "gate", "nv") else take(pe, *sub_key(l, n))
                    pe.wait_ge(*past("sub_lo", l, n))
                    wd, k_n = {"a": (2 * LR, KD), "v": (UW, 2), "gate": (UW, 2), "nv": (UW, 2)}.get(nm, (P, KD))
                    w_hi, w_lo = [x[:, 0:k_n * wd].rearrange("p (k n) -> p k n", k=k_n) for x in sub_ring[n % 2]]
                    pairs = ((w_hi, hTh), (w_hi, hTl), (w_lo, hTh))
                    if b is None:
                        for t in tiles_out(l) if nm == "gate" else range(NT):
                            before = {"gate": "v_t", "nv": "gate_t"}.get(nm)
                            if i == 0 and before and (before == "v_t" or t in tiles_out(l)):
                                pe.wait_ge(*emptied(before, l, t))
                            if i == 0 and nm == "nv" and t not in tiles_out(l):
                                pe.wait_ge(*emptied("v_t", l, t))
                            for k2 in range(2):
                                kk = 2 * i + k2
                                for j, (w, h) in enumerate(pairs):
                                    mm = pe.matmul(psum[t][:, 0:UW], h[:, kk, t * P:(t + 1) * P], w[:, k2, :],
                                                   start=(kk, j) == (0, 0), stop=(kk, j) == (KD - 1, 2))
                    else:
                        width = streams_out(l) * SEQ if nm in ("ca", "cg") else T
                        for kk in range(KD):
                            for j, (w, h) in enumerate(pairs):
                                mm = pe.matmul(b[0:wd, 0:width], w[:, kk, :], h[:, kk, 0:width],
                                               start=(kk, j) == (0, 0), stop=(kk, j) == (KD - 1, 2))
                    full(mm, *sub_key(l, n))

                for n, (nm, i, _) in enumerate(SUBS):
                    sub_job(n)
                    if nm == "ca":
                        if i == 0:
                            pe.wait_ge(*emptied("a", l))
                            pe.wait_ge(*past("small", l))
                        for d, f in GROUPS[2 * i:2 * i + 2]:
                            b = take(pe, "z", l, d, f)
                            full(pe.matmul(b[:, :], wap[:, d, 2 * f:2 * f + 2, :], aT[0:2 * LR, :], start=True, stop=True), "z", l, d, f)
                    if nm == "v" and i < 2:
                        rot, X = (("rq", q3), ("rk", k3))[i]
                        for f in range(2):
                            pe.wait_ge(*emptied(rot[1], l, f))
                            b = take(pe, rot, l, f)
                            full(pe.matmul(b[:, 0:SEQ], cst("rot"), X[:, f, 0:SEQ], start=True, stop=True), rot, l, f)
                b = take(pe, "cc", l)
                for ct in range(2):
                    mm = pe.transpose(b[:, ct * (CK + 3):(ct + 1) * (CK + 3)], crow[:, ct * P:(ct + 1) * P], ident[0:CK + 3, 0:CK + 3])
                full(mm, "cc", l)
                lst = na_list(l)
                pe.wait_ge(*past("masked", l, 1))
                pe.wait_ge(*emptied("nq", l, 2))
                pe.wait_ge(*emptied("nk", l, 2))

                def scores(n):
                    h, t = lst[n]
                    r = slice((h % 2) * DH, (h % 2 + 1) * DH)
                    b = take(pe, "s", l, h, t)
                    lat = t < NX
                    k0 = 0 if lat else SEQ
                    if lat:
                        pe.matmul(b[:, 0:SEQ], ident, bias4[:, t, h, :], start=True, stop=False, skip_group_check=True)
                    mm = pe.matmul(b[:, 0:T - k0], nq3[r, h // 2, t * P:(t + 1) * P], nk3[r, h // 2, k0:T],
                                   start=not lat, stop=True, skip_group_check=True)
                    full(mm, "s", l, h, t)

                def na(steps):
                    for n in steps:
                        h, t = lst[n]
                        if n + 1 < len(lst):
                            scores(n + 1)
                        js = range(4) if t < NX else range(2)
                        t0 = 0 if t < NX else NX
                        b = take(pe, "pt", l, h, t)
                        pe.wait_ge(*emptied("s", l, h, t))
                        for j in js:
                            mm = pe.transpose(b[:, j * P:(j + 1) * P], na_sc(n % 2)[:, j * P:(j + 1) * P], ident)
                        full(mm, "pt", l, h, t)
                        for ml, (part, u) in share(mod_units(l), n, len(lst)):
                            mod_unit(ml, part, u)
                        b = take(pe, "no", l, h, t)
                        pe.wait_ge(*emptied("pt", l, h, t))
                        for j in js:
                            mm = pe.matmul(b[:, 0:DH], na_pt(n % 2)[:, j * P:(j + 1) * P], nv3[:, t0 + j, h * DH:(h + 1) * DH],
                                           start=j == 0, stop=j == len(js) - 1)
                        full(mm, "no", l, h, t)

                scores(0)
                for t in range(NT):
                    pe.wait_ge(*emptied("nv_t", l, t))
                for n_g, (d, f) in enumerate(GROUPS):
                    na(na_steps(l, n_g, 0))
                    order = gla_order(d)
                    pe.wait_ge(*past("kint", l, d, f))
                    b = take(pe, "kt", l, d, f)
                    for t in range(NT):
                        mm = pe.transpose(b[:, t * P:(t + 1) * P], KI[:, t * P:(t + 1) * P], ident)
                    full(mm, "kt", l, d, f)
                    na(na_steps(l, n_g, 1))
                    b = take(pe, "kv", l, d, f)
                    pe.wait_ge(*emptied("kt", l, d, f))
                    for t in range(NT):
                        for hh in range(2):
                            h = 2 * f + hh
                            mm = pe.matmul(b[hh * DKP:(hh + 1) * DKP, t * DV:(t + 1) * DV],
                                           kit[:, t * P + hh * DKP:t * P + (hh + 1) * DKP], v3[:, t, h * DV:(h + 1) * DV],
                                           start=True, stop=True)
                    full(mm, "kv", l, d, f)
                    pe.wait_ge(*past("scaled", l, d, f))
                    qs, ks = (1, 0) if d == 0 else (0, 1)
                    for hh in range(2):
                        r = slice(hh * DKP, (hh + 1) * DKP)
                        b = take(pe, "sc", l, d, f, hh)
                        pe.matmul(b[:, :], zeros[:, 0:P], zeros[:, :], start=True, stop=True, skip_group_check=True)
                        for t in tiles_out(l):
                            def block_of(s0, t0, w, kx, qx):
                                return pe.matmul(b[s0:s0 + w, t * P + t0:t * P + t0 + w], kx[r, t * P + s0:t * P + s0 + w],
                                                 qx[r, t * P + t0:t * P + t0 + w], start=False, stop=True, skip_group_check=True)
                            block_of(64 * ks, 64 * qs, 64, X64, X64)
                            for i in range(2):
                                block_of(64 * i + 32 * ks, 64 * i + 32 * qs, 32, X32, X32)
                            for i in range(4):
                                mm = block_of(32 * i, 32 * i, 32, Kd, Qd)
                        full(mm, "sc", l, d, f, hh)
                    behind = na_steps(l, n_g, 2)
                    na(behind[:1])
                    pe.wait_ge(*emptied("kv", l, d, f))
                    for hh in range(2):
                        pe.wait_ge(*emptied("sc", l, d, f, hh))
                        h = 2 * f + hh
                        for t in tiles_out(l):
                            o = psum[t][:, h * DV:(h + 1) * DV]
                            pe.matmul(o, ST[:, hh * 512 + t * P:hh * 512 + (t + 1) * P], v3[:, t, h * DV:(h + 1) * DV],
                                      start=(d, f, hh) == (0, 0, 0), stop=False, skip_group_check=True)
                    for t in tiles_out(l):
                        j = order.index(t)
                        mm = pe.matmul(psum[t][:, 2 * f * DV:(2 * f + 2) * DV], QI[:, t * P:(t + 1) * P],
                                       states[:, 2 * j * DV:(2 * j + 2) * DV], start=False, stop=d == 1,
                                       skip_group_check=True)
                    mm.then_inc(*up("group_done", l, d, f))
                    na(behind[1:])
                w = streams_out(l) * SEQ

                def tail(part):
                    if part != 1:
                        return
                    for nm in ("cs", "cs2"):
                        b = take(pe, nm, l)
                        pe.wait_ge(*past("csq", l, 1))
                        for ct in range(2):
                            src = ca4[:, ct, 0:streams_out(l), :].rearrange("p s n -> p (s n)") if nm == "cs" else lnb(ct)[:, 0:w]
                            mm = pe.matmul(b[:, 0:w], ones[:, :], src, start=ct == 0, stop=ct == 1)
                        full(mm, nm, l)

                for n_, parts in tail_steps(l):
                    for part in parts:
                        tail(part)
                    na([n_])
                for nm, X in (("nt", nout3), ("gt", gout3)):
                    for t in tiles_out(l):
                        b = take(pe, nm, l, t)
                        pe.wait_ge(*(past("gout", l, t) if nm == "gt" else emptied("no", l, NH - 1, t)))
                        for kk in range(3):
                            mm = pe.transpose(b[:, kk * P:(kk + 1) * P], X[:, t, kk * P:(kk + 1) * P], ident)
                        full(mm, nm, l, t)
                pe.wait_ge(*past("cact", l, 1))
                for t in tiles_out(l):
                    pe.wait_ge(*emptied("gt", l, t))
                    pe.wait_ge(*emptied("nt", l, t))
                    pe.wait_ge(*past("o_free", l, t))
                for u in range(3):
                    pe.wait_ge(*landed("out", l, u))
                def project(t):
                    for c in range(2):
                        if t >= 2:
                            pe.wait_ge(*past("y_free", l, t - 2, c))
                        b = psum[t % 2 * 2 + c]
                        for kk in range(KD):
                            mm = pe.matmul(b[:, :], hT3[:, kk, t * P:(t + 1) * P],
                                           slabs(("out", l, kk // 3))[:, (kk % 3) * D + c * 512:(kk % 3) * D + (c + 1) * 512],
                                           start=kk == 0, stop=kk == KD - 1)
                        mm.then_inc(*up("y_full", l, t, c))

                def router(t):
                    if t == 0:
                        pe.wait_ge(*past("rw", 1))
                        pe.wait_ge(*past("y_free", l, tiles_out(l)[-2], 0))
                    for c in range(2):
                        pe.wait_ge(*emptied("ht", l, "ffn", t, c))
                    for kk in range(KD):
                        mm = pe.matmul(psum[0][:, t * E:(t + 1) * E], hT3[:, kk, t * P:(t + 1) * P], rw[:, kk, :],
                                       start=kk == 0, stop=kk == KD - 1)
                    if t == tiles_out(l)[-1]:
                        full(mm, "lg", l)

                project(0)
                project(1)
                if len(tiles_out(l)) > 2:
                    project(2)
                    turn_rows(l, "ffn", 0)
                    project(3)
                    turn_rows(l, "ffn", 1)
                    for t in (2, 3):
                        router(t - 2)
                        turn_rows(l, "ffn", t)
                else:
                    for t in (0, 1):
                        turn_rows(l, "ffn", t)
                for t in tiles_out(l)[-2:]:
                    router(t)
                b = take(pe, "count", l)
                pe.wait_ge(*past("assigned", l))
                n_t = len(tiles_out(l))
                n = n_t * E
                run = rt[:, 12:14, :].rearrange("p a b -> p (a b)")
                pe.matmul(b[:, 0:E], cst("before"), rt[:, 10, 0:E], start=True, stop=True)
                pe.matmul(b[:, E:n], cst("before"), rt[:, 10, E:n], start=True, stop=False)
                pe.matmul(b[:, E:n], ones[:, :], run[:, 0:n - E], start=False, stop=True)
                mm = pe.matmul(b[:, NT * E:(NT + 1) * E], ones[:, :], run[:, n - E:n], start=True, stop=True)
                full(mm, "count", l)
                pe.wait_ge(*past("routed", l))
                nb = pe.value_load(tabi[0:1, TAB:TAB + 1], min_val=4, max_val=MAXB)
                s = {x: sem(f"m{l}_{x}") for x in ("lo", "used", "xg", "xf", "xe", "hf", "he", "hl", "mul", "ye")}

                def turn_x(i):
                    pe.wait_ge(s["xg"], i * 16 + 16)
                    for kk in range(KD):
                        mm = pe.transpose(psum[6 + kk // 4][:, kk % 4 * P:(kk % 4 + 1) * P], xe[:, kk * P:(kk + 1) * P], ident)
                    mm.then_inc(s["xf"], 1)

                def turn_h(i):
                    pe.wait_ge(s["mul"], i * 2 + 2)
                    for kk in range(KD):
                        mm = pe.transpose(psum[6 + kk // 4][:, kk % 4 * P:(kk % 4 + 1) * P], hb[:, kk * P:(kk + 1) * P], ident)
                    mm.then_inc(s["hf"], 1)

                def slab_products(slabs, hi, lo, bank):
                    for before, n, _, _, _ in slabs:
                        pe.wait_ge(s["lo"], before + 1)
                        kk, base = bank(n)
                        f, g_ = split_of(n)
                        at = slice(kk * P, (kk + 1) * P)
                        for x, w, first, last in ((hi, f, True, False), (hi, g_, False, False), (lo, f, False, True)):
                            for c in range(2):
                                mm = pe.matmul(psum[base + c][:, :], x[:, at], w[:, c * 512:(c + 1) * 512],
                                               start=first and kk == 0, stop=last and kk == KD - 1)
                        mm.then_inc(s["used"], 1)

                def gate_up(slabs):
                    slab_products(slabs, xTh, xTl, lambda n: (n // 4 * 2 + n % 2, n // 2 % 2 * 2))

                def down(slabs):
                    slab_products(slabs, gTh, gTl, lambda n: (n, 4))

                turn_x(0)
                pe.wait_ge(s["xe"], 2)
                gate_up(gate_ups(0, 0, 16))
                turn_x(1)
                pe.wait_ge(s["xe"], 4)
                turn_h(0)
                with pe.Fori(1, nb) as i:
                    pe.wait_ge(s["mul"], i * 2)
                    gate_up(gate_ups(i, 0, 16))
                    pe.wait_ge(s["hl"], i * 2)
                    turn_x(i + 1)
                    pe.wait_ge(s["ye"], i * 2)
                    down(downs(i, 0, 8))
                    pe.wait_ge(s["xe"], i * 2 + 4)
                    turn_h(i)
                pe.wait_ge(s["hl"], nb * 2)
                pe.wait_ge(s["ye"], nb * 2)
                down(downs(nb, 0, 8, tail=True))
                pe.wait_ge(s["ye"], nb * 2 + 2)

        led.now[("order",)] = {k: v for k, v in led.order.items() if k[0] != "d"}
        led.now[("dorder",)] = {k[1:]: v for k, v in led.order.items() if k[0] == "d"}
        return led.now


_INS = ['x', 'c', 'ctx', 'c_ctx', 'w_mod', 'b_mod', 'g_mix', 'g_ffn', 'w_in', 'gla_wa_f', 'gla_ba_f', 'gla_wa_b',
        'gla_ba_b', 'gla_g_norm', 'na_rpb', 'conv_w', 'conv_b', 'conv_ln_g', 'conv_ln_b', 'w_out', 'router_w',
        'router_bias', 'w_gate', 'w_up', 'w_down', 'g_final']


def kernel(**inputs):
    import numpy as _np
    import concourse.bacc as _bacc
    from concourse.bass_utils import run_bass_kernel_spmd as _run

    arrays = {f"in_{n}": _np.ascontiguousarray(inputs[n]) for n in _INS}
    arrays["in_const"] = CONST

    def program(known):
        nc = _bacc.Bacc("TRN2", target_bir_lowering=False, num_devices=1)
        io = {n[3:]: nc.dram_tensor(n, a.shape, mybir.dt.from_np(a.dtype), kind="ExternalInput").ap() for n, a in arrays.items()}
        io["out"] = nc.dram_tensor("out_0", (1, SEQ, D), F32, kind="ExternalOutput").ap()
        return nc, build(nc, io, known)

    _, known = program({})
    nc, _ = program(known)
    r = _run(nc, [arrays], core_ids=[0])
    return r.results[0]["out_0"]
```
